# Optimizing a Trainium2 kernel written in Bass

```python
import math
import jax, jax.numpy as jnp
from jax import lax
import numpy as np

D_MODEL = 1024
BATCH = 1
SEQ = 256
DEPTH = 1

MLA_HEADS = 8
MLA_Q_RANK = 384
MLA_KV_RANK = 256
MLA_NOPE = 64
MLA_ROPE = 32
MLA_V = 64
MLA_SCALE = 1.0 / math.sqrt(MLA_NOPE + MLA_ROPE)
ROPE_THETA = 10000.0
FOX_HEADS = 8
FOX_DIM = 64
FOX_SCALE = 1.0 / math.sqrt(FOX_DIM)
D_FF = 2816
CONV_WIDTH = 3
BLOCK_Q = 128
EPS = 1e-6
N_ADA = 6

IN_SPLITS = (
    MLA_Q_RANK,
    MLA_KV_RANK,
    MLA_ROPE,
    FOX_HEADS * FOX_DIM,
    FOX_HEADS * FOX_DIM,
    FOX_HEADS * FOX_DIM,
    FOX_HEADS,
    D_MODEL,
    D_MODEL,
)
D_IN = sum(IN_SPLITS)
IN_OFFSETS = tuple(int(v) for v in np.cumsum(IN_SPLITS)[:-1])


def rmsnorm(x, g):
    xf = x.astype(jnp.float32)
    y = xf * lax.rsqrt(jnp.mean(xf * xf, axis=-1, keepdims=True) + EPS)
    return (y * g.astype(jnp.float32)).astype(x.dtype)

def rope(x, positions):
    r = x.shape[-1]
    inv_freq = ROPE_THETA ** (-jnp.arange(0, r, 2, dtype=jnp.float32) / r)
    ang = positions.astype(jnp.float32)[..., None] * inv_freq
    cos = jnp.cos(ang)[:, :, None, :]
    sin = jnp.sin(ang)[:, :, None, :]
    xf = x.astype(jnp.float32)
    x1, x2 = xf[..., : r // 2], xf[..., r // 2:]
    out = jnp.concatenate([x1 * cos - x2 * sin, x2 * cos + x1 * sin], axis=-1)
    return out.astype(x.dtype)

def causal_block_attention(q, k, v, scale, log_cum=None):
    b, s, h, dk = q.shape
    nb = s // BLOCK_Q
    idx = jnp.arange(nb)
    qb = q.reshape(b, nb, BLOCK_Q, h, dk).transpose(1, 0, 2, 3, 4)
    key_pos = jnp.arange(s)
    if log_cum is not None:
        f_keys = log_cum.transpose(0, 2, 1)
        fb = log_cum.reshape(b, nb, BLOCK_Q, h).transpose(1, 0, 2, 3)
        xs = (idx, qb, fb)
    else:
        xs = (idx, qb)

    def one_block(args):
        i, qi = args[0], args[1]
        logits = jnp.einsum('bqhd,bkhd->bhqk', qi, k,
                            preferred_element_type=jnp.float32) * scale
        if log_cum is not None:
            fi = args[2].transpose(0, 2, 1)
            logits = logits + (fi[..., :, None] - f_keys[:, :, None, :])
        q_pos = i * BLOCK_Q + jnp.arange(BLOCK_Q)
        mask = key_pos[None, :] <= q_pos[:, None]
        logits = jnp.where(mask[None, None], logits, -jnp.inf)
        p = jax.nn.softmax(logits, axis=-1)
        return jnp.einsum('bhqk,bkhd->bqhd', p.astype(v.dtype), v)

    out = lax.map(one_block, xs)
    return out.transpose(1, 0, 2, 3, 4).reshape(b, s, h, v.shape[-1])

def hybrid_mixer(h, positions, w_in, q_norm_g, w_uq, kv_norm_g, w_ukv, b_forget,
                 w_o_mla, w_o_fox, w_out):
    b, s, _ = h.shape
    proj = h @ w_in
    cq, ckv, k_rope, fq, fk, fv, f_logit, g_mla, g_fox = jnp.split(proj, IN_OFFSETS, axis=-1)

    q = (rmsnorm(cq, q_norm_g) @ w_uq).reshape(b, s, MLA_HEADS, MLA_NOPE + MLA_ROPE)
    q_nope, q_rope = q[..., :MLA_NOPE], q[..., MLA_NOPE:]
    kv = (rmsnorm(ckv, kv_norm_g) @ w_ukv).reshape(b, s, MLA_HEADS, MLA_NOPE + MLA_V)
    k_nope, v_mla = kv[..., :MLA_NOPE], kv[..., MLA_NOPE:]
    q_rope = rope(q_rope, positions)
    k_rope = rope(k_rope[:, :, None, :], positions)
    q_mla = jnp.concatenate([q_nope, q_rope], axis=-1)
    k_mla = jnp.concatenate(
        [k_nope, jnp.broadcast_to(k_rope, (b, s, MLA_HEADS, MLA_ROPE))], axis=-1)
    o_mla = causal_block_attention(q_mla, k_mla, v_mla, MLA_SCALE).reshape(b, s, MLA_HEADS * MLA_V)

    log_f = jax.nn.log_sigmoid(f_logit.astype(jnp.float32) + b_forget.astype(jnp.float32))
    f_cum = jnp.cumsum(log_f, axis=1)
    o_fox = causal_block_attention(
        fq.reshape(b, s, FOX_HEADS, FOX_DIM), fk.reshape(b, s, FOX_HEADS, FOX_DIM),
        fv.reshape(b, s, FOX_HEADS, FOX_DIM), FOX_SCALE, f_cum).reshape(b, s, FOX_HEADS * FOX_DIM)

    y = jax.nn.sigmoid(g_mla) * (o_mla @ w_o_mla) + jax.nn.sigmoid(g_fox) * (o_fox @ w_o_fox)
    return y @ w_out

def conv_ffn(h, w_up, conv_w, conv_b, w_down):
    s = h.shape[1]
    u = h @ w_up
    up = jnp.pad(u, ((0, 0), (CONV_WIDTH - 1, 0), (0, 0)))
    u = conv_b + sum(conv_w[j] * up[:, j:j + s] for j in range(CONV_WIDTH))
    gate, val = u[..., :D_FF], u[..., D_FF:]
    return (jax.nn.silu(gate) * val) @ w_down

def modulate(hn, shift, scale):
    return hn * (1.0 + scale[:, None, :]) + shift[:, None, :]

def first_inputs(seed: int = 0) -> dict:
    key = jax.random.key(seed)
    ks = jax.random.split(key, 24)
    nrm = lambda k, shape, fan: jax.random.normal(k, shape, jnp.float32) * (fan ** -0.5)
    L = DEPTH
    x = jax.random.normal(ks[0], (BATCH, SEQ, D_MODEL), jnp.float32)
    c = jax.random.normal(ks[1], (BATCH, D_MODEL), jnp.float32)
    offsets = jax.random.randint(ks[2], (BATCH, 1), 0, 4096, dtype=jnp.int32)
    positions = offsets + jnp.arange(SEQ, dtype=jnp.int32)[None, :]
    return {
        "x": x,
        "c": c,
        "positions": positions,
        "w_ada": 0.5 * nrm(ks[3], (L, D_MODEL, N_ADA * D_MODEL), D_MODEL),
        "b_ada": 0.01 * jax.random.normal(ks[4], (L, N_ADA * D_MODEL), jnp.float32),
        "norm_mix_g": 1.0 + 0.1 * jax.random.normal(ks[5], (L, D_MODEL), jnp.float32),
        "w_in": nrm(ks[6], (L, D_MODEL, D_IN), D_MODEL),
        "q_norm_g": 1.0 + 0.1 * jax.random.normal(ks[7], (L, MLA_Q_RANK), jnp.float32),
        "w_uq": nrm(ks[8], (L, MLA_Q_RANK, MLA_HEADS * (MLA_NOPE + MLA_ROPE)), MLA_Q_RANK),
        "kv_norm_g": 1.0 + 0.1 * jax.random.normal(ks[9], (L, MLA_KV_RANK), jnp.float32),
        "w_ukv": nrm(ks[10], (L, MLA_KV_RANK, MLA_HEADS * (MLA_NOPE + MLA_V)), MLA_KV_RANK),
        "b_forget": jax.random.uniform(ks[11], (L, FOX_HEADS), jnp.float32, 1.0, 6.0),
        "w_o_mla": nrm(ks[12], (L, MLA_HEADS * MLA_V, D_MODEL), MLA_HEADS * MLA_V),
        "w_o_fox": nrm(ks[13], (L, FOX_HEADS * FOX_DIM, D_MODEL), FOX_HEADS * FOX_DIM),
        "w_out": nrm(ks[14], (L, D_MODEL, D_MODEL), D_MODEL),
        "norm_ffn_g": 1.0 + 0.1 * jax.random.normal(ks[15], (L, D_MODEL), jnp.float32),
        "w_up": nrm(ks[16], (L, D_MODEL, 2 * D_FF), D_MODEL),
        "conv_w": nrm(ks[17], (L, CONV_WIDTH, 2 * D_FF), CONV_WIDTH),
        "conv_b": 0.01 * jax.random.normal(ks[18], (L, 2 * D_FF), jnp.float32),
        "w_down": nrm(ks[19], (L, D_FF, D_MODEL), D_FF),
        "norm_final_g": 1.0 + 0.1 * jax.random.normal(ks[20], (D_MODEL,), jnp.float32),
    }

def first_block(x, c, positions, w_ada, b_ada, norm_mix_g, w_in, q_norm_g, w_uq, kv_norm_g,
              w_ukv, b_forget, w_o_mla, w_o_fox, w_out, norm_ffn_g, w_up, conv_w, conv_b,
              w_down, norm_final_g):
    c_act = jax.nn.silu(c)
    for l in range(DEPTH):
        ada = c_act @ w_ada[l] + b_ada[l]
        sh_m, sc_m, g_m, sh_f, sc_f, g_f = jnp.split(ada, N_ADA, axis=-1)
        h = modulate(rmsnorm(x, norm_mix_g[l]), sh_m, sc_m)
        mix = hybrid_mixer(h, positions, w_in[l], q_norm_g[l], w_uq[l], kv_norm_g[l], w_ukv[l],
                           b_forget[l], w_o_mla[l], w_o_fox[l], w_out[l])
        x = x + g_m[:, None, :] * mix
        h = modulate(rmsnorm(x, norm_ffn_g[l]), sh_f, sc_f)
        x = x + g_f[:, None, :] * conv_ffn(h, w_up[l], conv_w[l], conv_b[l], w_down[l])
    return rmsnorm(x, norm_final_g)


D_MIX = D_MODEL
D_CONV = D_MIX // 2
D_ATTN = D_MIX - D_CONV
CONV_GROUPS = 8
HEAD_DIM = 64
V_DIM = 2 * HEAD_DIM
N_HEADS = D_ATTN // V_DIM
Q_WIDTH = N_HEADS * 2 * HEAD_DIM
D_IN_2 = 3 * D_CONV + 2 * Q_WIDTH + N_HEADS * V_DIM
Q_BLOCK = 128
N_EXPERT_GROUPS = 4
EXPERTS_PER_GROUP = 8
TOP_K = 2
D_EXPERT = D_MODEL // 2


def rms_norm(x, g):
    xf = x.astype(jnp.float32)
    y = xf * lax.rsqrt(jnp.mean(xf * xf, axis=-1, keepdims=True) + EPS)
    return (y * g.astype(jnp.float32)).astype(x.dtype)

def lambda_init(layer_idx):
    return 0.8 - 0.6 * math.exp(-0.3 * layer_idx)

def causal_depthwise_conv(u, w):
    K = w.shape[0]
    S = u.shape[1]
    up = jnp.pad(u, ((0, 0), (K - 1, 0), (0, 0)))
    y = up[:, 0:S, :] * w[0]
    for k in range(1, K):
        y = y + up[:, k:k + S, :] * w[k]
    return y

def short_conv_group(xc, b_gate, c_gate, conv_w, conv_out_g):
    y = b_gate * causal_depthwise_conv(c_gate * xc, conv_w)
    Bsz, S, _ = y.shape
    yg = y.reshape(Bsz, S, CONV_GROUPS, D_CONV // CONV_GROUPS)
    yg = rms_norm(yg, jnp.ones((D_CONV // CONV_GROUPS,), y.dtype))
    return yg.reshape(Bsz, S, D_CONV) * conv_out_g.astype(y.dtype)

def diff_attention_group(q, k, v, q_norm_g, k_norm_g, lq1, lk1, lq2, lk2, subln_g, lam_init):
    Bsz, S, _ = q.shape
    q = rms_norm(q.reshape(Bsz, S, N_HEADS, 2, HEAD_DIM), q_norm_g) * (HEAD_DIM ** -0.5)
    k = rms_norm(k.reshape(Bsz, S, N_HEADS, 2, HEAD_DIM), k_norm_g)
    v = v.reshape(Bsz, S, N_HEADS, V_DIM)
    qT = q.transpose(0, 2, 3, 1, 4)
    kT = k.transpose(0, 2, 3, 1, 4)
    vT = v.transpose(0, 2, 1, 3)
    lam = (jnp.exp(jnp.sum(lq1.astype(jnp.float32) * lk1.astype(jnp.float32)))
           - jnp.exp(jnp.sum(lq2.astype(jnp.float32) * lk2.astype(jnp.float32)))
           + lam_init)
    key_pos = jnp.arange(S)
    n_blocks = S // Q_BLOCK

    def one_block(i):
        start = i * Q_BLOCK
        qb = lax.dynamic_slice_in_dim(qT, start, Q_BLOCK, axis=3)
        s = jnp.einsum('bhcqd,bhckd->bhcqk', qb, kT).astype(jnp.float32)
        q_pos = start + jnp.arange(Q_BLOCK)
        mask = key_pos[None, :] <= q_pos[:, None]
        s = jnp.where(mask, s, -jnp.inf)
        p = jax.nn.softmax(s, axis=-1)
        a = (p[:, :, 0] - lam * p[:, :, 1]).astype(vT.dtype)
        return jnp.einsum('bhqk,bhkv->bqhv', a, vT)

    out = lax.map(one_block, jnp.arange(n_blocks))
    out = out.transpose(1, 0, 2, 3, 4).reshape(Bsz, S, N_HEADS, V_DIM)
    out = rms_norm(out, subln_g) * (1.0 - lam_init)
    return out.reshape(Bsz, S, D_ATTN)

def hierarchical_moe(h, w_router_group, w_router_expert, w_gate, w_up, w_down):
    T = h.shape[0]
    G, E = N_EXPERT_GROUPS, EXPERTS_PER_GROUP
    p_group = jax.nn.softmax(jnp.einsum('td,dg->tg', h, w_router_group).astype(jnp.float32), axis=-1)
    g_idx = jnp.argmax(p_group, axis=-1)
    g_gate = jnp.max(p_group, axis=-1)
    logits_e = jnp.einsum('td,de->te', h, w_router_expert).astype(jnp.float32).reshape(T, G, E)
    logits_sel = jnp.take_along_axis(logits_e, g_idx[:, None, None], axis=1)[:, 0]
    top_vals, top_idx = lax.top_k(logits_sel, TOP_K)
    top_w = jax.nn.softmax(top_vals, axis=-1)
    exp_w = jnp.sum(jax.nn.one_hot(top_idx, E, dtype=jnp.float32) * top_w[..., None], axis=1)
    comb = (jax.nn.one_hot(g_idx, G, dtype=jnp.float32)[:, :, None]
            * exp_w[:, None, :] * g_gate[:, None, None]).astype(h.dtype)
    y = jnp.zeros_like(h)
    for g in range(G):
        hg = jnp.einsum('td,edf->tef', h, w_gate[g])
        hu = jnp.einsum('td,edf->tef', h, w_up[g])
        act = jax.nn.silu(hg) * hu * comb[:, g, :, None]
        y = y + jnp.einsum('tef,efd->td', act, w_down[g])
    return y

def second_inputs(seed: int = 0) -> dict:
    key = jax.random.key(seed)
    ks = jax.random.split(key, 20)
    f32 = jnp.float32
    G, E, F = N_EXPERT_GROUPS, EXPERTS_PER_GROUP, D_EXPERT

    def nrm(k, shape, scale):
        return jax.random.normal(k, shape, f32) * scale

    return {
        "x": nrm(ks[0], (BATCH, SEQ, D_MODEL), 1.0),
        "attn_norm_g": 1.0 + nrm(ks[1], (DEPTH, D_MODEL), 0.02),
        "w_in": nrm(ks[2], (DEPTH, D_MODEL, D_IN_2), D_MODEL ** -0.5),
        "conv_w": nrm(ks[3], (DEPTH, CONV_WIDTH, D_CONV), CONV_WIDTH ** -0.5),
        "conv_out_g": 1.0 + nrm(ks[4], (DEPTH, D_CONV), 0.02),
        "q_norm_g": 1.0 + nrm(ks[5], (DEPTH, HEAD_DIM), 0.02),
        "k_norm_g": 1.0 + nrm(ks[6], (DEPTH, HEAD_DIM), 0.02),
        "lambda_q1": nrm(ks[7], (DEPTH, HEAD_DIM), 0.1),
        "lambda_k1": nrm(ks[8], (DEPTH, HEAD_DIM), 0.1),
        "lambda_q2": nrm(ks[9], (DEPTH, HEAD_DIM), 0.1),
        "lambda_k2": nrm(ks[10], (DEPTH, HEAD_DIM), 0.1),
        "attn_subln_g": 1.0 + nrm(ks[11], (DEPTH, V_DIM), 0.02),
        "w_out": nrm(ks[12], (DEPTH, D_MIX, D_MODEL), D_MIX ** -0.5),
        "ffn_norm_g": 1.0 + nrm(ks[13], (DEPTH, D_MODEL), 0.02),
        "w_router_group": nrm(ks[14], (DEPTH, D_MODEL, G), D_MODEL ** -0.5),
        "w_router_expert": nrm(ks[15], (DEPTH, D_MODEL, G * E), D_MODEL ** -0.5),
        "w_exp_gate": nrm(ks[16], (DEPTH, G, E, D_MODEL, F), D_MODEL ** -0.5),
        "w_exp_up": nrm(ks[17], (DEPTH, G, E, D_MODEL, F), D_MODEL ** -0.5),
        "w_exp_down": nrm(ks[18], (DEPTH, G, E, F, D_MODEL), F ** -0.5),
    }

def second_block(x, attn_norm_g, w_in, conv_w, conv_out_g, q_norm_g, k_norm_g,
              lambda_q1, lambda_k1, lambda_q2, lambda_k2, attn_subln_g, w_out,
              ffn_norm_g, w_router_group, w_router_expert, w_exp_gate, w_exp_up, w_exp_down):
    Bsz, S, D = x.shape
    split_points = [D_CONV, 2 * D_CONV, 3 * D_CONV,
                    3 * D_CONV + Q_WIDTH, 3 * D_CONV + 2 * Q_WIDTH]
    h = x
    for l in range(DEPTH):
        lam_init = lambda_init(l)
        hn = rms_norm(h, attn_norm_g[l])
        proj = jnp.einsum('bsd,de->bse', hn, w_in[l])
        xc, b_gate, c_gate, q, k, v = jnp.split(proj, split_points, axis=-1)
        y_conv = short_conv_group(xc, b_gate, c_gate, conv_w[l], conv_out_g[l])
        y_attn = diff_attention_group(q, k, v, q_norm_g[l], k_norm_g[l],
                                      lambda_q1[l], lambda_k1[l], lambda_q2[l], lambda_k2[l],
                                      attn_subln_g[l], lam_init)
        mix = jnp.concatenate([y_conv, y_attn], axis=-1)
        h = h + jnp.einsum('bse,ed->bsd', mix, w_out[l])
        hn2 = rms_norm(h, ffn_norm_g[l]).reshape(Bsz * S, D)
        y_ffn = hierarchical_moe(hn2, w_router_group[l], w_router_expert[l],
                                 w_exp_gate[l], w_exp_up[l], w_exp_down[l])
        h = h + y_ffn.reshape(Bsz, S, D)
    return h


def setup_inputs(seed=0):
    out = dict(first_inputs(seed))
    for name, value in second_inputs(seed + 1).items():
        if name != "x":
            out[name + "_2"] = value
    return out


def reference(
    x, c, positions, w_ada, b_ada, norm_mix_g, w_in, q_norm_g, w_uq, kv_norm_g, w_ukv, b_forget,
    w_o_mla, w_o_fox, w_out, norm_ffn_g, w_up, conv_w, conv_b, w_down, norm_final_g,
    attn_norm_g_2, w_in_2, conv_w_2, conv_out_g_2, q_norm_g_2, k_norm_g_2, lambda_q1_2,
    lambda_k1_2, lambda_q2_2, lambda_k2_2, attn_subln_g_2, w_out_2, ffn_norm_g_2,
    w_router_group_2, w_router_expert_2, w_exp_gate_2, w_exp_up_2, w_exp_down_2,
):
    x = first_block(
        x, c, positions, w_ada, b_ada, norm_mix_g, w_in, q_norm_g, w_uq, kv_norm_g, w_ukv,
        b_forget, w_o_mla, w_o_fox, w_out, norm_ffn_g, w_up, conv_w, conv_b, w_down,
        norm_final_g,
    )
    return second_block(
        x, attn_norm_g_2, w_in_2, conv_w_2, conv_out_g_2, q_norm_g_2, k_norm_g_2, lambda_q1_2,
        lambda_k1_2, lambda_q2_2, lambda_k2_2, attn_subln_g_2, w_out_2, ffn_norm_g_2,
        w_router_group_2, w_router_expert_2, w_exp_gate_2, w_exp_up_2, w_exp_down_2,
    )


_drawn_inputs = setup_inputs


def setup_inputs(seed=0):
    import zlib

    import numpy as np

    out = dict(_drawn_inputs(seed))
    spreads = {}
    factors = {'q_norm_g': 3.365,
     'kv_norm_g': 2.671,
     'conv_b': 3.641,
     'q_norm_g_2': 2.728,
     'k_norm_g_2': 3.502,
     'lambda_k2_2': 3.998,
     'conv_out_g_2': 11.115,
     'attn_subln_g_2': 12.358,
     'ffn_norm_g_2': 5.17}
    for name, (base, spread) in spreads.items():
        noise = np.random.default_rng([zlib.crc32(name.encode()), seed]).standard_normal(out[name].shape)
        drawn = base * np.exp(spread * noise) if base else spread * noise
        out[name] = __import__('jax').numpy.asarray(drawn.astype(out[name].dtype))
    for name, factor in factors.items():
        out[name] = (out[name] * factor).astype(out[name].dtype)
    return out
```

```python
import math
from contextlib import ExitStack

import numpy as np

import concourse.bass as bass
from concourse import mybir

F32 = mybir.dt.float32
F32R = mybir.dt.float32r
I32 = mybir.dt.int32
ALU = mybir.AluOpType
ACT = mybir.ActivationFunctionType
AX_X = mybir.AxisListType.X

P = 128
SEQ = 256
TT = SEQ // P
D = 1024
KD = D // P
EPS = 1e-6
NEG = -1e30

Q_RANK, KV_RANK, ROPE = 384, 256, 32
HEADS = 8
NOPE, VDIM, FOXD = 64, 64, 64
QK = NOPE + ROPE
HALF = ROPE // 2
ATT = HEADS * VDIM
MLA_SCALE = 1.0 / math.sqrt(QK)
FOX_SCALE = 1.0 / math.sqrt(FOXD)
D_FF = 2816
FT = D_FF // P
CONV_W = 3

D_CONV = 512
N_HEADS2, HEAD2, V2 = 4, 64, 128
LAM_INIT = 0.8 - 0.6 * math.exp(0.0)
GROUPS, EPG, D_EXP = 4, 8, 512
EXPERTS = GROUPS * EPG
CAP = 64
PER_IT = 4
TURNS = EXPERTS // PER_IT
LG = GROUPS + EXPERTS

SLOT = 8 * 520
SLOTS = 6
RING1 = 4
CHUNK = 2 * 520

ROW = {}
_at = 0
for _name, _n in (("c", 8), ("b_ada", 48), ("mix_g", 8), ("q_g", 3), ("kv_g", 2), ("ffn_g", 8), ("fin_g", 8),
                  ("attn_g2", 8), ("conv_w2", 12), ("conv_out_g2", 4), ("subln", 1), ("ffn_g2", 8),
                  ("qg2", 1), ("kg2", 1), ("lam", 4)):
    ROW[_name] = _at
    _at += _n
assert _at <= P
ROW["conv_w0"], ROW["conv_w1"], ROW["conv_w2_ff"], ROW["conv_b"] = P, P + 2 * FT, 2 * P, 2 * P + 2 * FT
ROWS_TOTAL = 16 * (13 + 3 + 4 + 4)
XT_READY = (4, 4 + KD, 4 + 2 * KD, 4 + 3 * KD, 8 + 3 * KD)
SPLIT_NORM = {0: 1, 1: 2, 3: 3, 4: 4}
SH_M, SC_M, G_M, SH_F, SC_F, G_F = (i * KD for i in range(6))


def two_pi_parts():
    parts, rest = [], 2 * math.pi
    for _ in range(3):
        e = math.floor(math.log2(rest))
        q = 2.0 ** (e - 7)
        parts.append(math.floor(rest / q) * q)
        rest -= parts[-1]
    return parts + [float(np.float32(rest))]


def build(nc, t, out):
    ctx = ExitStack()
    sems = {}

    def S(name):
        if name not in sems:
            sems[name] = ctx.enter_context(nc.semaphore(name))
        return sems[name]

    def sb(name, shape, dt=F32):
        return ctx.enter_context(nc.sbuf_tensor(name, shape, dt))

    with ctx:
        ps = ctx.enter_context(nc.psum_tensor("ps", [P, 8, 512], F32))
        ring = sb("ring", [P, SLOTS, SLOT])
        wh = sb("wh", [P, 2, CHUNK], F32R)
        wl = sb("wl", [P, 2, CHUNK], F32R)
        hH = sb("hH", [P, KD, SEQ], F32R)
        hL = sb("hL", [P, KD, SEQ], F32R)
        aH = sb("aH", [P, 12, SEQ], F32R)
        aL = sb("aL", [P, 12, SEQ], F32R)
        xT = sb("xT", [P, KD, SEQ])
        wa = sb("wa", [P, 3072])
        wb = sb("wb", [P, 4096])
        wc = sb("wc", [P, 1920])
        colT = sb("colT", [P, 3 * P])
        adaT = sb("adaT", [P, 6 * KD])
        cact = sb("cact", [P, KD])
        scale_m = sb("scale_m", [P, KD])
        scale_f = sb("scale_f", [P, KD])
        ident = sb("ident", [P, P])
        tri_ones = sb("tri_ones", [P, 2 * P])
        tri, ones = tri_ones[:, 0:P], tri_ones[:, P:2 * P]
        mask = sb("mask", [P, 3 * P])
        minus_half = sb("minus_half", [P, 16])
        invf = sb("invf", [P, HALF])
        half_ind = sb("half_ind", [P, 2])
        pos_i = sb("pos_i", [P, TT], I32)
        pos_f = sb("pos_f", [P, TT])
        trig = sb("trig", [P, 5, TT, HALF])
        bf_b = sb("bf_b", [P, HEADS])
        ms = sb("ms", [P, 16])
        rstd = sb("rstd", [P, 16])
        ssq = sb("ssq", [P, 4])
        nmax = sb("nmax", [P, 3, 2])
        rsum = sb("rsum", [P, 3, 2])
        rinv = sb("rinv", [P, 3, 2])
        fz = sb("fz", [P, 3, TT, HEADS])
        f_tok = sb("f_tok", [P, TT, HEADS])
        nFT = sb("nFT", [HEADS, SEQ])
        qg8 = sb("qg8", [P, 1])
        sub8 = sb("sub8", [P, 1])
        lam = sb("lam", [P, 6])

        flatE = ring[:, RING1:SLOTS, :].rearrange("p s n -> p (s n)")
        rows = wc[:, 0:3 * P].rearrange("p (i n) -> p i n", i=3)
        ada_row = wc[:, 3 * P:3 * P + 512]
        x_tok = wa[:, 0:TT * D].rearrange("p (t d) -> p t d", t=TT)
        n_sq = wb[:, 0:KD * SEQ].rearrange("p (k n) -> p k n", k=KD)
        n_xn = wb[:, KD * SEQ:2 * KD * SEQ].rearrange("p (k n) -> p k n", k=KD)
        n_red = wc[:, 1152:1152 + SEQ]
        CKQ = Q_RANK + KV_RANK + ROPE
        cqkv = wc[:, 0:TT * CKQ].rearrange("p (t n) -> p t n", t=TT)
        fqT = wa[:, 0:1024].rearrange("p (m n) -> p m n", m=4)
        fkT = wa[:, 1024:2048].rearrange("p (m n) -> p m n", m=4)
        fv_tok = wa[:, 2048:3072].rearrange("p (t n) -> p t n", t=TT)
        q_tok = wb[:, 0:1536].rearrange("p (t h n) -> p t h n", t=TT, h=HEADS)
        k_tok = wb[:, 1536:3072].rearrange("p (t h n) -> p t h n", t=TT, h=HEADS)
        v_tok = wb[:, 3072:4096].rearrange("p (t n) -> p t n", t=TT)
        rope_tmp = wc[:, 1408:1920].rearrange("p (i n) -> p i n", i=2)
        sig = flatE[:, 0:4096].rearrange("p (m n) -> p m n", m=16)
        qT = flatE[:, 4096:6144].rearrange("p (h n) -> p h n", h=HEADS)
        kT = flatE[:, 6144:8192].rearrange("p (h n) -> p h n", h=HEADS)
        prob = wc[:, 0:1152].rearrange("p (b n) -> p b n", b=3)
        pT = wc[:, 1152:1920].rearrange("p (b n) -> p b n", b=2)
        yF = wb[:, 0:2048].rearrange("p (m n) -> p m n", m=KD)
        conv = flatE[:, 0:2048].rearrange("p (b m n) -> p b m n", b=2, m=4)
        actF = flatE[:, 2048:3072].rearrange("p (b m n) -> p b m n", b=2, m=2)
        q2 = wa[:, 0:1024].rearrange("p (t n) -> p t n", t=TT)
        k2 = wa[:, 1024:2048].rearrange("p (t n) -> p t n", t=TT)
        v2 = wa[:, 2048:3072].rearrange("p (t n) -> p t n", t=TT)
        o2 = wa[:, 0:1024].rearrange("p (t n) -> p t n", t=TT)
        qT2 = wb[:, 0:1024].rearrange("p (m n) -> p m n", m=4)
        kT2 = wb[:, 1024:2048].rearrange("p (m n) -> p m n", m=4)
        cz = wb[:, 2048:3072].rearrange("p (m n) -> p m n", m=4)
        cb = wb[:, 3072:4096].rearrange("p (m n) -> p m n", m=4)
        cy = flatE[:, 0:1024].rearrange("p (m n) -> p m n", m=4)
        csq = flatE[:, 1024:2048].rearrange("p (m n) -> p m n", m=4)
        sq2 = flatE[:, 2048:3072].rearrange("p (t n) -> p t n", t=TT)
        qn = flatE[:, 3072:4096].rearrange("p (t n) -> p t n", t=TT)
        kn = flatE[:, 4096:5120].rearrange("p (t n) -> p t n", t=TT)
        mixF = flatE[:, 5120:6144].rearrange("p (m n) -> p m n", m=4)
        wr = sb("wr", [P, KD, LG])
        lg = wa[:, 2048:2048 + TT * LG].rearrange("p (t n) -> p t n", t=TT)
        _r = [2048 + TT * LG]

        def rt(*shape):
            n = int(np.prod(shape))
            v = wa[:, _r[0]:_r[0] + n]
            _r[0] += n
            if len(shape) == 2:
                v = v.rearrange("p (a b) -> p a b", a=shape[0])
            if len(shape) == 3:
                v = v.rearrange("p (a b c) -> p a b c", a=shape[0], b=shape[1])
            return v

        gmax, gsum, ggate = rt(TT), rt(TT), rt(TT)
        gexp, goh, gtmp = rt(TT, GROUPS), rt(TT, GROUPS), rt(TT, GROUPS)
        gprod = rt(TT, GROUPS, EPG)
        lsel, oh1, oh2, etmp, l2 = (rt(TT, EPG) for _ in range(5))
        m1, m2, wm, ed, w1, w2 = (rt(TT) for _ in range(6))
        sel = rt(TT, GROUPS, EPG)
        comb = sb("comb", [P, TT, EXPERTS + PER_IT])
        posm = sb("posm", [P, TT, EXPERTS + PER_IT])
        desc = sb("desc", [P, EPG])
        slot_no = sb("slot_no", [P, CAP])
        npass_f = sb("npass_f", [1, 2])
        npass = sb("npass", [1, 2], I32)
        hnH = aH[:, 0:8, :].rearrange("p a b -> p (a b)").rearrange("p (t d) -> p t d", t=TT)
        hnL = aL[:, 0:8, :].rearrange("p a b -> p (a b)").rearrange("p (t d) -> p t d", t=TT)
        pick = hH[:, 0:2, :]
        xg = xT
        sg = wc[:, 0:512]
        eact = wc[:, 512:1024]
        eactT = wc[:, 1024:1536].rearrange("p (k n) -> p k n", k=4)
        eout = wa[:, 0:1024]
        put = wa[:, 1024:1536].rearrange("p (t n) -> p t n", t=TT)
        putT = wa[:, 1536:2048].rearrange("p (r n) -> p r n", r=2)
        y_acc = wb[:, 2048:4096].rearrange("p (t d) -> p t d", t=TT)

        W = {k: t[k] for k in t}

        def rows_of(w, c0, n, k0=0, kn=None):
            v = w.rearrange("(k p) n -> p k n", p=P)
            return v[:, k0:(kn or v.shape[1] - k0) + k0, c0:c0 + n]

        items = []

        def item(name, kn, n, srcs, per_chunk):
            chunks = [(k, min(per_chunk, kn - k)) for k in range(0, kn, per_chunk)] if per_chunk else []
            items.append({"name": name, "kn": kn, "n": n, "srcs": srcs, "chunks": chunks})

        def ada_items(third):
            for i in range(4):
                item(f"ada{third}{i}", 2, 2048, [(0, 2048, rows_of(W["w_ada"], 2048 * third, 2048, 2 * i, 2))], 0)

        o = np.cumsum([0, Q_RANK, KV_RANK + ROPE, 512, 512, 520, 512, 512, 512, 512]).tolist()
        names = ["cq", "ckv", "fq", "fk", "fv", "g0", "g1", "g2", "g3"]
        win = {nm: (o[i], o[i + 1] - o[i]) for i, nm in enumerate(names)}

        def in_item(nm):
            c0, n = win[nm]
            item(nm, KD, n, [(0, n, rows_of(W["w_in"], c0, n))], 2)

        def half_items(nm, w, kn, n, c, per):
            for i in range(c):
                item(f"{nm}{i}", kn, n, [(0, n, rows_of(W[w], n * i, n))], per)

        ada_items(0)
        for nm in names[:5]:
            in_item(nm)
        half_items("uq", "w_uq", 3, 384, 2, 2)
        half_items("ukv", "w_ukv", 2, 512, 2, 2)
        for nm in names[5:]:
            in_item(nm)
        half_items("om", "w_o_mla", 4, 512, 2, 2)
        half_items("of", "w_o_fox", 4, 512, 2, 2)
        ada_items(1)
        half_items("wo", "w_out", KD, 512, 2, 2)
        ada_items(2)

        def up_item(j):
            item(f"up{j}", KD, 512, [(0, 256, rows_of(W["w_up"], 256 * j, 256)),
                                     (256, 256, rows_of(W["w_up"], D_FF + 256 * j, 256))], 2)

        def down_item(j):
            kn = min(4, FT - 4 * j)
            item(f"dn{j}", kn, D, [(0, D, rows_of(W["w_down"], 0, D, 4 * j, kn))], 1)

        UP_A = 6
        for j in range(UP_A):
            up_item(j)
        for j in range(3):
            down_item(j)
        for j in range(UP_A, 11):
            up_item(j)
        for j in range(3, 6):
            down_item(j)
        for nm, c in (("q2", 3), ("k2", 4), ("v2", 5), ("xc", 0), ("bg", 1), ("cg", 2)):
            item(nm, KD, 512, [(0, 512, rows_of(W["w_in_2"], 512 * c, 512))], 2)
        half_items("w2o", "w_out_2", KD, 512, 2, 2)

        IT = {}
        n_chunk = n_ada = 0
        n_lin = 0
        loaded = [0] * SLOTS
        for i, it in enumerate(items):
            it["slot"] = i % RING1
            loaded[it["slot"]] += 16 * len(it["srcs"])
            it["loaded"] = loaded[it["slot"]]
            it["c0"] = n_chunk
            n_chunk += len(it["chunks"])
            it["c1"] = n_chunk
            if it["chunks"]:
                it["acc"] = 2 * (n_lin % 2)
                n_lin += 1
            else:
                n_ada += 1
            it["ada"] = n_ada
            IT[it["name"]] = it
        first_expert = len(items)
        base_loaded = list(loaded)

        def slot_view(it):
            return ring[:, it["slot"], 0:it["kn"] * it["n"]].rearrange("p (k n) -> p k n", n=it["n"])

        def raw_chunk(it, ci):
            k0, kn = it["chunks"][ci]
            return ring[:, it["slot"], k0 * it["n"]:(k0 + kn) * it["n"]], kn * it["n"]

        w_gate = W["w_exp_gate_2"].rearrange("e (k p) n -> e p k n", p=P)
        w_upx = W["w_exp_up_2"].rearrange("e (k p) n -> e p k n", p=P)
        w_downx = W["w_exp_down_2"].rearrange("e (k p) n -> e p k n", p=P)
        out_v = out.rearrange("(t p) d -> p t d", p=P)

        block = ctx.enter_context(nc.Block())

        @block.sync
        def _(sp):
            for i, it in enumerate(items):
                if i >= RING1:
                    before = items[i - RING1]
                    if before["chunks"]:
                        sp.wait_ge(S("chunk_low"), before["c1"])
                    else:
                        sp.wait_ge(S("ada_used"), before["ada"])
                for c0, n, src in it["srcs"]:
                    sp.dma_start(slot_view(it)[:, :, c0:c0 + n], src).then_inc(S(f"slot{it['slot']}_loaded"), 16)

            def load_pair(e, wait):
                for part, w in enumerate((w_gate, w_upx, w_downx)):
                    if wait is not None:
                        sp.wait_ge(S("expert_used"), wait + part)
                    for j in range(2):
                        s = 2 * part + j
                        kn = 8 if part < 2 else 4
                        dst = ring[:, s, 0:4096].rearrange("p (k n) -> p k n", k=kn)
                        if isinstance(e, int):
                            src = w[e + j]
                        else:
                            src = w[bass.ds(e + j, 1)].rearrange("e p k n -> (e p) k n")
                        sp.dma_start(dst, src).then_inc(S(f"slot{s}_loaded"), 16)

            for part, w in enumerate((w_gate, w_upx, w_downx)):
                for j in range(2):
                    s = 2 * part + j
                    if s < RING1:
                        last = max((it for it in items if it["slot"] == s), key=lambda it: it["c1"])
                        sp.wait_ge(S("chunk_low"), last["c1"])
                    else:
                        sp.wait_ge(S("mix_ready"), 1)
                    sp.dma_start(ring[:, s, 0:4096].rearrange("p (k n) -> p k n", k=8 if part < 2 else 4), w[j])\
                        .then_inc(S(f"slot{s}_loaded"), 16)
            pairs = EXPERTS // 2
            with sp.Fori(1, pairs) as q:
                load_pair(2 * q, 3 * q - 2)
            sp.wait_ge(S("npass_ready"), 1)
            n = sp.value_load(npass[0:1, 0:1], min_val=1, max_val=SEQ // CAP)
            with sp.If(n > 1):
                with sp.Fori(1, n) as p:
                    with sp.Fori(0, pairs) as q:
                        load_pair(2 * q, p * (3 * pairs) + 3 * q - 2)
            sp.wait_ge(S("y_sum"), n * (8 * TURNS) + 4)
            sp.dma_start(out_v, y_acc).then_inc(S("stored"), 16)
            sp.wait_ge(S("stored"), 16)

        @block.gpsimd
        def _(pool):
            chain = [0]

            def link(ins):
                chain[0] += 1
                ins.then_inc(S("pool_chain"), 1)
                pool.wait_ge(S("pool_chain"), chain[0])

            nc.gpsimd.memset(tri_ones[:, 0:2 * P], 1.0).then_inc(S("pool_chain"), 1)
            nc.gpsimd.memset(mask[:], 0.0).then_inc(S("pool_chain"), 1)
            chain[0] = 2
            link(nc.gpsimd.memset(ident[:], 0.0))
            link(nc.gpsimd.affine_select(out=ident[:], in_=ident[:], compare_op=ALU.not_equal, fill=1.0, base=0,
                                         pattern=[[-1, P]], channel_multiplier=1))
            nc.gpsimd.affine_select(out=tri, in_=tri, compare_op=ALU.is_ge, fill=0.0, base=0,
                                    pattern=[[1, P]], channel_multiplier=-1)
            nc.gpsimd.affine_select(out=mask[:, 0:P], in_=mask[:, 0:P], compare_op=ALU.is_ge, fill=NEG, base=0,
                                    pattern=[[-1, P]], channel_multiplier=1)
            nc.gpsimd.affine_select(out=mask[:, 2 * P:3 * P], in_=mask[:, 2 * P:3 * P], compare_op=ALU.is_ge, fill=NEG,
                                    base=0, pattern=[[-1, P]], channel_multiplier=1)
            nc.gpsimd.memset(minus_half[:], -0.5)
            for i in range(HALF):
                nc.gpsimd.memset(invf[:, i:i + 1], float(np.float32(10000.0) ** np.float32(-2.0 * i / ROPE)))
            for i in range(EPG):
                nc.gpsimd.memset(desc[:, i:i + 1], float(EPG - i))
            nc.gpsimd.iota(slot_no[:], pattern=[[1, CAP]], base=0, channel_multiplier=0,
                           allow_small_or_imprecise_dtypes=True).then_inc(S("consts"), 1)

            def power(name, n, count=1):
                pool.wait_ge(S(f"{name}_ms"), count)
                nc.gpsimd.tensor_tensor(rstd[:, 0:n], ms[:, 0:n], minus_half[:, 0:n], ALU.pow)\
                    .then_inc(S(f"{name}_rstd"), 1)

            power("norm", TT, 1)
            power("lat", 4)
            power("norm", TT, 2)
            power("norm", TT, 3)
            power("norm", TT, 4)
            power("q2", 16)
            power("k2", 16)
            power("cv", 16)
            power("sub", 8)
            power("norm", TT, 5)

        @block.scalar
        def _(act):
            chain = [0]

            def link(ins):
                chain[0] += 1
                ins.then_inc(S("act_chain"), 1)
                act.wait_ge(S("act_chain"), chain[0])

            def split(name, a=0, b=None):
                it = IT[name]
                for ci in range(a, len(it["chunks"]) if b is None else b):
                    c = it["c0"] + ci
                    if ci == 0:
                        act.wait_ge(S(f"slot{it['slot']}_loaded"), it["loaded"])
                    if c >= 2:
                        act.wait_ge(S("chunk_used"), c - 1)
                    src, n = raw_chunk(it, ci)
                    nc.scalar.activation(wh[:, c % 2, 0:n], src, ACT.Copy).then_inc(S("chunk_high"), 1)

            def done(name):
                act.wait_ge(S("chunk_used"), IT[name]["c1"])

            act.wait_ge(S("rows_zero"), 1)
            act.dma_start(x_tok, t["x"].rearrange("(t p) d -> p t d", p=P)).then_inc(S("x_loaded"), 16)
            n_rows = 0

            def row_dma(r, src, c0=0, n=P):
                i, p0 = divmod(r, P)
                k = src.shape[0]
                act.dma_start(rows[p0:p0 + k, i, c0:c0 + n], src).then_inc(S("rows_loaded"), 16)
                return 16

            def as_rows(a):
                return a.rearrange("o (r n) -> (o r) n", n=P)

            for key, name in (("c", "c"), ("b_ada", "b_ada"), ("norm_mix_g", "mix_g"), ("q_norm_g", "q_g"),
                              ("kv_norm_g", "kv_g"), ("norm_ffn_g", "ffn_g"), ("norm_final_g", "fin_g"),
                              ("attn_norm_g_2", "attn_g2"), ("conv_w_2", "conv_w2"), ("conv_out_g_2", "conv_out_g2"),
                              ("attn_subln_g_2", "subln"), ("ffn_norm_g_2", "ffn_g2"), ("conv_b", "conv_b")):
                n_rows += row_dma(ROW[name], as_rows(t[key]))
            for j, name in enumerate(("conv_w0", "conv_w1", "conv_w2_ff")):
                n_rows += row_dma(ROW[name], as_rows(t["conv_w"][j:j + 1, :]))
            for key, name in (("q_norm_g_2", "qg2"), ("k_norm_g_2", "kg2")):
                for h in range(2):
                    n_rows += row_dma(ROW[name], t[key], 64 * h, 64)
            for j, key in enumerate(("lambda_q1_2", "lambda_k1_2", "lambda_q2_2", "lambda_k2_2")):
                n_rows += row_dma(ROW["lam"] + j, t[key], 0, 64)
            assert n_rows == ROWS_TOTAL
            with nc.allow_non_contiguous_dma("few small rows"):
                act.dma_start(pos_i[:], t["positions"].rearrange("o (t p) -> p (o t)", p=P)).then_inc(S("misc_loaded"), 16)
                act.dma_start(bf_b[:], t["b_forget"].partition_broadcast(P) if t["b_forget"].ndim == 1 else
                              t["b_forget"][0].partition_broadcast(P)).then_inc(S("misc_loaded"), 16)
                act.dma_start(wr[:, :, 0:GROUPS], t["w_router_group_2"].rearrange("(k p) n -> p k n", p=P))\
                    .then_inc(S("misc_loaded"), 16)
                act.dma_start(wr[:, :, GROUPS:LG], t["w_router_expert_2"].rearrange("(k p) n -> p k n", p=P))\
                    .then_inc(S("misc_loaded"), 16)

            def norm_squares(n):
                act.wait_ge(S("xT_ready"), XT_READY[n])
                nc.scalar.activation(n_sq, xT[:], ACT.Square).then_inc(S("norm_sq"), 1)

            def norm_high(n, scale, shift):
                act.wait_ge(S("norm_xn"), n + 1)
                for k in range(KD):
                    nc.scalar.activation(hH[:, k, :], n_xn[:, k, :], ACT.Identity, scale=scale[:, k:k + 1],
                                         bias=shift[:, k:k + 1] if shift is not None else 0.0)\
                        .then_inc(S("norm_high"), 1)

            act.wait_ge(S("cols"), 1)
            nc.scalar.activation(cact[:], colT[:, ROW["c"]:ROW["c"] + KD], ACT.Silu).then_inc(S("cact"), 1)
            act.wait_ge(S("rope_angle"), 1)
            nc.scalar.activation(trig[:, 3], trig[:, 2], ACT.Sin).then_inc(S("rope_sin"), 1)
            nc.scalar.activation(trig[:, 4], trig[:, 2], ACT.Sin, scale=0.5).then_inc(S("rope_sin"), 1)
            norm_squares(0)
            split("cq", 0, 2)
            act.wait_ge(S("ada_cols"), 1)
            norm_high(0, scale_m, adaT[:, SH_M:SH_M + KD])
            split("cq", 2)
            split("ckv", 0, 2)
            split("ckv", 2)
            split("fq", 0, 2)
            act.wait_ge(S("lat_copied"), 4)
            for j, (c0, n) in enumerate(((0, Q_RANK), (Q_RANK, KV_RANK))):
                for tt in range(TT):
                    nc.scalar.activation(flatE[:, 4096 + 384 * (2 * j + tt):4096 + 384 * (2 * j + tt) + n],
                                         cqkv[:, tt, c0:c0 + n], ACT.Square,
                                         accum_out=ssq[:, 2 * j + tt:2 * j + tt + 1]).then_inc(S("lat_sq"), 1)
            split("fq", 2)
            split("fk", 0, 2)
            done("fq")
            for i in range(2):
                nc.scalar.activation(fqT[:, 2 * i:2 * i + 2, :].rearrange("p a b -> p (a b)"), ps[:, IT["fq"]["acc"] + i, :],
                                     ACT.Copy, scale=FOX_SCALE).then_inc(S("fq_out"), 1)
            split("fk", 2)
            split("fv", 0, 2)
            done("fk")
            for i in range(2):
                nc.scalar.activation(fkT[:, 2 * i:2 * i + 2, :].rearrange("p a b -> p (a b)"), ps[:, IT["fk"]["acc"] + i, :],
                                     ACT.Copy).then_inc(S("fk_out"), 1)
            split("fv", 2)
            split("uq0", 0, 2)
            for j in range(5):
                act.wait_ge(S("lat_turned"), j // 2 + 1)
                g = colT[:, ROW["q_g"] + j:ROW["q_g"] + j + 1]
                nc.scalar.activation(aH[:, j, :], ps[:, 4 + j // 2, 256 * (j % 2):256 * (j % 2) + 256], ACT.Copy, scale=g)\
                    .then_inc(S("lat_high"), 1)
            act.wait_ge(S("fz_abs"), 1)
            link(nc.scalar.activation(fz[:, 1], fz[:, 1], ACT.Exp))
            nc.scalar.activation(fz[:, 1], fz[:, 1], ACT.Ln, bias=1.0).then_inc(S("fz_ln"), 1)
            split("uq1", 0, 2)
            done("uq0")

            def uq_out(i):
                for tt in range(TT):
                    nc.scalar.activation(q_tok[:, tt, 4 * i:4 * i + 4, :].rearrange("p h n -> p (h n)"),
                                         ps[:, IT[f"uq{i}"]["acc"] + tt, 0:384], ACT.Copy).then_inc(S("uq_out"), 1)

            def ukv_out(i):
                for tt in range(TT):
                    kv = ps[:, IT[f"ukv{i}"]["acc"] + tt, :].rearrange("p (h n) -> p h n", h=4)
                    nc.scalar.activation(k_tok[:, tt, 4 * i:4 * i + 4, 0:NOPE], kv[:, :, 0:NOPE], ACT.Copy)\
                        .then_inc(S("ukv_out"), 1)
                    nc.scalar.activation(v_tok[:, tt, 256 * i:256 * i + 256].rearrange("p (h n) -> p h n", h=4),
                                         kv[:, :, NOPE:NOPE + VDIM], ACT.Copy).then_inc(S("ukv_out"), 1)

            uq_out(0)
            split("ukv0")
            done("uq1")
            uq_out(1)
            split("ukv1")
            done("ukv0")
            ukv_out(0)
            split("g0", 0, 1)
            done("ukv1")
            ukv_out(1)
            split("g0", 1)

            def gate_out(j):
                done(f"g{j}")
                for i in range(2):
                    nc.scalar.activation(sig[:, 4 * j + 2 * i:4 * j + 2 * i + 2, :].rearrange("p a b -> p (a b)"),
                                         ps[:, IT[f"g{j}"]["acc"] + i, :], ACT.Sigmoid).then_inc(S("gate_out"), 1)

            for j in range(1, 4):
                split(f"g{j}", 0, 2)
                gate_out(j - 1)
                split(f"g{j}", 2)
            split("om0", 0, 2)
            gate_out(3)
            for i in range(4):
                act.wait_ge(S("k_turned"), i + 1)
                nc.scalar.activation(kT[0:QK, 2 * i:2 * i + 2, :].rearrange("p a b -> p (a b)"), ps[0:QK, 6 + i % 2, :],
                                     ACT.Copy).then_inc(S("kT_out"), 1)

            def exps(a):
                act.wait_ge(S("att_max"), a + 1)
                for tt, (c0, n) in enumerate(((0, P), (P, 2 * P))):
                    v = prob[:, a % 3, c0:c0 + n]
                    nc.scalar.activation(v, v, ACT.Exp, bias=nmax[:, a % 3, tt:tt + 1],
                                         accum_out=rsum[:, a % 3, tt:tt + 1]).then_inc(S("att_exp"), 1)

            def turn_out(a, base):
                act.wait_ge(S("att_turned"), a + 1)
                if a >= base + 2:
                    act.wait_ge(S("att_pv"), a - 1)
                nc.scalar.activation(pT[:, a % 2, :], ps[:, 4 + a % 2, 0:3 * P], ACT.Copy).then_inc(S("att_pT"), 1)

            def o_high(j):
                act.wait_ge(S("att_pv"), 2 * j + 2)
                nc.scalar.activation(hH[:, (j + 4) % 8, :], ps[:, 6 + j % 2, 0:SEQ], ACT.Copy).then_inc(S("o_high"), 1)

            N1 = 2 * HEADS
            exps(0)
            for a in range(N1):
                if a + 1 < N1:
                    exps(a + 1)
                turn_out(a, 0)
                if a >= 2 and a % 2 == 0:
                    o_high(a // 2 - 1)
            o_high(HEADS - 1)
            split("om1")
            split("of0")
            split("of1")
            for m in range(KD):
                act.wait_ge(S("y_ready"), m // 2 + 1)
                nc.scalar.activation(aH[:, m, :], yF[:, m, :], ACT.Copy).then_inc(S("y_high"), 1)
            split("wo0")
            split("wo1")
            norm_squares(1)
            split("up0", 0, 2)
            act.wait_ge(S("ada_cols"), 3)
            norm_high(1, scale_f, adaT[:, SH_F:SH_F + KD])

            def conv_first(j):
                done(f"up{j}")
                if j >= 2:
                    act.wait_ge(S("act_f"), j - 1)
                for m in range(4):
                    tile = 2 * j + m if m < 2 else FT + 2 * j + m - 2
                    nc.scalar.activation(conv[:, j % 2, m, :], ps[:, IT[f"up{j}"]["acc"] + m // 2, 256 * (m % 2):256 * (m % 2) + 256],
                                         ACT.Identity, scale=colT[:, ROW["conv_w2_ff"] + tile:ROW["conv_w2_ff"] + tile + 1],
                                         bias=colT[:, ROW["conv_b"] + tile:ROW["conv_b"] + tile + 1]).then_inc(S("conv_1"), 1)

            def silu_gate(j):
                act.wait_ge(S("conv_2"), j + 1)
                v = conv[:, j % 2, 0:2, :]
                nc.scalar.activation(v, v, ACT.Silu).then_inc(S("silu"), 1)

            def ff_high(j):
                act.wait_ge(S("act_f"), j + 1)
                if j >= UP_A:
                    act.wait_ge(S("chunk_used"), IT["dn2"]["c1"])
                k = 2 * j if j < UP_A else 2 * (j - UP_A)
                nc.scalar.activation(aH[:, k:k + 2, :], actF[:, j % 2], ACT.Copy).then_inc(S("ff_high"), 1)

            def after_up(j, name):
                n = len(IT[name]["chunks"])
                split(name, 0, min(2, n))
                conv_first(j)
                split(name, 2, min(3, n))
                silu_gate(j)
                split(name, 3, n)
                ff_high(j)

            split("up0", 2)
            for j in range(1, UP_A):
                after_up(j - 1, f"up{j}")
            after_up(UP_A - 1, "dn0")
            split("dn1")
            split("dn2")
            split(f"up{UP_A}")
            for j in range(UP_A + 1, 11):
                after_up(j - 1, f"up{j}")
            after_up(10, "dn3")
            split("dn4")
            split("dn5")
            norm_squares(2)
            norm_squares(3)
            split("q2", 0, 2)
            norm_high(3, colT[:, ROW["attn_g2"]:ROW["attn_g2"] + KD], None)
            split("q2", 2)
            split("k2", 0, 2)
            act.wait_ge(S("q2_out"), 2)
            nc.scalar.activation(sq2, q2, ACT.Square).then_inc(S("q2_sq"), 1)
            split("k2", 2)
            split("v2", 0, 2)
            act.wait_ge(S("k2_out"), 2)
            act.wait_ge(S("q2_ms"), 1)
            nc.scalar.activation(sq2, k2, ACT.Square).then_inc(S("k2_sq"), 1)
            split("v2", 2)
            split("xc", 0, 2)
            done("v2")
            for tt in range(TT):
                nc.scalar.activation(v2[:, tt, :], ps[:, IT["v2"]["acc"] + tt, :], ACT.Copy).then_inc(S("v2_out"), 1)
            split("xc", 2)
            split("bg", 0, 2)
            done("xc")
            for i in range(2):
                nc.scalar.activation(cz[:, 2 * i:2 * i + 2, :].rearrange("p a b -> p (a b)"), ps[:, IT["xc"]["acc"] + i, :],
                                     ACT.Copy).then_inc(S("xc_out"), 1)
            split("bg", 2)
            split("cg", 0, 2)
            done("bg")
            for i in range(2):
                nc.scalar.activation(cb[:, 2 * i:2 * i + 2, :].rearrange("p a b -> p (a b)"), ps[:, IT["bg"]["acc"] + i, :],
                                     ACT.Copy).then_inc(S("bg_out"), 1)
            split("cg", 2)
            act.wait_ge(S("lam_sum"), 1)
            nc.scalar.activation(lam[:, 2:4], ps[:, 4, 0:2], ACT.Exp).then_inc(S("lam_exp"), 1)
            for i in range(2):
                act.wait_ge(S("k2_turned"), i + 1)
                nc.scalar.activation(kT2[:, 2 * i:2 * i + 2, :].rearrange("p a b -> p (a b)"), ps[:, 6 + i, :], ACT.Copy,
                                     scale=colT[:, ROW["kg2"]:ROW["kg2"] + 1]).then_inc(S("kT2_out"), 1)
            N2 = 2 * N_HEADS2

            def exps2(a):
                exps(N1 + a)

            def turn_out2(h):
                act.wait_ge(S("diff_turned"), h + 1)
                if h >= 2:
                    act.wait_ge(S("diff_pv"), h - 1)
                nc.scalar.activation(pT[:, h % 2, :], ps[:, 4 + h % 2, 0:3 * P], ACT.Copy).then_inc(S("diff_pT"), 1)

            exps2(0)
            exps2(1)
            for h in range(N_HEADS2):
                if h + 1 < N_HEADS2:
                    exps2(2 * h + 2)
                turn_out2(h)
                if h + 1 < N_HEADS2:
                    exps2(2 * h + 3)
            act.wait_ge(S("cy_ready"), 1)
            nc.scalar.activation(csq, cy, ACT.Square).then_inc(S("cv_sq"), 1)
            act.wait_ge(S("o2_out"), N_HEADS2)
            nc.scalar.activation(sq2, o2, ACT.Square).then_inc(S("sub_sq"), 1)
            act.wait_ge(S("mixF"), 4)
            nc.scalar.activation(aH[:, 0:4, :], mixF, ACT.Copy).then_inc(S("mix_high"), 1)
            for i in range(2):
                act.wait_ge(S("o2_turned"), i + 1)
                nc.scalar.activation(aH[:, 4 + 2 * i:6 + 2 * i, :].rearrange("p a b -> p (a b)"), ps[:, 4 + i, :], ACT.Copy,
                                     scale=sub8[:, 0:1]).then_inc(S("mix_high"), 1)
            split("w2o0")
            split("w2o1")
            norm_squares(4)
            act.wait_ge(S("g_shift"), 1)
            nc.scalar.activation(gexp, gtmp, ACT.Exp).then_inc(S("g_exp"), 1)
            for i in range(4):
                act.wait_ge(S("hn_turned"), i + 1)
                nc.scalar.activation(hnH[:, i // 2, 512 * (i % 2):512 * (i % 2) + 512], ps[:, 4 + i % 2, :], ACT.Copy)\
                    .then_inc(S("hn_high"), 1)
            act.wait_ge(S("e_shift"), 1)
            nc.scalar.activation(ed, ed, ACT.Exp).then_inc(S("e_exp"), 1)

            def gather_out(first, count):
                for i in range(4):
                    act.wait_ge(S("gathered"), count + i)
                    nc.scalar.activation(xg[:, 2 * i:2 * i + 2, :].rearrange("p a b -> p (a b)"), ps[:, 6 + i % 2, :], ACT.Copy)\
                        .then_inc(S("xg_out"), 1)

            act.wait_ge(S("npass_ready"), 1)
            n = act.value_load(npass[0:1, 0:1], min_val=1, max_val=SEQ // CAP)
            with act.Fori(0, n) as p:
                gather_out(True, p * (4 * TURNS + 4) + 1)
                with act.Fori(0, TURNS) as g:
                    turn = p * TURNS + g
                    act.wait_ge(S("put_turned"), turn + 1)
                    nc.scalar.activation(putT.rearrange("p a b -> p (a b)"), ps[:, 5, :], ACT.Copy).then_inc(S("putT_out"), 1)
                    for r in range(2):
                        act.wait_ge(S("expert_used"), turn * 6 + 3 * r + 1)
                        nc.scalar.activation(sg, ps[:, 0, :], ACT.Silu).then_inc(S("e_silu"), 1)
                        if r == 1:
                            gather_out(False, (p * (TURNS + 1) + g) * 4 + 5)
                        act.wait_ge(S("e_turned"), turn * 2 + r + 1)
                        nc.scalar.activation(eactT.rearrange("p a b -> p (a b)"), ps[:, 2, :], ACT.Copy).then_inc(S("e_actT"), 1)
                        act.wait_ge(S("expert_used"), turn * 6 + 3 * r + 3)
                        nc.scalar.activation(eout, ps[:, 3:5, :].rearrange("p a b -> p (a b)"), ACT.Copy)\
                            .then_inc(S("e_out"), 1)

        @block.tensor
        def _(pe):
            def mm(o_, l, r, start, stop):
                return nc.tensor.matmul(o_, l, r, start=start, stop=stop, skip_group_check=True)

            def linear(name, xh, xl, by_token, k_base=0, k_total=None, banks=None, extra=None):
                it = IT[name]
                n, k_total = it["n"], k_total or it["kn"]
                b0 = it["acc"] if banks is None else banks
                main = min(n, 512)
                for ci, (k0, kn) in enumerate(it["chunks"]):
                    c = it["c0"] + ci
                    pe.wait_ge(S("chunk_low"), c + 1)
                    for kk in range(kn):
                        k = k0 + kk
                        kx = k_base + k if banks is None else k_base + k
                        first, last = k == 0 and (banks is None or k_base == 0 and DOWN_FIRST[0]), k == k_total - 1
                        h = wh[:, c % 2, kk * n:(kk + 1) * n]
                        l = wl[:, c % 2, kk * n:(kk + 1) * n]
                        if by_token:
                            for tt in range(TT):
                                ts = slice(tt * P, tt * P + P)
                                o_ = ps[:, b0 + tt, 0:main]
                                mm(o_, xh[:, kx, ts], h[:, 0:main], first, False)
                                mm(o_, xl[:, kx, ts], h[:, 0:main], False, False)
                                ins = mm(o_, xh[:, kx, ts], l[:, 0:main], False, last)
                                if n > main:
                                    o_ = ps[:, 4, tt * (n - main):(tt + 1) * (n - main)]
                                    mm(o_, xh[:, kx, ts], h[:, main:n], first and tt == 0, False)
                                    mm(o_, xl[:, kx, ts], h[:, main:n], False, False)
                                    ins = mm(o_, xh[:, kx, ts], l[:, main:n], False, last)
                        else:
                            for m in range(n // P):
                                cs = slice(m * P, m * P + P)
                                o_ = ps[:, b0 + m // 2, 256 * (m % 2):256 * (m % 2) + 256]
                                mm(o_, h[:, cs], xh[:, kx, :], first and m % 2 == 0, False)
                                mm(o_, h[:, cs], xl[:, kx, :], False, False)
                                ins = mm(o_, l[:, cs], xh[:, kx, :], False, last)
                    ins.then_inc(S("chunk_used"), 1)

            DOWN_FIRST = [True]

            def ada(third):
                for i in range(4):
                    it = IT[f"ada{third}{i}"]
                    pe.wait_ge(S(f"slot{it['slot']}_loaded"), it["loaded"])
                    w = slot_view(it)
                    for kk in range(2):
                        k = 2 * i + kk
                        for q in range(4):
                            ins = mm(ps[32 * q:32 * q + 1, 7, :], cact[:, k:k + 1], w[:, kk, 512 * q:512 * q + 512],
                                     k == 0, k == KD - 1)
                    ins.then_inc(S("ada_used"), 1)
                pe.wait_ge(S("ada_row"), 4 * third + 4)
                for s in range(4):
                    ins = nc.tensor.transpose(ps[:, 6, s * P:s * P + P], ada_row[:, s * P:s * P + P], ident[:])
                ins.then_inc(S("ada_turned"), 1)

            def norm(n, last_wait=None):
                pe.wait_ge(S("norm_red"), n + 1)
                for tt in range(TT):
                    ins = mm(ps[:, 4, tt:tt + 1], n_red[:, tt * P:tt * P + P], ones[:, 0:1], tt == 0, True)
                ins.then_inc(S("norm_sum"), 1)
                pe.wait_ge(S("norm_rstd"), n + 1)
                for tt in range(TT):
                    ins = mm(ps[:, 5, tt * P:tt * P + P], rstd[:, tt:tt + 1].to_broadcast([P, P]), ident[:], tt == 0, True)
                ins.then_inc(S("norm_bc"), 1)

            pe.wait_ge(S("consts"), 1)
            pe.wait_ge(S("rows_loaded"), ROWS_TOTAL)
            for i in range(3):
                ins = nc.tensor.transpose(ps[:, 0, i * P:i * P + P], rows[:, i, :], ident[:])
            ins.then_inc(S("rows_turned"), 1)
            pe.wait_ge(S("x_loaded"), 16)
            for i in range(4):
                for kk in range(2):
                    for tt in range(TT):
                        k = 2 * i + kk
                        ins = nc.tensor.transpose(ps[:, 1 + i, 256 * kk + P * tt:256 * kk + P * tt + P],
                                                  x_tok[:, tt, k * P:k * P + P], ident[:])
                ins.then_inc(S("x_turned"), 1)
            pe.wait_ge(S("xT_ready"), 4)
            norm(0)
            pe.wait_ge(S("cact"), 1)
            ada(0)
            pe.wait_ge(S("norm_in"), SPLIT_NORM[0])
            linear("cq", hH, hL, True)
            linear("ckv", hH, hL, True)
            pe.wait_ge(S("lat_copied"), 2)
            linear("fq", hH, hL, False)
            pe.wait_ge(S("lat_copied"), 4)
            linear("fk", hH, hL, False)
            pe.wait_ge(S("fq_out"), 2)
            linear("fv", hH, hL, True)
            pe.wait_ge(S("lat_n"), 1)
            pe.wait_ge(S("fz_in"), 1)
            for j in range(5):
                for tt in range(TT):
                    src = cqkv[:, tt, j * P:j * P + P]
                    ins = nc.tensor.transpose(ps[:, 4 + j // 2, 256 * (j % 2) + P * tt:256 * (j % 2) + P * tt + P], src, ident[:])
                if j % 2 or j == 4:
                    ins.then_inc(S("lat_turned"), 1)
            pe.wait_ge(S("logf"), 1)
            logf = fz[:, 2]
            mm(ps[:, 7, 0:8], tri, logf[:, 0, :], True, True)
            mm(ps[:, 7, 8:16], ones, logf[:, 0, :], False, False)
            mm(ps[:, 7, 8:16], tri, logf[:, 1, :], False, True)
            mm(ps[0:8, 7, 256:512], logf[:, 0, :], tri_ones[:], False, False)
            mm(ps[0:8, 7, 384:512], logf[:, 1, :], tri, False, True).then_inc(S("f_cum"), 1)
            pe.wait_ge(S("lat_low"), 5)
            pe.wait_ge(S("fk_out"), 2)
            linear("uq0", aH, aL, True)
            pe.wait_ge(S("fv_out"), 2)
            linear("uq1", aH, aL, True)
            pe.wait_ge(S("uq_out"), 2)
            linear("ukv0", aH[:, 3:5], aL[:, 3:5], True)
            pe.wait_ge(S("uq_out"), 4)
            linear("ukv1", aH[:, 3:5], aL[:, 3:5], True)
            for j in range(4):
                if j < 2:
                    pe.wait_ge(S("ukv_out"), 4 * j + 4)
                else:
                    pe.wait_ge(S("gate_out"), 2 * j - 2)
                linear(f"g{j}", hH, hL, False)
            pe.wait_ge(S("rope_done"), 1)
            for i in range(4):
                for src, bank, sem, free in ((q_tok, 4, "q_turned", "qT_out"), (k_tok, 6, "k_turned", "kT_out")):
                    if i >= 2:
                        pe.wait_ge(S(free), i - 1)
                    elif bank == 6 and i == 1:
                        pe.wait_ge(S("f_out"), 2)
                    for hh in range(2):
                        for tt in range(TT):
                            c0 = 256 * hh + P * tt
                            ins = nc.tensor.transpose(ps[0:QK, bank + i % 2, c0:c0 + P], src[:, tt, 2 * i + hh, :], ident[:])
                    ins.then_inc(S(sem), 1)

            def scores(a):
                if a >= 4:
                    pe.wait_ge(S("att_in"), a - 3)
                h = a % HEADS
                for tt, (c0, n) in enumerate(((0, P), (P, 2 * P))):
                    o_ = ps[:, a % 4, c0:c0 + n]
                    qs = slice(tt * P, tt * P + P)
                    if a < HEADS:
                        r = slice(64 * (h % 2), 64 * (h % 2) + 64)
                        mm(o_, fqT[r, h // 2, qs], fkT[r, h // 2, 0:n], tt == 0, False)
                        ins = mm(o_, ident[0:HEADS, h:h + 1].to_broadcast([HEADS, P]), nFT[:, 0:n], False, True)
                    else:
                        ins = mm(o_, qT[0:QK, h, qs], kT[0:QK, h, 0:n], tt == 0, True)
                ins.then_inc(S("att_logits"), 1)

            def turn(a):
                pe.wait_ge(S("att_p"), a + 1)
                if a >= 2:
                    pe.wait_ge(S("att_pT"), a - 1)
                for i, c0 in enumerate((0, P, 2 * P)):
                    ins = nc.tensor.transpose(ps[:, 4 + a % 2, i * P:i * P + P], prob[:, a % 3, c0:c0 + P], ident[:])
                ins.then_inc(S("att_turned"), 1)

            def values(a):
                pe.wait_ge(S("att_pT"), a + 1)
                j = a // 2
                if a % 2 == 0 and j >= 2:
                    pe.wait_ge(S("o_low"), j - 1)
                h = a % HEADS
                v = fv_tok if a < HEADS else v_tok
                r = slice(64 * (a % 2), 64 * (a % 2) + 64)
                mm(ps[r, 6 + j % 2, 0:SEQ], v[:, 0, 64 * h:64 * h + 64], pT[:, a % 2, 0:SEQ], True, False)
                mm(ps[r, 6 + j % 2, P:SEQ], v[:, 1, 64 * h:64 * h + 64], pT[:, a % 2, SEQ:SEQ + P], False, True)\
                    .then_inc(S("att_pv"), 1)

            N1 = 2 * HEADS
            pe.wait_ge(S("f_out"), 2)
            pe.wait_ge(S("gate_out"), 8)
            pe.wait_ge(S("qT_out"), 4)
            pe.wait_ge(S("kT_out"), 4)
            scores(0)
            scores(1)
            for a in range(N1):
                if a + 2 < N1:
                    scores(a + 2)
                turn(a)
                if a >= 1:
                    values(a - 1)
            values(N1 - 1)
            pe.wait_ge(S("o_low"), HEADS)
            linear("om0", hH, hL, False)
            linear("om1", hH, hL, False)
            pe.wait_ge(S("om_out"), 2)
            linear("of0", hH[:, 4:8], hL[:, 4:8], False)
            pe.wait_ge(S("om_out"), 4)
            linear("of1", hH[:, 4:8], hL[:, 4:8], False)
            ada(1)
            pe.wait_ge(S("y_low"), 1)
            linear("wo0", aH, aL, False)
            linear("wo1", aH, aL, False)
            ada(2)
            norm(1)
            pe.wait_ge(S("norm_in"), SPLIT_NORM[1])
            for j in range(UP_A):
                if j >= 2:
                    pe.wait_ge(S("act_f"), j - 1)
                linear(f"up{j}", hH, hL, False)
            pe.wait_ge(S("norm_xn"), 2)
            for i in range(3):
                pe.wait_ge(S("ff_low"), 2 * i + 2)
                DOWN_FIRST[0] = i == 0
                linear(f"dn{i}", aH[:, 4 * i:4 * i + 4], aL[:, 4 * i:4 * i + 4], False, 0, 99, 4)
            DOWN_FIRST[0] = False
            for j in range(UP_A, 11):
                pe.wait_ge(S("act_f"), j - 1)
                linear(f"up{j}", hH, hL, False)
            for i in range(3, 6):
                pe.wait_ge(S("ff_low"), min(2 * i + 2, 11))
                k = 4 * (i - 3)
                linear(f"dn{i}", aH[:, k:k + 4], aL[:, k:k + 4], False, 0, IT["dn5"]["kn"] if i == 5 else 99, 4)
            norm(2)
            norm(3)
            pe.wait_ge(S("norm_in"), SPLIT_NORM[3])
            linear("q2", hH, hL, True)
            linear("k2", hH, hL, True)
            pe.wait_ge(S("q2_out"), 2)
            linear("v2", hH, hL, True)
            pe.wait_ge(S("k2_out"), 2)
            linear("xc", hH, hL, False)
            pe.wait_ge(S("v2_out"), 2)
            linear("bg", hH, hL, False)
            pe.wait_ge(S("xc_out"), 2)
            linear("cg", hH, hL, False)
            pe.wait_ge(S("lam_prod"), 1)
            mm(ps[:, 4, 0:2], ones, lam[:, 0:2], True, True).then_inc(S("lam_sum"), 1)
            pe.wait_ge(S("lam_exp"), 1)
            for src, bank, ready, sem in ((qn, 4, "qn", "q2_turned"), (kn, 6, "kn", "k2_turned")):
                pe.wait_ge(S(ready), 1)
                for i in range(2):
                    for hh in range(2):
                        for tt in range(TT):
                            h = 2 * i + hh
                            ins = nc.tensor.transpose(ps[:, bank + i, 256 * hh + P * tt:256 * hh + P * tt + P],
                                                      src[:, tt, h * P:h * P + P], ident[:])
                    ins.then_inc(S(sem), 1)

            def scores2(a):
                h, c = divmod(a, 2)
                if a >= 4:
                    pe.wait_ge(S("att_in"), N1 + a - 3)
                r = slice(64 * c, 64 * c + 64)
                for tt, (c0, n) in enumerate(((0, P), (P, 2 * P))):
                    ins = mm(ps[:, a % 4, c0:c0 + n], qT2[r, h, tt * P:tt * P + P], kT2[r, h, 0:n], tt == 0, True)
                ins.then_inc(S("att_logits"), 1)

            def turn2(h):
                pe.wait_ge(S("diff_p"), h + 1)
                if h >= 2:
                    pe.wait_ge(S("diff_pT"), h - 1)
                for i, c0 in enumerate((0, P, 2 * P)):
                    ins = nc.tensor.transpose(ps[:, 4 + h % 2, i * P:i * P + P], prob[:, (N1 + 2 * h) % 3, c0:c0 + P], ident[:])
                ins.then_inc(S("diff_turned"), 1)

            def values2(h):
                pe.wait_ge(S("diff_pT"), h + 1)
                if h >= 2:
                    pe.wait_ge(S("o2_out"), h - 1)
                vs = slice(h * V2, h * V2 + V2)
                mm(ps[:, 6 + h % 2, 0:P], pT[:, h % 2, 0:P], v2[:, 0, vs], True, True)
                mm(ps[:, 6 + h % 2, P:2 * P], pT[:, h % 2, P:2 * P], v2[:, 0, vs], False, False)
                mm(ps[:, 6 + h % 2, P:2 * P], pT[:, h % 2, 2 * P:3 * P], v2[:, 1, vs], False, True).then_inc(S("diff_pv"), 1)

            pe.wait_ge(S("bg_out"), 2)
            pe.wait_ge(S("cg_out"), 2)
            pe.wait_ge(S("qT2_out"), 2)
            pe.wait_ge(S("kT2_out"), 2)
            scores2(0)
            scores2(1)
            for h in range(N_HEADS2):
                if h + 1 < N_HEADS2:
                    scores2(2 * h + 2)
                    scores2(2 * h + 3)
                turn2(h)
                if h >= 1:
                    values2(h - 1)
            values2(N_HEADS2 - 1)
            pe.wait_ge(S("cv_sq"), 1)
            for tt in range(TT):
                for m in range(4):
                    c0 = 8 * tt + 2 * m
                    ins = mm(ps[:, 0, c0:c0 + 2], csq[:, m, tt * P:tt * P + P], half_ind[:], tt == 0 and m == 0, True)
            ins.then_inc(S("cv_sum"), 1)
            pe.wait_ge(S("cv_rstd"), 1)
            for m in range(4):
                for tt in range(TT):
                    for g in range(2):
                        c0 = 8 * tt + 2 * m + g
                        ins = mm(ps[64 * g:64 * g + 64, 2 + m // 2, 256 * (m % 2) + P * tt:256 * (m % 2) + P * tt + P],
                                 rstd[:, c0:c0 + 1].to_broadcast([P, 64]), ident[:], tt == 0 and m % 2 == 0, True)
            ins.then_inc(S("cv_bc"), 1)
            pe.wait_ge(S("sub_n"), 1)
            for i in range(2):
                for hh in range(2):
                    for tt in range(TT):
                        h = 2 * i + hh
                        ins = nc.tensor.transpose(ps[:, 4 + i, 256 * hh + P * tt:256 * hh + P * tt + P],
                                                  o2[:, tt, h * P:h * P + P], ident[:])
                ins.then_inc(S("o2_turned"), 1)
            pe.wait_ge(S("mix_ready"), 1)
            linear("w2o0", aH, aL, False)
            linear("w2o1", aH, aL, False)
            norm(4)
            pe.wait_ge(S("norm_in"), SPLIT_NORM[4])
            pe.wait_ge(S("misc_loaded"), 64)
            for tt in range(TT):
                for k in range(KD):
                    ins = mm(ps[:, 6, tt * 64:tt * 64 + LG], n_sq[:, k, tt * P:tt * P + P], wr[:, k, :],
                             tt == 0 and k == 0, k == KD - 1)
            ins.then_inc(S("logits"), 1)
            for i in range(4):
                if i >= 2:
                    pe.wait_ge(S("hn_low"), i - 1)
                for j in range(4):
                    k = 4 * (i % 2) + j
                    ins = nc.tensor.transpose(ps[:, 4 + i % 2, j * P:j * P + P], n_sq[:, k, (i // 2) * P:(i // 2) * P + P], ident[:])
                ins.then_inc(S("hn_turned"), 1)
            for i in range(4):
                for j in range(4):
                    k = 4 * (i % 2) + j
                    ins = nc.tensor.transpose(ps[:, i, j * P:j * P + P], xT[:, k, (i // 2) * P:(i // 2) * P + P], ident[:])
                ins.then_inc(S("res_turned"), 1)
            pe.wait_ge(S("sel"), 1)
            s0, s1 = (sel[:, tt].rearrange("p g e -> p (g e)") for tt in range(TT))
            mm(ps[:, 7, 0:32], tri, s0, True, True)
            mm(ps[:, 7, 32:64], ones, s0, False, False)
            mm(ps[:, 7, 32:64], tri, s1, False, True)
            mm(ps[0:1, 7, 64:96], ones[:, 0:1], s0, False, False)
            mm(ps[0:1, 7, 64:96], ones[:, 0:1], s1, False, True).then_inc(S("places"), 1)
            pe.wait_ge(S("y_sum"), 4)
            pe.wait_ge(S("hn_low"), 4)

            pe.wait_ge(S("npass_ready"), 1)
            n = pe.value_load(npass[0:1, 0:1], min_val=1, max_val=SEQ // CAP)

            def gather_body(count, gidx, part):
                pe.wait_ge(S("pick_half"), count * 2)
                pe.wait_ge(S("y_sum"), part)
                for i in range(4):
                    if i >= 2:
                        pe.wait_ge(S("xg_out"), gidx * 4 + i - 1)
                    for kk in range(2):
                        k = 2 * i + kk
                        o_ = ps[:, 6 + i % 2, 256 * kk:256 * kk + 256]
                        for tt in range(TT):
                            mm(o_, hnH[:, tt, k * P:k * P + P], pick[:, tt, :], kk == 0 and tt == 0, False)
                            ins = mm(o_, hnL[:, tt, k * P:k * P + P], pick[:, tt, :], False, tt == TT - 1)
                    ins.then_inc(S("gathered"), 1)

            with pe.Fori(0, n) as p:
                gather_body(p * (TURNS + 1) + 1, p * (TURNS + 1), p * (8 * TURNS) + 4)
                with pe.Fori(0, TURNS) as g:
                    turn = p * TURNS + g
                    gidx = p * (TURNS + 1) + g
                    pe.wait_ge(S("put_half"), gidx * 2 + 2)
                    for r in range(2):
                        for tt in range(TT):
                            ins = nc.tensor.transpose(ps[:, 5, 256 * r + P * tt:256 * r + P * tt + P],
                                                      put[:, tt, P * r:P * r + P], ident[:])
                    ins.then_inc(S("put_turned"), 1)
                    pe.wait_ge(S("xg_out"), gidx * 4 + 4)
                    for r in range(2):
                        for part in range(2):
                            for j in range(2):
                                s = 2 * part + j
                                pe.wait_ge(S(f"slot{s}_loaded"), turn * 32 + base_loaded[s] + 16 * r + 16)
                            for k in range(KD):
                                for j in range(2):
                                    cs = slice(64 * (2 * r + j), 64 * (2 * r + j) + 64)
                                    w = ring[:, 2 * part + j, 512 * k:512 * k + 512]
                                    ins = mm(ps[64 * j:64 * j + 64, part, :], xg[:, k, cs], w, k == 0, k == KD - 1)
                            ins.then_inc(S("expert_used"), 1)
                        if r == 1:
                            gather_body(gidx + 2, gidx + 1, turn * 8 + 8)
                        pe.wait_ge(S("e_act"), turn * 2 + r + 1)
                        for f in range(4):
                            ins = nc.tensor.transpose(ps[:, 2, f * P:f * P + P], eact[:, f * P:f * P + P], ident[:])
                        ins.then_inc(S("e_turned"), 1)
                        pe.wait_ge(S("e_actT"), turn * 2 + r + 1)
                        for j in range(2):
                            s = 4 + j
                            pe.wait_ge(S(f"slot{s}_loaded"), turn * 32 + base_loaded[s] + 16 * r + 16)
                        for hf in range(2):
                            for k in range(4):
                                for j in range(2):
                                    w = ring[:, 4 + j, D * k + 512 * hf:D * k + 512 * hf + 512]
                                    ins = mm(ps[64 * j:64 * j + 64, 3 + hf, :], eactT[:, k, 64 * j:64 * j + 64], w,
                                             k == 0, k == 3)
                        ins.then_inc(S("expert_used"), 1)
                        pe.wait_ge(S("e_out"), turn * 2 + r + 1)
                        pe.wait_ge(S("putT_out"), turn + 1)
                        if r == 1:
                            pe.wait_ge(S("xg_out"), gidx * 4 + 8)
                        for i in range(4):
                            tt, hf = divmod(i, 2)
                            if i >= 2:
                                pe.wait_ge(S("y_sum"), turn * 8 + 4 * r + 4 + i - 1)
                            mm(ps[:, 6 + i % 2, :], putT[:, r, P * tt:P * tt + P], eout[:, 512 * hf:512 * hf + 512],
                               True, True).then_inc(S("e_put"), 1)

        @block.vector
        def _(dve):
            chain = [0]
            V = nc.vector

            def link(ins):
                chain[0] += 1
                ins.then_inc(S("dve_chain"), 1)
                dve.wait_ge(S("dve_chain"), chain[0])

            def split(name, a=0, b=None):
                it = IT[name]
                for ci in range(a, len(it["chunks"]) if b is None else b):
                    c = it["c0"] + ci
                    dve.wait_ge(S("chunk_high"), c + 1)
                    src, n = raw_chunk(it, ci)
                    V.tensor_tensor(wl[:, c % 2, 0:n], src, wh[:, c % 2, 0:n].bitcast(F32), ALU.subtract)\
                        .then_inc(S("chunk_low"), 1)

            def done(name):
                dve.wait_ge(S("chunk_used"), IT[name]["c1"])

            def mean_sq(dst, src, width, sem):
                V.tensor_scalar(dst, src, 1.0 / width, EPS, ALU.mult, ALU.add).then_inc(S(sem), 1)

            def norm_a(n):
                dve.wait_ge(S("norm_sq"), n + 1)
                V.tensor_reduce(n_red, n_sq.rearrange("p k n -> p n k"), AX_X, ALU.add).then_inc(S("norm_red"), 1)
                dve.wait_ge(S("norm_sum"), n + 1)
                mean_sq(ms[:, 0:TT], ps[:, 4, 0:TT], D, "norm_ms")
                dve.wait_ge(S("norm_bc"), n + 1)
                V.tensor_tensor(n_xn, xT[:], ps[:, 5, 0:SEQ].unsqueeze(1).to_broadcast([P, KD, SEQ]), ALU.mult)\
                    .then_inc(S("norm_xn"), 1)

            def norm_b(n, scale, shift, dst):
                dve.wait_ge(S("norm_xn"), n + 1)
                for k in range(KD):
                    if shift is not None:
                        ins = V.tensor_scalar(dst[:, k, :], n_xn[:, k, :], scale[:, k:k + 1], shift[:, k:k + 1],
                                              ALU.mult, ALU.add)
                    else:
                        ins = V.tensor_scalar(dst[:, k, :], n_xn[:, k, :], scale[:, k:k + 1], None, ALU.mult)
                return ins

            def norm_low(n):
                dve.wait_ge(S("norm_high"), KD * SPLIT_NORM[n])
                V.tensor_tensor(hL[:], n_sq, hH[:].bitcast(F32), ALU.subtract).then_inc(S("norm_in"), 1)

            for g in range(2):
                V.memset(half_ind[64 * g:64 * g + 64, g:g + 1], 1.0)
                V.memset(half_ind[64 * g:64 * g + 64, 1 - g:2 - g], 0.0)
            V.memset(wc[:, 0:3 * P + 512], 0.0).then_inc(S("rows_zero"), 1)
            dve.wait_ge(S("rows_turned"), 1)
            V.tensor_copy(colT[:], ps[:, 0, 0:3 * P]).then_inc(S("cols"), 1)
            for i in range(4):
                dve.wait_ge(S("x_turned"), i + 1)
                V.tensor_copy(xT[:, 2 * i:2 * i + 2, :].rearrange("p a b -> p (a b)"), ps[:, 1 + i, :])\
                    .then_inc(S("xT_ready"), 1)
            dve.wait_ge(S("misc_loaded"), 64)
            dve.wait_ge(S("consts"), 1)
            link(V.tensor_copy(pos_f[:], pos_i[:]))
            for tt in range(TT):
                ins = V.tensor_scalar(trig[:, 0, tt], invf[:], pos_f[:, tt:tt + 1], None, ALU.mult)
            link(ins)
            magic = 1.5 * 2.0 ** 23
            link(V.tensor_scalar(trig[:, 1], trig[:, 0], 1.0 / (2 * math.pi), None, ALU.mult))
            link(V.tensor_scalar(trig[:, 1], trig[:, 1], magic, None, ALU.add))
            link(V.tensor_scalar(trig[:, 1], trig[:, 1], magic, None, ALU.subtract))
            cur = trig[:, 0]
            for part in two_pi_parts():
                link(V.scalar_tensor_tensor(out=trig[:, 2], in0=trig[:, 1], scalar=-part, in1=cur, op0=ALU.mult, op1=ALU.add))
                cur = trig[:, 2]
            pi_lo = float(np.nextafter(np.float32(math.pi), np.float32(0)))
            V.tensor_scalar(trig[:, 2], trig[:, 2], pi_lo, -pi_lo, ALU.min, ALU.max).then_inc(S("rope_angle"), 1)
            norm_a(0)
            dve.wait_ge(S("rope_sin"), 2)
            link(V.tensor_tensor(trig[:, 1], trig[:, 4], trig[:, 4], ALU.mult))
            V.tensor_scalar(trig[:, 4], trig[:, 1], -2.0, 1.0, ALU.mult, ALU.add).then_inc(S("trig"), 1)
            sin_t, cos_t = trig[:, 3], trig[:, 4]

            def ada_out(third):
                dve.wait_ge(S("ada_used"), 4 * third + 4)
                for q in range(4):
                    V.tensor_copy(ada_row[32 * q:32 * q + 1, :], ps[32 * q:32 * q + 1, 7, :]).then_inc(S("ada_row"), 1)
                dve.wait_ge(S("ada_turned"), third + 1)
                src = ps[:, 6, :].rearrange("p (s q r) -> p q s r", s=4, q=4)[:, :, :, 0]
                dst = adaT[:, 16 * third:16 * third + 16].rearrange("p (q s) -> p q s", q=4)
                b = colT[:, ROW["b_ada"] + 16 * third:ROW["b_ada"] + 16 * third + 16].rearrange("p (q s) -> p q s", q=4)
                link(V.tensor_tensor(dst, src, b, ALU.add))

            ada_out(0)
            V.scalar_tensor_tensor(out=scale_m[:], in0=adaT[:, SC_M:SC_M + KD], scalar=1.0,
                                   in1=colT[:, ROW["mix_g"]:ROW["mix_g"] + KD], op0=ALU.add, op1=ALU.mult)\
                .then_inc(S("ada_cols"), 1)
            split("cq", 0, 2)
            dve.wait_ge(S("ada_cols"), 1)
            link(norm_b(0, scale_m, adaT[:, SH_M:SH_M + KD], n_sq))
            norm_low(0)
            split("cq", 2)
            split("ckv", 0, 2)
            done("cq")
            for tt in range(TT):
                V.tensor_copy(cqkv[:, tt, 0:Q_RANK], ps[:, IT["cq"]["acc"] + tt, 0:Q_RANK]).then_inc(S("lat_copied"), 1)
            split("ckv", 2)
            split("fq", 0, 2)
            done("ckv")
            for tt in range(TT):
                V.tensor_copy(cqkv[:, tt, Q_RANK:CKQ], ps[:, IT["ckv"]["acc"] + tt, 0:CKQ - Q_RANK]).then_inc(S("lat_copied"), 1)
            split("fq", 2)
            dve.wait_ge(S("lat_sq"), 4)
            link(V.tensor_scalar(ms[:, 0:2], ssq[:, 0:2], 1.0 / Q_RANK, EPS, ALU.mult, ALU.add))
            mean_sq(ms[:, 2:4], ssq[:, 2:4], KV_RANK, "lat_ms")
            split("fk", 0, 2)
            dve.wait_ge(S("lat_rstd"), 1)
            for j, (c0, n) in enumerate(((0, Q_RANK), (Q_RANK, KV_RANK))):
                for tt in range(TT):
                    v = cqkv[:, tt, c0:c0 + n]
                    ins = V.tensor_scalar(v, v, rstd[:, 2 * j + tt:2 * j + tt + 1], None, ALU.mult)
            ins.then_inc(S("lat_n"), 1)
            split("fk", 2)
            split("fv")
            split("uq0", 0, 1)
            done("fv")
            link(V.tensor_tensor(fz[:, 0], ps[:, 4, 0:TT * HEADS].rearrange("p (t h) -> p t h", t=TT),
                                 bf_b[:].unsqueeze(1).to_broadcast([P, TT, HEADS]), ALU.add))
            V.scalar_tensor_tensor(out=fz[:, 1], in0=fz[:, 0], scalar=-1.0, in1=fz[:, 0], op0=ALU.mult, op1=ALU.min)\
                .then_inc(S("fz_abs"), 1)
            V.tensor_scalar(fz[:, 0], fz[:, 0], 0.0, None, ALU.min).then_inc(S("fz_in"), 1)
            for tt in range(TT):
                V.tensor_copy(fv_tok[:, tt, :], ps[:, IT["fv"]["acc"] + tt, :]).then_inc(S("fv_out"), 1)
            for j in range(5):
                dve.wait_ge(S("lat_high"), min(2 * (j // 2) + 2, 5))
                g = colT[:, ROW["q_g"] + j:ROW["q_g"] + j + 1]
                V.scalar_tensor_tensor(out=aL[:, j, :], in0=ps[:, 4 + j // 2, 256 * (j % 2):256 * (j % 2) + 256], scalar=g,
                                       in1=aH[:, j, :].bitcast(F32), op0=ALU.mult, op1=ALU.subtract).then_inc(S("lat_low"), 1)
            dve.wait_ge(S("fz_ln"), 1)
            V.tensor_tensor(fz[:, 2], fz[:, 0], fz[:, 1], ALU.subtract).then_inc(S("logf"), 1)
            split("uq0", 1)
            split("uq1")
            dve.wait_ge(S("f_cum"), 1)
            V.tensor_copy(f_tok[:].rearrange("p t h -> p (t h)"), ps[:, 7, 0:TT * HEADS]).then_inc(S("f_out"), 1)
            V.tensor_scalar(nFT[:], ps[0:HEADS, 7, 256:512], -1.0, None, ALU.mult).then_inc(S("f_out"), 1)
            split("ukv0")
            split("ukv1")
            split("g0", 0, 1)

            def rope(x1, x2, cos_b, sin_b, tmp_a, tmp_b, last_sem):
                V.tensor_tensor(tmp_a, x2, sin_b, ALU.mult)
                link(V.tensor_tensor(tmp_b, x1, sin_b, ALU.mult))
                V.tensor_tensor(x1, x1, cos_b, ALU.mult)
                link(V.tensor_tensor(x2, x2, cos_b, ALU.mult))
                V.tensor_tensor(x1, x1, tmp_a, ALU.subtract)
                ins = V.tensor_tensor(x2, x2, tmp_b, ALU.add)
                if last_sem:
                    ins.then_inc(S(last_sem), 1)
                else:
                    link(ins)

            dve.wait_ge(S("trig"), 1)
            r0 = Q_RANK + KV_RANK
            ta = wc[:, 1408:1408 + TT * HALF].rearrange("p (t n) -> p t n", t=TT)
            tb = wc[:, 1664:1664 + TT * HALF].rearrange("p (t n) -> p t n", t=TT)
            rope(cqkv[:, :, r0:r0 + HALF], cqkv[:, :, r0 + HALF:r0 + ROPE], cos_t, sin_t, ta, tb, None)
            for tt in range(TT):
                V.tensor_copy(k_tok[:, tt, :, NOPE:QK], cqkv[:, tt, r0:r0 + ROPE].unsqueeze(1).to_broadcast([P, HEADS, ROPE]))
            dve.wait_ge(S("uq_out"), 4)
            ta = wc[:, 1408:1664].rearrange("p (t h n) -> p t h n", t=TT, h=HEADS)
            tb = wc[:, 1664:1920].rearrange("p (t h n) -> p t h n", t=TT, h=HEADS)
            cos_b = cos_t.unsqueeze(2).to_broadcast([P, TT, HEADS, HALF])
            sin_b = sin_t.unsqueeze(2).to_broadcast([P, TT, HEADS, HALF])
            rope(q_tok[:, :, :, NOPE:NOPE + HALF], q_tok[:, :, :, NOPE + HALF:QK], cos_b, sin_b, ta, tb, "rope_done")
            split("g0", 1)
            for j in range(1, 4):
                split(f"g{j}")
            split("om0", 0, 2)
            for i in range(4):
                dve.wait_ge(S("q_turned"), i + 1)
                V.tensor_copy(qT[0:QK, 2 * i:2 * i + 2, :].rearrange("p a b -> p (a b)"), ps[0:QK, 4 + i % 2, :])\
                    .then_inc(S("qT_out"), 1)

            def logits_in(a):
                dve.wait_ge(S("att_logits"), a + 1)
                b = a % 3
                if a == 0:
                    dve.wait_ge(S("k_turned"), 4)
                if 3 <= a < 2 * HEADS + 3:
                    dve.wait_ge(S("att_turned"), min(a - 2, 2 * HEADS))
                if a >= 2 * HEADS + 3:
                    dve.wait_ge(S("diff_turned"), (a - 3 - 2 * HEADS) // 2 + 1)
                bank = a % 4 if a < 2 * HEADS else (a - 2 * HEADS) % 4
                src = ps[:, bank, 0:3 * P]
                if a < HEADS:
                    for tt, (c0, n) in enumerate(((0, P), (P, 2 * P))):
                        ins = V.scalar_tensor_tensor(out=prob[:, b, c0:c0 + n], in0=src[:, c0:c0 + n],
                                                     scalar=f_tok[:, tt, a:a + 1], in1=mask[:, c0:c0 + n],
                                                     op0=ALU.add, op1=ALU.add)
                elif a < 2 * HEADS:
                    ins = V.scalar_tensor_tensor(out=prob[:, b, :], in0=src, scalar=MLA_SCALE, in1=mask[:],
                                                 op0=ALU.mult, op1=ALU.add)
                else:
                    ins = V.tensor_tensor(prob[:, b, :], src, mask[:], ALU.add)
                ins.then_inc(S("att_in"), 1)
                dve.wait_ge(S("att_in"), a + 1)
                V.tensor_reduce(nmax[:, b, 0:1], prob[:, b, 0:P], AX_X, ALU.max, negate=True)
                V.tensor_reduce(nmax[:, b, 1:2], prob[:, b, P:3 * P], AX_X, ALU.max, negate=True).then_inc(S("att_max"), 1)

            def norm_p(a):
                b = a % 3
                dve.wait_ge(S("att_exp"), 2 * a + 2)
                link(V.reciprocal(rinv[:, b, :], rsum[:, b, :]))
                V.tensor_scalar(prob[:, b, 0:P], prob[:, b, 0:P], rinv[:, b, 0:1], None, ALU.mult)
                V.tensor_scalar(prob[:, b, P:3 * P], prob[:, b, P:3 * P], rinv[:, b, 1:2], None, ALU.mult)\
                    .then_inc(S("att_p"), 1)

            def o_low(j):
                dve.wait_ge(S("o_high"), j + 1)
                V.tensor_tensor(hL[:, (j + 4) % 8, :], ps[:, 6 + j % 2, 0:SEQ], hH[:, (j + 4) % 8, :].bitcast(F32),
                                ALU.subtract).then_inc(S("o_low"), 1)

            N1 = 2 * HEADS
            logits_in(0)
            for a in range(N1):
                if a + 1 < N1:
                    logits_in(a + 1)
                norm_p(a)
                if a >= 3 and a % 2 == 1:
                    o_low((a - 3) // 2)
            o_low(HEADS - 1)
            split("om1")

            def o_proj(name, i):
                done(f"{name}{i}")
                for j in range(2):
                    m = 4 * i + 2 * j
                    src = ps[:, IT[f"{name}{i}"]["acc"] + j, :].rearrange("p (a b) -> p a b", a=2)
                    if name == "om":
                        V.tensor_tensor(yF[:, m:m + 2, :], sig[:, m:m + 2, :], src, ALU.mult).then_inc(S("om_out"), 1)
                    else:
                        link(V.tensor_tensor(sig[:, 8 + m:10 + m, :], sig[:, 8 + m:10 + m, :], src, ALU.mult))
                        V.tensor_tensor(yF[:, m:m + 2, :], yF[:, m:m + 2, :], sig[:, 8 + m:10 + m, :], ALU.add)\
                            .then_inc(S("y_ready"), 1)

            split("of0")
            o_proj("om", 0)
            split("of1")
            o_proj("om", 1)
            dve.wait_ge(S("om_out"), 4)
            o_proj("of", 0)
            o_proj("of", 1)
            dve.wait_ge(S("y_high"), KD)
            V.tensor_tensor(aL[:, 0:KD, :], yF, aH[:, 0:KD, :].bitcast(F32), ALU.subtract).then_inc(S("y_low"), 1)
            V.memset(ada_row, 0.0).then_inc(S("ada_zero"), 1)
            dve.wait_ge(S("ada_zero"), 1)
            ada_out(1)
            V.tensor_copy(lam[:, 4:5], adaT[:, 0:1]).then_inc(S("ada_cols"), 1)
            split("wo0")
            split("wo1")

            def residual(m, src, scale, sem):
                V.scalar_tensor_tensor(out=xT[:, m, :], in0=src, scalar=scale, in1=xT[:, m, :], op0=ALU.mult, op1=ALU.add)\
                    .then_inc(S(sem), 1)

            for i in range(2):
                done(f"wo{i}")
                for j in range(4):
                    residual(4 * i + j, ps[:, IT[f"wo{i}"]["acc"] + j // 2, 256 * (j % 2):256 * (j % 2) + 256],
                             adaT[:, G_M + 4 * i + j:G_M + 4 * i + j + 1], "xT_ready")
            dve.wait_ge(S("xT_ready"), XT_READY[1])
            ada_out(2)
            V.scalar_tensor_tensor(out=scale_f[:], in0=adaT[:, SC_F:SC_F + KD], scalar=1.0,
                                   in1=colT[:, ROW["ffn_g"]:ROW["ffn_g"] + KD], op0=ALU.add, op1=ALU.mult)\
                .then_inc(S("ada_cols"), 1)
            norm_a(1)
            split("up0", 0, 2)
            dve.wait_ge(S("ada_cols"), 3)
            link(norm_b(1, scale_f, adaT[:, SH_F:SH_F + KD], n_sq))
            norm_low(1)

            def conv_rest(j):
                dve.wait_ge(S("conv_1"), 4 * j + 4)
                for tap, row in ((1, "conv_w1"), (2, "conv_w0")):
                    for m in range(4):
                        tile = 2 * j + m if m < 2 else FT + 2 * j + m - 2
                        src = ps[:, IT[f"up{j}"]["acc"] + m // 2, 256 * (m % 2):256 * (m % 2) + 256 - tap]
                        v = conv[:, j % 2, m, tap:SEQ]
                        ins = V.scalar_tensor_tensor(out=v, in0=src, scalar=colT[:, ROW[row] + tile:ROW[row] + tile + 1], in1=v,
                                                     op0=ALU.mult, op1=ALU.add)
                    if tap == 1:
                        link(ins)
                ins.then_inc(S("conv_2"), 1)

            def act_mul(j):
                dve.wait_ge(S("silu"), j + 1)
                if j >= 2:
                    dve.wait_ge(S("ff_low"), j - 1)
                V.tensor_tensor(actF[:, j % 2], conv[:, j % 2, 0:2, :], conv[:, j % 2, 2:4, :], ALU.mult).then_inc(S("act_f"), 1)

            def ff_low(j):
                dve.wait_ge(S("ff_high"), j + 1)
                k = 2 * j if j < UP_A else 2 * (j - UP_A)
                V.tensor_tensor(aL[:, k:k + 2, :], actF[:, j % 2], aH[:, k:k + 2, :].bitcast(F32), ALU.subtract)\
                    .then_inc(S("ff_low"), 1)

            def after_up(j, name):
                n = len(IT[name]["chunks"])
                split(name, 0, min(2, n))
                conv_rest(j)
                split(name, 2, min(3, n))
                act_mul(j)
                split(name, 3, n)
                ff_low(j)

            split("up0", 2)
            for j in range(1, UP_A):
                after_up(j - 1, f"up{j}")
            after_up(UP_A - 1, "dn0")
            split("dn1")
            split("dn2")
            split(f"up{UP_A}")
            for j in range(UP_A + 1, 11):
                after_up(j - 1, f"up{j}")
            after_up(10, "dn3")
            split("dn4")
            split("dn5")
            done("dn5")
            for m in range(KD):
                residual(m, ps[:, 4 + m // 2, 256 * (m % 2):256 * (m % 2) + 256], adaT[:, G_F + m:G_F + m + 1], "xT_ready")
            norm_a(2)
            dve.wait_ge(S("norm_xn"), 3)
            for k in range(KD):
                V.tensor_scalar(xT[:, k, :], n_xn[:, k, :], colT[:, ROW["fin_g"] + k:ROW["fin_g"] + k + 1], None, ALU.mult)\
                    .then_inc(S("xT_ready"), 1)
            dve.wait_ge(S("xT_ready"), XT_READY[3])
            norm_a(3)
            split("q2", 0, 2)
            link(norm_b(3, colT[:, ROW["attn_g2"]:ROW["attn_g2"] + KD], None, n_sq))
            norm_low(3)
            V.tensor_scalar(qg8[:], colT[:, ROW["qg2"]:ROW["qg2"] + 1], HEAD2 ** -0.5, None, ALU.mult)
            V.tensor_scalar(sub8[:], colT[:, ROW["subln"]:ROW["subln"] + 1], 1.0 - LAM_INIT, None, ALU.mult)
            lr = colT[:, ROW["lam"]:ROW["lam"] + 4].rearrange("p (a b) -> p a b", b=2)
            V.tensor_tensor(lam[:, 0:2], lr[:, :, 0], lr[:, :, 1], ALU.mult).then_inc(S("lam_prod"), 1)
            split("q2", 2)
            split("k2", 0, 2)

            def tok_out(name, dst):
                done(name)
                for tt in range(TT):
                    V.tensor_copy(dst[:, tt, :], ps[:, IT[name]["acc"] + tt, :]).then_inc(S(f"{name}_out"), 1)

            def tok_sum(name, width, n):
                dve.wait_ge(S(f"{name}_sq"), 1)
                link(V.tensor_reduce(ms[:, 0:n], sq2.rearrange("p t (h n) -> p (t h) n", n=width), AX_X, ALU.add))
                mean_sq(ms[:, 0:n], ms[:, 0:n], width, f"{name}_ms")

            def tok_norm(name, src, dst, width, n, sem):
                dve.wait_ge(S(f"{name}_rstd"), 1)
                V.tensor_tensor(dst.rearrange("p t (h n) -> p (t h) n", n=width), src.rearrange("p t (h n) -> p (t h) n", n=width),
                                rstd[:, 0:n].unsqueeze(2).to_broadcast([P, n, width]), ALU.mult).then_inc(S(sem), 1)

            tok_out("q2", q2)
            split("k2", 2)
            tok_sum("q2", HEAD2, 16)
            split("v2", 0, 2)
            tok_out("k2", k2)
            tok_norm("q2", q2, qn, HEAD2, 16, "qn")
            tok_sum("k2", HEAD2, 16)
            split("v2", 2)
            split("xc", 0, 2)
            tok_norm("k2", k2, kn, HEAD2, 16, "kn")
            split("xc", 2)
            split("bg")
            split("cg")
            done("cg")
            dve.wait_ge(S("xc_out"), 2)
            for i in range(2):
                V.tensor_tensor(cz[:, 2 * i:2 * i + 2, :], ps[:, IT["cg"]["acc"] + i, :].rearrange("p (a b) -> p a b", a=2),
                                cz[:, 2 * i:2 * i + 2, :], ALU.mult).then_inc(S("cg_out"), 1)
            dve.wait_ge(S("lam_exp"), 1)
            link(V.tensor_tensor(lam[:, 5:6], lam[:, 2:3], lam[:, 3:4], ALU.subtract))
            link(V.tensor_scalar(lam[:, 5:6], lam[:, 5:6], LAM_INIT, None, ALU.add))
            for i in range(2):
                dve.wait_ge(S("q2_turned"), i + 1)
                V.tensor_scalar(qT2[:, 2 * i:2 * i + 2, :].rearrange("p a b -> p (a b)"), ps[:, 4 + i, :], qg8[:, 0:1], None,
                                ALU.mult).then_inc(S("qT2_out"), 1)

            def diff_p(h):
                a0, a1 = N1 + 2 * h, N1 + 2 * h + 1
                b0, b1 = a0 % 3, a1 % 3
                dve.wait_ge(S("att_exp"), 2 * a1 + 2)
                V.reciprocal(rinv[:, b0, :], rsum[:, b0, :])
                link(V.reciprocal(rinv[:, b1, :], rsum[:, b1, :]))
                link(V.tensor_scalar(rinv[:, b1, :], rinv[:, b1, :], lam[:, 5:6], None, ALU.mult))
                halves = ((0, P), (P, 2 * P))
                for tt, (c0, n) in enumerate(halves):
                    v = prob[:, b1, c0:c0 + n]
                    ins = V.tensor_scalar(v, v, rinv[:, b1, tt:tt + 1], None, ALU.mult)
                link(ins)
                for tt, (c0, n) in enumerate(halves):
                    v = prob[:, b0, c0:c0 + n]
                    ins = V.scalar_tensor_tensor(out=v, in0=v, scalar=rinv[:, b0, tt:tt + 1], in1=prob[:, b1, c0:c0 + n],
                                                 op0=ALU.mult, op1=ALU.subtract)
                ins.then_inc(S("diff_p"), 1)

            def o2_out(h):
                dve.wait_ge(S("diff_pv"), h + 1)
                V.tensor_copy(o2[:, :, h * V2:h * V2 + V2], ps[:, 6 + h % 2, 0:SEQ].rearrange("p (t n) -> p t n", t=TT))\
                    .then_inc(S("o2_out"), 1)

            dve.wait_ge(S("k2_turned"), 2)
            logits_in(N1)
            logits_in(N1 + 1)
            for h in range(N_HEADS2):
                if h + 1 < N_HEADS2:
                    logits_in(N1 + 2 * h + 2)
                diff_p(h)
                if h + 1 < N_HEADS2:
                    dve.wait_ge(S("diff_p"), h + 1)
                    logits_in(N1 + 2 * h + 3)
                if h >= 1:
                    o2_out(h - 1)
            dve.wait_ge(S("cg_out"), 2)
            w2c = ROW["conv_w2"]
            for m in range(4):
                ins = V.tensor_scalar(cy[:, m, :], cz[:, m, :], colT[:, w2c + 8 + m:w2c + 9 + m], None, ALU.mult)
            link(ins)
            for tap in (1, 2):
                for m in range(4):
                    v = cy[:, m, tap:SEQ]
                    col = w2c + 4 * (2 - tap) + m
                    ins = V.scalar_tensor_tensor(out=v, in0=cz[:, m, 0:SEQ - tap], scalar=colT[:, col:col + 1], in1=v,
                                                 op0=ALU.mult, op1=ALU.add)
                link(ins)
            dve.wait_ge(S("bg_out"), 2)
            V.tensor_tensor(cy, cy, cb, ALU.mult).then_inc(S("cy_ready"), 1)
            o2_out(N_HEADS2 - 1)
            dve.wait_ge(S("cv_sum"), 1)
            mean_sq(ms[:, 0:16], ps[:, 0, 0:16], D_CONV // 8, "cv_ms")
            dve.wait_ge(S("cv_bc"), 1)
            for m in range(4):
                V.scalar_tensor_tensor(out=mixF[:, m, :], in0=cy[:, m, :],
                                       scalar=colT[:, ROW["conv_out_g2"] + m:ROW["conv_out_g2"] + m + 1],
                                       in1=ps[:, 2 + m // 2, 256 * (m % 2):256 * (m % 2) + 256],
                                       op0=ALU.mult, op1=ALU.mult).then_inc(S("mixF"), 1)
            tok_sum("sub", V2, 8)
            tok_norm("sub", o2, o2, V2, 8, "sub_n")
            dve.wait_ge(S("mix_high"), 1)
            V.tensor_tensor(aL[:, 0:4, :], mixF, aH[:, 0:4, :].bitcast(F32), ALU.subtract)
            dve.wait_ge(S("mix_high"), 3)
            for i in range(2):
                ins = V.scalar_tensor_tensor(out=aL[:, 4 + 2 * i:6 + 2 * i, :].rearrange("p a b -> p (a b)"), in0=ps[:, 4 + i, :],
                                             scalar=sub8[:, 0:1],
                                             in1=aH[:, 4 + 2 * i:6 + 2 * i, :].rearrange("p a b -> p (a b)").bitcast(F32),
                                             op0=ALU.mult, op1=ALU.subtract)
            ins.then_inc(S("mix_ready"), 1)
            split("w2o0")
            split("w2o1")
            for i in range(2):
                done(f"w2o{i}")
                for j in range(2):
                    m = 4 * i + 2 * j
                    V.tensor_tensor(xT[:, m:m + 2, :], ps[:, IT[f"w2o{i}"]["acc"] + j, :].rearrange("p (a b) -> p a b", a=2),
                                    xT[:, m:m + 2, :], ALU.add).then_inc(S("xT_ready"), 1)
            dve.wait_ge(S("xT_ready"), XT_READY[4])
            norm_a(4)
            norm_b(4, colT[:, ROW["ffn_g2"]:ROW["ffn_g2"] + KD], None, n_sq).then_inc(S("norm_in"), 1)

            dve.wait_ge(S("logits"), 1)
            link(V.tensor_copy(lg, ps[:, 6, 0:P].rearrange("p (t n) -> p t n", t=TT)[:, :, 0:LG]))
            gl = lg[:, :, 0:GROUPS]

            def wide(v, n):
                return v.unsqueeze(2).to_broadcast([P, TT, n])

            def first_max(src, top, tmp, oh, n):
                link(V.tensor_reduce(top, src, AX_X, ALU.max))
                link(V.tensor_tensor(tmp, src, wide(top, n), ALU.is_equal))
                link(V.tensor_tensor(tmp, tmp, desc[:, 0:n].unsqueeze(1).to_broadcast([P, TT, n]), ALU.mult))
                link(V.tensor_reduce(wm, tmp, AX_X, ALU.max))
                link(V.tensor_tensor(oh, tmp, wide(wm, n), ALU.is_equal))

            first_max(gl, gmax, gtmp, goh, GROUPS)
            V.tensor_tensor(gtmp, gl, wide(gmax, GROUPS), ALU.subtract).then_inc(S("g_shift"), 1)
            link(V.tensor_tensor(gprod, lg[:, :, GROUPS:LG].rearrange("p t (g e) -> p t g e", g=GROUPS),
                                 goh.unsqueeze(3).to_broadcast([P, TT, GROUPS, EPG]), ALU.mult))
            link(V.tensor_reduce(lsel, gprod.rearrange("p t g e -> p t e g"), AX_X, ALU.add))
            first_max(lsel, m1, etmp, oh1, EPG)
            link(V.scalar_tensor_tensor(out=l2, in0=oh1, scalar=NEG, in1=lsel, op0=ALU.mult, op1=ALU.add))
            first_max(l2, m2, etmp, oh2, EPG)
            V.tensor_tensor(ed, m2, m1, ALU.subtract).then_inc(S("e_shift"), 1)
            link(V.tensor_tensor(etmp, oh1, oh2, ALU.add))
            gw = goh.unsqueeze(3).to_broadcast([P, TT, GROUPS, EPG])
            V.tensor_tensor(sel, etmp.unsqueeze(2).to_broadcast([P, TT, GROUPS, EPG]), gw, ALU.mult).then_inc(S("sel"), 1)
            dve.wait_ge(S("g_exp"), 1)
            link(V.tensor_reduce(gsum, gexp, AX_X, ALU.add))
            link(V.reciprocal(ggate, gsum))
            for i in range(4):
                dve.wait_ge(S("hn_high"), i + 1)
                V.tensor_tensor(hnL[:, i // 2, 512 * (i % 2):512 * (i % 2) + 512], ps[:, 4 + i % 2, :],
                                hnH[:, i // 2, 512 * (i % 2):512 * (i % 2) + 512].bitcast(F32), ALU.subtract)\
                    .then_inc(S("hn_low"), 1)
            for i in range(4):
                dve.wait_ge(S("res_turned"), i + 1)
                V.tensor_copy(y_acc[:, i // 2, 512 * (i % 2):512 * (i % 2) + 512], ps[:, i, :]).then_inc(S("y_sum"), 1)
            dve.wait_ge(S("e_exp"), 1)
            link(V.tensor_scalar(w1, ed, 1.0, None, ALU.add))
            link(V.reciprocal(w1, w1))
            link(V.tensor_tensor(w2, ed, w1, ALU.mult))
            link(V.tensor_tensor(oh1, oh1, wide(w1, EPG), ALU.mult))
            link(V.tensor_tensor(oh2, oh2, wide(w2, EPG), ALU.mult))
            link(V.tensor_tensor(oh1, oh1, oh2, ALU.add))
            link(V.tensor_tensor(oh1, oh1, wide(ggate, EPG), ALU.mult))
            V.memset(comb[:], 0.0)
            link(V.memset(posm[:], -1.0))
            for tt in range(TT):
                V.tensor_tensor(comb[:, tt, 0:EXPERTS].rearrange("p (g e) -> p g e", g=GROUPS),
                                oh1[:, tt].unsqueeze(1).to_broadcast([P, GROUPS, EPG]),
                                goh[:, tt].unsqueeze(2).to_broadcast([P, GROUPS, EPG]), ALU.mult)
            dve.wait_ge(S("places"), 1)
            for tt in range(TT):
                ins = V.tensor_tensor(posm[:, tt, 0:EXPERTS], ps[:, 7, 32 * tt:32 * tt + 32],
                                      sel[:, tt].rearrange("p g e -> p (g e)"), ALU.mult)
            link(ins)
            link(V.tensor_scalar(posm[:, :, 0:EXPERTS], posm[:, :, 0:EXPERTS], -1.0, None, ALU.add))
            link(V.tensor_reduce(npass_f[0:1, 0:1], ps[0:1, 7, 64:96], AX_X, ALU.max))
            link(V.tensor_scalar(npass[0:1, 1:2], npass_f[0:1, 0:1], float(CAP - 1), None, ALU.add))
            V.tensor_scalar(npass[0:1, 0:1], npass[0:1, 1:2], int(math.log2(CAP)), None, ALU.arith_shift_right)\
                .then_inc(S("npass_ready"), 1)
            dve.wait_ge(S("npass_ready"), 1)
            n = dve.value_load(npass[0:1, 0:1], min_val=1, max_val=SEQ // CAP)

            def pick_tokens(e0, turn, passed):
                sel_e = bass.ds(e0, PER_IT)
                for tt in range(TT):
                    V.tensor_tensor(pick[:, tt, :].rearrange("p (e s) -> p e s", e=PER_IT),
                                    slot_no[:].unsqueeze(1).to_broadcast([P, PER_IT, CAP]),
                                    posm[:, tt, sel_e].unsqueeze(2).to_broadcast([P, PER_IT, CAP]), ALU.is_equal)\
                        .then_inc(S("pick_half"), 1)
                dve.wait_ge(S("pick_half"), turn * 2 + 2)
                if passed is not None:
                    dve.wait_ge(S("put_turned"), passed)
                for tt in range(TT):
                    V.tensor_tensor(put[:, tt, :].rearrange("p (e s) -> p e s", e=PER_IT),
                                    pick[:, tt, :].bitcast(F32).rearrange("p (e s) -> p e s", e=PER_IT),
                                    comb[:, tt, sel_e].unsqueeze(2).to_broadcast([P, PER_IT, CAP]), ALU.mult)\
                        .then_inc(S("put_half"), 1)

            pick_tokens(0, 0, None)
            with dve.Fori(0, n) as p:
                with dve.Fori(0, TURNS) as g:
                    turn = p * TURNS + g
                    gidx = p * (TURNS + 1) + g
                    for r in range(2):
                        dve.wait_ge(S("e_silu"), turn * 2 + r + 1)
                        dve.wait_ge(S("expert_used"), turn * 6 + 3 * r + 2)
                        V.tensor_tensor(eact, sg, ps[:, 1, :], ALU.mult).then_inc(S("e_act"), 1)
                        if r == 0:
                            dve.wait_ge(S("gathered"), gidx * 4 + 4)
                            dve.wait_ge(S("put_half"), gidx * 2 + 2)
                            pick_tokens((g + 1) * PER_IT, gidx + 1, turn + 1)
                        for i in range(4):
                            tt, hf = divmod(i, 2)
                            v = y_acc[:, tt, 512 * hf:512 * hf + 512]
                            dve.wait_ge(S("e_put"), turn * 8 + 4 * r + i + 1)
                            dve.wait_ge(S("y_sum"), turn * 8 + 4 * r + i + 1)
                            V.tensor_tensor(v, v, ps[:, 6 + i % 2, :], ALU.add).then_inc(S("y_sum"), 1)
                dve.wait_ge(S("gathered"), p * (4 * (TURNS + 1)) + 4 * (TURNS + 1))
                dve.wait_ge(S("put_half"), p * (2 * (TURNS + 1)) + 2 * (TURNS + 1))
                V.tensor_scalar(slot_no[:], slot_no[:], float(CAP), None, ALU.add).then_inc(S("slot_next"), 1)
                dve.wait_ge(S("slot_next"), p + 1)
                pick_tokens(0, p * (TURNS + 1) + TURNS + 1, p * TURNS + TURNS)


def kernel(**inputs):
    import concourse.bacc as bacc
    from concourse.bass_utils import run_bass_kernel_spmd

    nc = bacc.Bacc("TRN2", target_bir_lowering=False, num_devices=1)
    two_dim = ("w_ada", "w_in", "w_uq", "w_ukv", "w_o_mla", "w_o_fox", "w_out", "w_up", "conv_w", "w_down", "w_in_2",
               "w_out_2", "w_router_group_2", "w_router_expert_2", "x")
    feeds, t = {}, {}
    for name, value in inputs.items():
        a = np.ascontiguousarray(np.asarray(value))
        if name in two_dim:
            a = a.reshape(a.shape[-2:])
        elif name.startswith("w_exp"):
            a = a.reshape((EXPERTS,) + a.shape[-2:])
        elif name == "b_forget":
            a = a.reshape(-1)
        else:
            a = a.reshape(1, -1)
        feeds[name] = a
        t[name] = nc.dram_tensor(name, a.shape, mybir.dt.from_np(a.dtype), kind="ExternalInput").ap()
    out = nc.dram_tensor("out", (SEQ, D), F32, kind="ExternalOutput").ap()
    build(nc, t, out)
    nc.finalize()
    res = run_bass_kernel_spmd(nc, [feeds], core_ids=[0])
    return res.results[0]["out"].reshape(1, SEQ, D)
```

```python
import math
from contextlib import ExitStack

import numpy as np

import concourse.bass as bass
from concourse import mybir

F32 = mybir.dt.float32
F32R = mybir.dt.float32r
I32 = mybir.dt.int32
ALU = mybir.AluOpType
ACT = mybir.ActivationFunctionType
AX_X = mybir.AxisListType.X

P = 128
SEQ = 256
TT = SEQ // P
D = 1024
KD = D // P
EPS = 1e-6
NEG = -1e30

Q_RANK, KV_RANK, ROPE = 384, 256, 32
HEADS = 8
NOPE, VDIM, FOXD = 64, 64, 64
QK = NOPE + ROPE
HALF = ROPE // 2
ATT = HEADS * VDIM
MLA_SCALE = 1.0 / math.sqrt(QK)
FOX_SCALE = 1.0 / math.sqrt(FOXD)
D_FF = 2816
FT = D_FF // P
CONV_W = 3

D_CONV = 512
N_HEADS2, HEAD2, V2 = 4, 64, 128
LAM_INIT = 0.8 - 0.6 * math.exp(0.0)
GROUPS, EPG, D_EXP = 4, 8, 512
EXPERTS = GROUPS * EPG
CAP = 64
PER_IT = 4
TURNS = EXPERTS // PER_IT
LG = GROUPS + EXPERTS

SLOT = 8 * 520
RING1 = 3
CHUNK = 2 * 520
CHUNKS = 4

ROW = {}
_at = 0
for _name, _n in (("b_ada", 48), ("mix_g", 8), ("q_g", 3), ("kv_g", 2), ("ffn_g", 8), ("fin_g", 8),
                  ("attn_g2", 8), ("conv_w2", 12), ("conv_out_g2", 4), ("subln", 1), ("ffn_g2", 8),
                  ("qg2", 1), ("kg2", 1), ("lam", 4)):
    ROW[_name] = _at
    _at += _n
assert _at <= P
ROW["conv_w0"], ROW["conv_w1"], ROW["conv_w2_ff"], ROW["conv_b"] = P, P + 2 * FT, 2 * P, 2 * P + 2 * FT
ROWS_TOTAL = 16 * (12 + 3 + 4 + 4)
XT_BASE = {0: 0, 1: 4, 2: 4 + KD, 4: 4 + 3 * KD}
SQ_BASE = {0: 0, 1: KD, 2: 2 * KD}
IN_BASE = {0: 0, 1: KD, 3: 2 * KD}
SH_M, SC_M, G_M, SH_F, SC_F, G_F = (i * KD for i in range(6))


def two_pi_parts():
    parts, rest = [], 2 * math.pi
    for _ in range(3):
        e = math.floor(math.log2(rest))
        q = 2.0 ** (e - 7)
        parts.append(math.floor(rest / q) * q)
        rest -= parts[-1]
    return parts + [float(np.float32(rest))]


def build(nc, t, out):
    ctx = ExitStack()
    sems = {}

    def S(name):
        if name not in sems:
            sems[name] = ctx.enter_context(nc.semaphore(name))
        return sems[name]

    def sb(name, shape, dt=F32):
        return ctx.enter_context(nc.sbuf_tensor(name, shape, dt))

    with ctx:
        ps = ctx.enter_context(nc.psum_tensor("ps", [P, 8, 512], F32))
        ring = sb("ring", [P, RING1, SLOT])
        work = sb("work", [P, 2 * SLOT])
        with nc.sbuf_tensor("wl", [P, CHUNKS, CHUNK], F32R) as wl:
            pass
        slot6 = sb("slot6", [P, SLOT])
        with nc.sbuf_tensor("wh", [P, CHUNKS, CHUNK], F32R) as wh:
            pass
        slot3 = sb("slot3", [P, SLOT])
        with nc.sbuf_tensor("hL", [P, KD, SEQ], F32R) as hL:
            pass
        slot7a = sb("slot7a", [P, KD * SEQ])
        hH = sb("hH", [P, KD, SEQ], F32R)
        aH = sb("aH", [P, 12, SEQ], F32R)
        aL = sb("aL", [P, 12, SEQ], F32R)
        xT = sb("xT", [P, KD, SEQ])
        wa = sb("wa", [P, 3072])
        wb = sb("wb", [P, 4096])
        wc = sb("wc", [P, 1920])
        colT = sb("colT", [P, 3 * P])
        adaT = sb("adaT", [P, 6 * KD])
        cact = sb("cact", [P, KD])
        c_rows = sb("c_rows", [KD, P])
        scale_m = sb("scale_m", [P, KD])
        scale_f = sb("scale_f", [P, KD])
        scale_2 = sb("scale_2", [P, KD])
        gain_sq = sb("gain_sq", [P, KD, 2])
        r12 = sb("r12", [P, TT])
        ssq_o = sb("ssq_o", [P, N_HEADS2, TT])
        ident = sb("ident", [P, P])
        tri_ones = sb("tri_ones", [P, 2 * P])
        tri, ones = tri_ones[:, 0:P], tri_ones[:, P:2 * P]
        mask = sb("mask", [P, 3 * P])
        minus_half = sb("minus_half", [P, 16])
        invf = sb("invf", [P, HALF])
        half_ind = sb("half_ind", [P, 2])
        pos_i = sb("pos_i", [P, TT], I32)
        pos_f = sb("pos_f", [P, TT])
        trig = sb("trig", [P, 5, TT, HALF])
        bf_b = sb("bf_b", [P, HEADS])
        ms = sb("ms", [P, 16])
        rstd = sb("rstd", [P, 16])
        ssq = sb("ssq", [P, 4])
        nmax = sb("nmax", [P, 4, 2])
        rsum = sb("rsum", [P, 4, 2])
        rinv = sb("rinv", [P, 4, 2])
        fz = sb("fz", [P, 3, TT, HEADS])
        f_tok = sb("f_tok", [P, TT, HEADS])
        nFT = sb("nFT", [HEADS, SEQ])
        qg8 = sb("qg8", [P, 1])
        sub8 = sb("sub8", [P, 1])
        lam = sb("lam", [P, 6])

        flatE = work[:]

        slot7b = wb[:, 0:2048]

        def slot(i):
            if i < RING1:
                return ring[:, i, :]
            return {3: slot3[:], 4: work[:, 0:SLOT], 5: work[:, SLOT:2 * SLOT], 6: slot6[:]}[i]

        rows = wc[:, 0:3 * P].rearrange("p (i n) -> p i n", i=3)
        ada_rows = (wc[:, 3 * P:3 * P + 512], flatE[:, 0:512], wc[:, 3 * P:3 * P + 512])
        x_tok = wa[:, 0:TT * D].rearrange("p (t d) -> p t d", t=TT)
        n_sq = wb[:, 0:KD * SEQ].rearrange("p (k n) -> p k n", k=KD)
        n_t = wb[:, KD * SEQ:2 * KD * SEQ].rearrange("p (k n) -> p k n", k=KD)
        n_row = wc[:, 1152:1152 + SEQ]
        CKQ = Q_RANK + KV_RANK + ROPE
        cqkv = wc[:, 0:TT * CKQ].rearrange("p (t n) -> p t n", t=TT)
        fqT = wa[:, 0:1024].rearrange("p (m n) -> p m n", m=4)
        fkT = wa[:, 1024:2048].rearrange("p (m n) -> p m n", m=4)
        fv_tok = wa[:, 2048:3072].rearrange("p (t n) -> p t n", t=TT)
        q_tok = wb[:, 0:1536].rearrange("p (t h n) -> p t h n", t=TT, h=HEADS)
        k_tok = wb[:, 1536:3072].rearrange("p (t h n) -> p t h n", t=TT, h=HEADS)
        v_tok = wb[:, 3072:4096].rearrange("p (t n) -> p t n", t=TT)
        rope_tmp = wc[:, 1408:1920].rearrange("p (i n) -> p i n", i=2)
        sig = flatE[:, 0:4096].rearrange("p (m n) -> p m n", m=16)
        qT = flatE[:, 4096:6144].rearrange("p (h n) -> p h n", h=HEADS)
        kT = flatE[:, 6144:8192].rearrange("p (h n) -> p h n", h=HEADS)
        prob = wc[:, 0:1152].rearrange("p (b n) -> p b n", b=3)
        pT = wc[:, 1152:1920].rearrange("p (b n) -> p b n", b=2)

        def prob_of(a):
            if a < 2 * HEADS:
                return prob[:, a % 3, :]
            i = (a - 2 * HEADS) % 4
            return prob[:, i, :] if i < 3 else wa[:, 1024:1024 + 3 * P]

        yF = wb[:, 0:2048].rearrange("p (m n) -> p m n", m=KD)
        conv = flatE[:, 0:2048].rearrange("p (b m n) -> p b m n", b=2, m=4)
        actF = flatE[:, 2048:3072].rearrange("p (b m n) -> p b m n", b=2, m=2)
        q2 = wa[:, 0:1024].rearrange("p (t n) -> p t n", t=TT)
        k2 = wa[:, 1024:2048].rearrange("p (t n) -> p t n", t=TT)
        v2 = wa[:, 2048:3072].rearrange("p (t n) -> p t n", t=TT)
        o2 = wa[:, 0:1024].rearrange("p (t n) -> p t n", t=TT)
        qT2 = wb[:, 0:1024].rearrange("p (m n) -> p m n", m=4)
        kT2 = wb[:, 1024:2048].rearrange("p (m n) -> p m n", m=4)
        cz = wb[:, 2048:3072].rearrange("p (m n) -> p m n", m=4)
        cy = wb[:, 3072:4096].rearrange("p (m n) -> p m n", m=4)
        csq = wb[:, 2048:3072].rearrange("p (m n) -> p m n", m=4)
        sq2 = flatE[:, 2048:3072].rearrange("p (t n) -> p t n", t=TT)
        qn = flatE[:, 3072:4096].rearrange("p (t n) -> p t n", t=TT)
        kn = flatE[:, 4096:5120].rearrange("p (t n) -> p t n", t=TT)
        squares_junk = wa[:, 1408:1408 + SEQ].rearrange("p (t n) -> p t n", t=TT)
        wr = sb("wr", [P, KD, LG])
        lg = wa[:, 2048:2048 + TT * LG].rearrange("p (t n) -> p t n", t=TT)
        _r = [2048 + TT * LG]

        def rt(*shape):
            n = int(np.prod(shape))
            v = wa[:, _r[0]:_r[0] + n]
            _r[0] += n
            if len(shape) == 2:
                v = v.rearrange("p (a b) -> p a b", a=shape[0])
            if len(shape) == 3:
                v = v.rearrange("p (a b c) -> p a b c", a=shape[0], b=shape[1])
            return v

        gmax, gsum, ggate = rt(TT), rt(TT), rt(TT)
        gexp, goh, gtmp = rt(TT, GROUPS), rt(TT, GROUPS), rt(TT, GROUPS)
        gprod = rt(TT, GROUPS, EPG)
        lsel, oh1, oh2, etmp, l2 = (rt(TT, EPG) for _ in range(5))
        m1, m2, wm, ed, w1, w2 = (rt(TT) for _ in range(6))
        sel = rt(TT, GROUPS, EPG)
        comb = sb("comb", [P, TT, EXPERTS + PER_IT])
        posm = sb("posm", [P, TT, EXPERTS + PER_IT])
        desc = sb("desc", [P, EPG])
        slot_no = sb("slot_no", [P, CAP])
        npass_f = sb("npass_f", [1, 2])
        npass = sb("npass", [1, 2], I32)
        hnH = aH[:, 0:8, :].rearrange("p a b -> p (a b)").rearrange("p (t d) -> p t d", t=TT)
        hnL = aL[:, 0:8, :].rearrange("p a b -> p (a b)").rearrange("p (t d) -> p t d", t=TT)
        pick = hH[:, 0:2, :]
        xg = xT
        sg = wc[:, 0:512]
        eact = wc[:, 512:1024]
        eactT = wc[:, 1024:1536].rearrange("p (k n) -> p k n", k=4)
        eout = wa[:, 0:1024]
        put = wa[:, 1024:1536].rearrange("p (t n) -> p t n", t=TT)
        putT = wa[:, 1536:2048].rearrange("p (r n) -> p r n", r=2)
        y_acc = wb[:, 2048:4096].rearrange("p (t d) -> p t d", t=TT)

        W = {k: t[k] for k in t}

        def rows_of(w, c0, n, k0=0, kn=None):
            v = w.rearrange("(k p) n -> p k n", p=P)
            return v[:, k0:(kn or v.shape[1] - k0) + k0, c0:c0 + n]

        items = []

        def item(name, kn, n, srcs, per_chunk, acc=None):
            chunks = [(k, min(per_chunk, kn - k)) for k in range(0, kn, per_chunk)] if per_chunk else []
            items.append({"name": name, "kn": kn, "n": n, "srcs": srcs, "chunks": chunks, "acc": acc})

        def ada_item(third, i):
            item(f"ada{third}{i}", 2, 2048, [(0, 2048, rows_of(W["w_ada"], 2048 * third, 2048, 2 * i, 2))], 0)

        o = np.cumsum([0, Q_RANK, KV_RANK + ROPE, 512, 512, 520, 512, 512, 512, 512]).tolist()
        win = {nm: (o[i], o[i + 1] - o[i]) for i, nm in enumerate(["cq", "ckv", "fq", "fk", "fv", "g0", "g1", "g2", "g3"])}

        def in_item(nm, acc):
            c0, n = win[nm]
            item(nm, KD, n, [(0, n, rows_of(W["w_in"], c0, n))], 2, acc)

        def half_item(nm, i, w, kn, n, acc):
            item(f"{nm}{i}", kn, n, [(0, n, rows_of(W[w], n * i, n))], 2, acc)

        for i in range(2):
            ada_item(0, i)
        in_item("cq", 0)
        for i in range(2, 4):
            ada_item(0, i)
        in_item("ckv", 2)
        in_item("fq", 0)
        ada_item(1, 0)
        in_item("fk", 2)
        ada_item(1, 1)
        in_item("fv", 0)
        ada_item(1, 2)
        half_item("uq", 0, "w_uq", 3, 384, 2)
        half_item("uq", 1, "w_uq", 3, 384, 0)
        half_item("ukv", 0, "w_ukv", 2, 512, 2)
        ada_item(1, 3)
        half_item("ukv", 1, "w_ukv", 2, 512, 0)
        for i, acc in enumerate((2, 0, 0, 0)):
            in_item(f"g{i}", acc)
            ada_item(2, i)
        for nm, w in (("om", "w_o_mla"), ("of", "w_o_fox")):
            for j in range(2):
                half_item(nm, j, w, 4, 512, 2 - 2 * j)
        for j in range(2):
            half_item("wo", j, "w_out", KD, 512, 2 - 2 * j)

        def up_item(j):
            item(f"up{j}", KD, 512, [(0, 256, rows_of(W["w_up"], 256 * j, 256)),
                                     (256, 256, rows_of(W["w_up"], D_FF + 256 * j, 256))], 2, 2 - 2 * (j % 2))

        def wide_item(nm, w, k0, kn):
            item(nm, kn, D, [(0, D, rows_of(W[w], 0, D, k0, kn))], 1)

        UP_A = 6
        for j in range(UP_A):
            up_item(j)
        for j in range(3):
            wide_item(f"dn{j}", "w_down", 4 * j, 4)
        for j in range(UP_A, 11):
            up_item(j)
        for j in range(3, 6):
            wide_item(f"dn{j}", "w_down", 4 * j, min(4, FT - 4 * j))
        for nm, c, acc in (("q2", 3, 0), ("k2", 4, 2), ("v2", 5, 0), ("xc", 0, 2), ("cg", 2, 0), ("bg", 1, 0)):
            item(nm, KD, 512, [(0, 512, rows_of(W["w_in_2"], 512 * c, 512))], 2, acc)
        wide_item("w2o_attn", "w_out_2", 4, 4)
        wide_item("w2o_conv", "w_out_2", 0, 4)

        IT = {}
        n_chunk = n_ada = 0
        loaded = [0] * 8
        for i, it in enumerate(items):
            it["slot"] = i % RING1
            loaded[it["slot"]] += 16 * len(it["srcs"])
            it["loaded"] = loaded[it["slot"]]
            it["c0"] = n_chunk
            n_chunk += len(it["chunks"])
            it["c1"] = n_chunk
            n_ada += not it["chunks"]
            it["ada"] = n_ada
            IT[it["name"]] = it
        base_loaded = list(loaded)

        def slot_view(it):
            return slot(it["slot"])[:, 0:it["kn"] * it["n"]].rearrange("p (k n) -> p k n", n=it["n"])

        def raw_chunk(it, ci):
            k0, kn = it["chunks"][ci]
            return slot(it["slot"])[:, k0 * it["n"]:(k0 + kn) * it["n"]], kn * it["n"]

        GATE_STEPS = [a for a in range(2 * HEADS) if a % 4 != 3]

        def split_gate(split, i):
            if i < 12:
                split(f"g{1 + i // 4}", i % 4, i % 4 + 1)
            else:
                split(f"om{(i - 12) // 2}", i % 2, i % 2 + 1)

        w_gate = W["w_exp_gate_2"].rearrange("e (k p) n -> e p k n", p=P)
        w_upx = W["w_exp_up_2"].rearrange("e (k p) n -> e p k n", p=P)
        w_downx = W["w_exp_down_2"].rearrange("e (k p) n -> e p k n", p=P)
        out_v = out.rearrange("(t p) d -> p t d", p=P)

        block = ctx.enter_context(nc.Block())

        @block.sync
        def _(sp):
            def load_rows():
                n_rows = 0
                sp.wait_ge(S("row_steps"), 1)

                def row_dma(r, src, c0=0, n=P):
                    i, p0 = divmod(r, P)
                    k = src.shape[0]
                    sp.dma_start(rows[p0:p0 + k, i, c0:c0 + n], src).then_inc(S("rows_loaded"), 16)
                    return 16

                def as_rows(a):
                    return a.rearrange("o (r n) -> (o r) n", n=P)

                for key, name in (("b_ada", "b_ada"), ("norm_mix_g", "mix_g"), ("q_norm_g", "q_g"),
                                  ("kv_norm_g", "kv_g"), ("norm_ffn_g", "ffn_g"), ("norm_final_g", "fin_g"),
                                  ("attn_norm_g_2", "attn_g2"), ("conv_w_2", "conv_w2"), ("conv_out_g_2", "conv_out_g2"),
                                  ("attn_subln_g_2", "subln"), ("ffn_norm_g_2", "ffn_g2"), ("conv_b", "conv_b")):
                    n_rows += row_dma(ROW[name], as_rows(t[key]))
                for j, name in enumerate(("conv_w0", "conv_w1", "conv_w2_ff")):
                    n_rows += row_dma(ROW[name], as_rows(t["conv_w"][j:j + 1, :]))
                for key, name in (("q_norm_g_2", "qg2"), ("k_norm_g_2", "kg2")):
                    for h in range(2):
                        n_rows += row_dma(ROW[name], t[key], 64 * h, 64)
                for j, key in enumerate(("lambda_q1_2", "lambda_k1_2", "lambda_q2_2", "lambda_k2_2")):
                    n_rows += row_dma(ROW["lam"] + j, t[key], 0, 64)
                assert n_rows == ROWS_TOTAL

            for i, it in enumerate(items):
                if i == RING1:
                    load_rows()
                if i >= RING1:
                    before = items[i - RING1]
                    if before["chunks"]:
                        sp.wait_ge(S("chunk_low"), before["c1"])
                    else:
                        sp.wait_ge(S("ada_used"), before["ada"])
                for c0, n, src in it["srcs"]:
                    sp.dma_start(slot_view(it)[:, :, c0:c0 + n], src).then_inc(S(f"slot{it['slot']}_loaded"), 16)

            def expert(w, e):
                return w[e] if isinstance(e, int) else w[bass.ds(e, 1)].rearrange("e p k n -> (e p) k n")

            def load(i, src, k0, kn, width, name):
                sp.dma_start(slot(i)[:, k0 * width:(k0 + kn) * width].rearrange("p (k n) -> p k n", k=kn), src[:, k0:k0 + kn, :])\
                    .then_inc(S(name), 16)

            def load_half7(dst, e, k0):
                sp.dma_start(dst.rearrange("p (k n) -> p k n", k=4), expert(w_gate, e)[:, k0:k0 + 4, :])\
                    .then_inc(S("slot7_loaded"), 16)

            def load_gate_half(j, e, half):
                load(j, expert(w_gate, e), 4 * half, 4, D_EXP, f"slot{j}_loaded")

            def load_gates(e, odd):
                if not odd:
                    for half in range(2):
                        for j in range(2):
                            load_gate_half(j, e + j, half)
                else:
                    load(6, expert(w_gate, e), 0, KD, D_EXP, "slot6_loaded")
                    load_half7(slot7a[:], e + 1, 0)
                    load_half7(slot7b, e + 1, 4)

            def load_up(j, e):
                for half in range(2):
                    load(2 + j, expert(w_upx, e), 4 * half, 4, D_EXP, f"ups_half{half}")

            def load_ups(e):
                for half in range(2):
                    for j in range(2):
                        load(2 + j, expert(w_upx, e + j), 4 * half, 4, D_EXP, f"ups_half{half}")

            def load_downs(e):
                for half in range(2):
                    cs = slice(512 * half, 512 * half + 512)
                    for j in range(2):
                        to = slot(4 + j)[:, 2048 * half:2048 * half + 2048].rearrange("p (k n) -> p k n", k=4)
                        sp.dma_start(to, expert(w_downx, e + j)[:, :, cs]).then_inc(S(f"downs_half{half}"), 16)

            sp.wait_ge(S("k2_turned"), 2)
            load_downs(0)
            last = {it["slot"]: it for it in items}
            for i in sorted(last, key=lambda i: last[i]["c1"]):
                sp.wait_ge(S("chunk_low"), last[i]["c1"])
                if i < 2:
                    for half in range(2):
                        load_gate_half(i, i, half)
                else:
                    load_up(0, 0)
            sp.wait_ge(S("att_logits"), 2 * HEADS + 2 * N_HEADS2)
            load_half7(slot7b, 3, 4)
            sp.wait_ge(S("chunk_used"), n_chunk)
            load_up(1, 1)
            load(6, expert(w_gate, 2), 0, KD, D_EXP, "slot6_loaded")
            load_half7(slot7a[:], 3, 0)

            def rest_of_pass(used, halves):
                def up_and_down(pair, e):
                    sp.wait_ge(S("expert_used"), pair * 4 + (used - 2))
                    load_ups(e)
                    sp.wait_ge(S("expert_used"), pair * 4 + used)
                    load_downs(e)

                sp.wait_ge(S("gate_half"), halves + 1)
                load_gate_half(0, 4, 0)
                load_gate_half(1, 5, 0)
                sp.wait_ge(S("expert_used"), used + 1)
                load_gate_half(0, 4, 1)
                load_gate_half(1, 5, 1)
                up_and_down(1, 2)
                sp.wait_ge(S("expert_used"), used + 5)
                load_gates(6, 1)
                up_and_down(2, 4)
                with sp.Fori(0, TURNS - 2) as g:
                    e0 = g * PER_IT
                    up_and_down(g * 2 + 3, e0 + 6)
                    load_gates(e0 + 8, 0)
                    up_and_down(g * 2 + 4, e0 + 8)
                    load_gates(e0 + 10, 1)
                up_and_down(EXPERTS // 2 - 1, EXPERTS - 2)

            rest_of_pass(0, 0)
            sp.wait_ge(S("npass_ready"), 1)
            n = sp.value_load(npass[0:1, 0:1], min_val=1, max_val=SEQ // CAP)
            with sp.If(n > 1):
                with sp.Fori(1, n) as p:
                    used = p * (4 * EXPERTS // 2)
                    sp.wait_ge(S("expert_used"), used - 7)
                    load_gates(0, 0)
                    sp.wait_ge(S("expert_used"), used - 2)
                    load_ups(0)
                    sp.wait_ge(S("expert_used"), used)
                    load_downs(0)
                    load_gates(2, 1)
                    rest_of_pass(used, p * (EXPERTS // 2))
            for i in range(4):
                hf, tt = divmod(i, 2)
                sp.wait_ge(S("y_sum"), n * (8 * TURNS) + (i + 1))
                sp.dma_start(out_v[:, tt, 512 * hf:512 * hf + 512], y_acc[:, tt, 512 * hf:512 * hf + 512]).then_inc(S("stored"), 16)
            sp.wait_ge(S("stored"), 64)

        @block.gpsimd
        def _(pool):
            chain = [0]

            def link(ins):
                chain[0] += 1
                ins.then_inc(S("pool_chain"), 1)
                pool.wait_ge(S("pool_chain"), chain[0])

            nc.gpsimd.memset(tri_ones[:, 0:2 * P], 1.0).then_inc(S("pool_chain"), 1)
            nc.gpsimd.memset(mask[:], 0.0).then_inc(S("pool_chain"), 1)
            chain[0] = 2
            link(nc.gpsimd.memset(ident[:], 0.0))
            link(nc.gpsimd.affine_select(out=ident[:], in_=ident[:], compare_op=ALU.not_equal, fill=1.0, base=0,
                                         pattern=[[-1, P]], channel_multiplier=1))
            nc.gpsimd.affine_select(out=tri, in_=tri, compare_op=ALU.is_ge, fill=0.0, base=0,
                                    pattern=[[1, P]], channel_multiplier=-1)
            nc.gpsimd.affine_select(out=mask[:, 0:P], in_=mask[:, 0:P], compare_op=ALU.is_ge, fill=NEG, base=0,
                                    pattern=[[-1, P]], channel_multiplier=1)
            nc.gpsimd.affine_select(out=mask[:, 2 * P:3 * P], in_=mask[:, 2 * P:3 * P], compare_op=ALU.is_ge, fill=NEG,
                                    base=0, pattern=[[-1, P]], channel_multiplier=1)
            nc.gpsimd.memset(minus_half[:], -0.5)
            for i in range(HALF):
                nc.gpsimd.memset(invf[:, i:i + 1], float(np.float32(10000.0) ** np.float32(-2.0 * i / ROPE)))
            for i in range(EPG):
                nc.gpsimd.memset(desc[:, i:i + 1], float(EPG - i))
            nc.gpsimd.iota(slot_no[:], pattern=[[1, CAP]], base=1, channel_multiplier=0,
                           allow_small_or_imprecise_dtypes=True).then_inc(S("consts"), 1)

            def power(name, n, count=1):
                pool.wait_ge(S(f"{name}_ms"), count)
                nc.gpsimd.tensor_tensor(rstd[:, 0:n], ms[:, 0:n], minus_half[:, 0:n], ALU.pow)\
                    .then_inc(S(f"{name}_rstd"), 1)

            power("norm", TT, 1)
            power("lat", 4)
            power("norm", TT, 2)
            power("norm", TT, 3)
            pool.wait_ge(S("norm_ms"), 4)
            nc.gpsimd.tensor_tensor(rstd[:, TT:2 * TT], ms[:, TT:2 * TT], minus_half[:, 0:TT], ALU.pow)\
                .then_inc(S("norm_rstd"), 1)
            power("q2", 16)
            power("k2", 16)
            for h in range(N_HEADS2):
                pool.wait_ge(S("sub_ms"), h + 1)
                nc.gpsimd.tensor_tensor(rstd[:, TT * h:TT * h + TT], ms[:, TT * h:TT * h + TT], minus_half[:, 0:TT], ALU.pow)\
                    .then_inc(S("sub_rstd"), 1)
            power("cv", 16)
            power("norm", TT, 5)

        @block.scalar
        def _(act):
            chain = [0]

            def link(ins):
                chain[0] += 1
                ins.then_inc(S("act_chain"), 1)
                act.wait_ge(S("act_chain"), chain[0])

            def split(name, a=0, b=None):
                it = IT[name]
                for ci in range(a, len(it["chunks"]) if b is None else b):
                    c = it["c0"] + ci
                    if ci == 0:
                        act.wait_ge(S(f"slot{it['slot']}_loaded"), it["loaded"])
                    if c >= CHUNKS:
                        act.wait_ge(S("chunk_used"), c - CHUNKS + 1)
                    src, n = raw_chunk(it, ci)
                    nc.scalar.activation(wh[:, c % CHUNKS, 0:n], src, ACT.Copy).then_inc(S("chunk_high"), 1)

            def done(name):
                act.wait_ge(S("chunk_used"), IT[name]["c1"])

            act.dma_start(c_rows[:], t["c"].rearrange("o (r n) -> (o r) n", n=P)).then_inc(S("c_loaded"), 16)
            act.dma_start(x_tok, t["x"].rearrange("(t p) d -> p t d", p=P)).then_inc(S("x_loaded"), 16)
            with nc.allow_non_contiguous_dma("few small rows"):
                act.dma_start(pos_i[:], t["positions"].rearrange("o (t p) -> p (o t)", p=P)).then_inc(S("misc_loaded"), 16)
                act.dma_start(bf_b[:], t["b_forget"].partition_broadcast(P) if t["b_forget"].ndim == 1 else
                              t["b_forget"][0].partition_broadcast(P)).then_inc(S("misc_loaded"), 16)
                act.dma_start(wr[:, :, 0:GROUPS], t["w_router_group_2"].rearrange("(k p) n -> p k n", p=P))\
                    .then_inc(S("misc_loaded"), 16)
                act.dma_start(wr[:, :, GROUPS:LG], t["w_router_expert_2"].rearrange("(k p) n -> p k n", p=P))\
                    .then_inc(S("misc_loaded"), 16)

            def norm_square(n, k, ready):
                act.wait_ge(S("xT_ready"), ready)
                nc.scalar.activation(n_sq[:, k, :], xT[:, k, :], ACT.Square).then_inc(S("norm_sq"), 1)

            def norm_squares(n):
                for k in range(KD):
                    norm_square(n, k, XT_BASE[n] + (k + 1 if n else k // 2 + 1))

            def norm_high(n, shift, k0=0, k1=KD):
                for k in range(k0, k1):
                    act.wait_ge(S("norm_t"), IN_BASE[n] + k + 1)
                    if shift is None:
                        ins = nc.scalar.activation(hH[:, k, :], n_t[:, k, :], ACT.Copy)
                    else:
                        ins = nc.scalar.activation(hH[:, k, :], n_t[:, k, :], ACT.Identity, bias=shift[:, k:k + 1])
                    ins.then_inc(S("norm_high"), 1)

            act.wait_ge(S("c_steps"), 1)
            nc.scalar.activation(cact[:], ps[:, 6, 0:KD], ACT.Silu).then_inc(S("c_steps"), 1)
            act.wait_ge(S("rope_steps"), 1)
            nc.scalar.activation(trig[:, 3], trig[:, 2], ACT.Sin).then_inc(S("rope_steps"), 1)
            nc.scalar.activation(trig[:, 4], trig[:, 2], ACT.Sin, scale=0.5).then_inc(S("rope_steps"), 1)
            norm_squares(0)
            split("cq")
            norm_high(0, adaT[:, SH_M:SH_M + KD])
            split("ckv")
            split("fq", 0, 2)
            act.wait_ge(S("lat_copied"), 4)
            for j, (c0, n) in enumerate(((0, Q_RANK), (Q_RANK, KV_RANK))):
                for tt in range(TT):
                    nc.scalar.activation(flatE[:, 4096 + 384 * (2 * j + tt):4096 + 384 * (2 * j + tt) + n],
                                         cqkv[:, tt, c0:c0 + n], ACT.Square,
                                         accum_out=ssq[:, 2 * j + tt:2 * j + tt + 1]).then_inc(S("lat_sq"), 1)
            split("fq", 2)
            split("fk", 0, 3)
            done("fq")
            for i in range(2):
                nc.scalar.activation(fqT[:, 2 * i:2 * i + 2, :].rearrange("p a b -> p (a b)"), ps[:, IT["fq"]["acc"] + i, :],
                                     ACT.Copy, scale=FOX_SCALE).then_inc(S("fq_out"), 1)
            split("fk", 3)
            split("fv", 0, 3)
            done("fk")
            for i in range(2):
                nc.scalar.activation(fkT[:, 2 * i:2 * i + 2, :].rearrange("p a b -> p (a b)"), ps[:, IT["fk"]["acc"] + i, :],
                                     ACT.Copy).then_inc(S("fk_out"), 1)
            split("fv", 3)
            split("uq0")
            split("uq1", 0, 1)
            for j in range(5):
                act.wait_ge(S("lat_turned"), j // 2 + 1)
                g = colT[:, ROW["q_g"] + j:ROW["q_g"] + j + 1]
                nc.scalar.activation(aH[:, j, :], ps[:, 4 + j // 2, 256 * (j % 2):256 * (j % 2) + 256], ACT.Copy, scale=g)\
                    .then_inc(S("lat_high"), 1)
            act.wait_ge(S("logf_steps"), 1)
            link(nc.scalar.activation(fz[:, 1], fz[:, 1], ACT.Exp))
            nc.scalar.activation(fz[:, 1], fz[:, 1], ACT.Ln, bias=1.0).then_inc(S("logf_steps"), 1)
            split("uq1", 1)
            split("ukv0")
            done("uq0")

            def uq_out(i):
                for tt in range(TT):
                    nc.scalar.activation(q_tok[:, tt, 4 * i:4 * i + 4, :].rearrange("p h n -> p (h n)"),
                                         ps[:, IT[f"uq{i}"]["acc"] + tt, 0:384], ACT.Copy).then_inc(S("uq_out"), 1)

            def ukv_out(i):
                for tt in range(TT):
                    kv = ps[:, IT[f"ukv{i}"]["acc"] + tt, :].rearrange("p (h n) -> p h n", h=4)
                    nc.scalar.activation(k_tok[:, tt, 4 * i:4 * i + 4, 0:NOPE], kv[:, :, 0:NOPE], ACT.Copy)\
                        .then_inc(S("ukv_out"), 1)
                    nc.scalar.activation(v_tok[:, tt, 256 * i:256 * i + 256].rearrange("p (h n) -> p h n", h=4),
                                         kv[:, :, NOPE:NOPE + VDIM], ACT.Copy).then_inc(S("ukv_out"), 1)

            uq_out(0)
            split("ukv1")
            done("uq1")
            uq_out(1)
            split("g0", 0, 2)
            done("ukv0")
            ukv_out(0)
            done("ukv1")
            ukv_out(1)
            split("g0", 2)

            def gate_out(j):
                done(f"g{j}")
                if j == 0:
                    act.wait_ge(S("ada_turned"), 2)
                for i in range(2):
                    nc.scalar.activation(sig[:, 4 * j + 2 * i:4 * j + 2 * i + 2, :].rearrange("p a b -> p (a b)"),
                                         ps[:, IT[f"g{j}"]["acc"] + i, :], ACT.Copy).then_inc(S("gate_out"), 1)

            split("g1", 0, 2)
            gate_out(0)
            for i in range(4):
                act.wait_ge(S("k_turned"), i + 1)
                nc.scalar.activation(kT[0:QK, 2 * i:2 * i + 2, :].rearrange("p a b -> p (a b)"), ps[0:QK, 6 + i % 2, :],
                                     ACT.Copy).then_inc(S("kT_out"), 1)

            def exps(a):
                act.wait_ge(S("att_max"), a + 1)
                for tt, (c0, n) in enumerate(((0, P), (P, 2 * P))):
                    v = prob_of(a)[:, c0:c0 + n]
                    nc.scalar.activation(v, v, ACT.Exp, bias=nmax[:, a % 4, tt:tt + 1],
                                         accum_out=rsum[:, a % 4, tt:tt + 1]).then_inc(S("att_exp"), 1)

            def turn_out(a):
                act.wait_ge(S("att_turned"), a + 1)
                if a >= 2:
                    act.wait_ge(S("att_pv"), a - 1)
                nc.scalar.activation(pT[:, a % 2, :], ps[:, 4, 0:3 * P], ACT.Copy).then_inc(S("att_pT"), 1)

            def o_high(j):
                act.wait_ge(S("att_pv"), 2 * j + 2)
                nc.scalar.activation(aH[:, (j + 4) % 8, :], ps[:, 5 + j % 2, 0:SEQ], ACT.Copy).then_inc(S("o_high"), 1)

            N1 = 2 * HEADS
            split("g1", 2, 3)
            exps(0)
            exps(1)
            for a in range(N1):
                if a in GATE_STEPS:
                    split_gate(split, GATE_STEPS.index(a) + CHUNKS - 1)
                turn_out(a)
                if a in GATE_STEPS and GATE_STEPS.index(a) % 4 == 3:
                    gate_out(1 + GATE_STEPS.index(a) // 4)
                if a + 2 < N1:
                    exps(a + 2)
                if a >= 2 and a % 2 == 0:
                    o_high(a // 2 - 1)
            split("om1", 1)
            o_high(HEADS - 1)
            for i in range(2):
                split(f"of{i}")
                for j in range(2):
                    v = sig[:, 8 * i + 4 * j:8 * i + 4 * j + 4, :]
                    act.wait_ge(S("gate_out"), 8)
                    nc.scalar.activation(v, v, ACT.Sigmoid).then_inc(S("sig_ready"), 1)
            split("wo0", 0, 2)
            for m in range(KD):
                if m == 4:
                    split("wo0", 2)
                act.wait_ge(S("y_ready"), m // 2 + 1)
                nc.scalar.activation(hH[:, m, :], yF[:, m, :], ACT.Copy).then_inc(S("y_high"), 1)
            split("wo1")
            split("up0", 0, 3)
            norm_squares(1)
            split("up0", 3)
            norm_high(1, adaT[:, SH_F:SH_F + KD])

            def conv_first(j):
                done(f"up{j}")
                if j >= 2:
                    act.wait_ge(S("act_f"), j - 1)
                for m in range(4):
                    tile = 2 * j + m if m < 2 else FT + 2 * j + m - 2
                    nc.scalar.activation(conv[:, j % 2, m, :], ps[:, IT[f"up{j}"]["acc"] + m // 2, 256 * (m % 2):256 * (m % 2) + 256],
                                         ACT.Identity, scale=colT[:, ROW["conv_w2_ff"] + tile:ROW["conv_w2_ff"] + tile + 1],
                                         bias=colT[:, ROW["conv_b"] + tile:ROW["conv_b"] + tile + 1]).then_inc(S("conv_1"), 1)

            def silu_gate(j):
                act.wait_ge(S("conv_2"), j + 1)
                v = conv[:, j % 2, 0:2, :]
                nc.scalar.activation(v, v, ACT.Silu).then_inc(S("silu"), 1)

            def ff_high(j):
                act.wait_ge(S("act_f"), j + 1)
                if j >= UP_A:
                    act.wait_ge(S("chunk_used"), IT["dn2"]["c1"])
                k = 2 * j if j < UP_A else 2 * (j - UP_A)
                nc.scalar.activation(aH[:, k:k + 2, :], actF[:, j % 2], ACT.Copy).then_inc(S("ff_high"), 1)

            def after_up(j, name):
                conv_first(j)
                split(name, 0, 1)
                silu_gate(j)
                split(name, 1, 2)
                ff_high(j)
                split(name, 2)

            split("up1")
            for j in range(2, UP_A):
                after_up(j - 2, f"up{j}")
            after_up(UP_A - 2, "dn0")
            after_up(UP_A - 1, "dn1")
            split("dn2")
            split(f"up{UP_A}")
            split(f"up{UP_A + 1}")
            for j in range(UP_A + 2, 11):
                after_up(j - 2, f"up{j}")
            after_up(9, "dn3")
            after_up(10, "dn4")
            split("dn5")
            split("q2", 0, 2)
            for k in range(KD):
                norm_square(2, k, XT_BASE[2] + k + 1)
            split("q2", 2)
            norm_high(3, None)
            split("k2")
            split("v2", 0, 2)
            act.wait_ge(S("q2_out"), 2)
            nc.scalar.activation(sq2, q2, ACT.Square).then_inc(S("q2_sq"), 1)
            split("v2", 2)
            split("xc", 0, 2)
            act.wait_ge(S("k2_out"), 2)
            act.wait_ge(S("q2_ms"), 1)
            nc.scalar.activation(sq2, k2, ACT.Square).then_inc(S("k2_sq"), 1)
            split("xc", 2)
            split("cg", 0, 2)
            done("v2")
            for tt in range(TT):
                nc.scalar.activation(v2[:, tt, :], ps[:, IT["v2"]["acc"] + tt, :], ACT.Copy).then_inc(S("v2_out"), 1)
            act.wait_ge(S("lam_steps"), 2)
            nc.scalar.activation(lam[:, 2:4], ps[:, 4, 0:2], ACT.Exp).then_inc(S("lam_steps"), 1)
            split("cg", 2)
            done("xc")
            for i in range(2):
                nc.scalar.activation(cz[:, 2 * i:2 * i + 2, :].rearrange("p a b -> p (a b)"), ps[:, IT["xc"]["acc"] + i, :],
                                     ACT.Copy).then_inc(S("xc_out"), 1)
            for i in range(2):
                act.wait_ge(S("k2_turned"), i + 1)
                nc.scalar.activation(kT2[:, 2 * i:2 * i + 2, :].rearrange("p a b -> p (a b)"), ps[:, 6 + i, :], ACT.Copy,
                                     scale=colT[:, ROW["kg2"]:ROW["kg2"] + 1]).then_inc(S("kT2_out"), 1)
            N2 = 2 * N_HEADS2

            def turn_out2(h):
                act.wait_ge(S("diff_turned"), h + 1)
                if h >= 2:
                    act.wait_ge(S("diff_pv"), h - 1)
                nc.scalar.activation(pT[:, h % 2, :], ps[:, 4, 0:3 * P], ACT.Copy).then_inc(S("diff_pT"), 1)

            w2c = ROW["conv_w2"]
            def squares_o2(h):
                act.wait_ge(S("o2_out"), h + 1)
                if h:
                    act.wait_ge(S("sub_sq"), TT * h)
                for tt in range(TT):
                    nc.scalar.activation(squares_junk[:, tt, :], o2[:, tt, h * V2:h * V2 + V2], ACT.Square,
                                         accum_out=ssq_o[:, h, tt:tt + 1]).then_inc(S("sub_sq"), 1)

            def high_o2(h):
                act.wait_ge(S("o2_turned"), h + 1)
                nc.scalar.activation(aH[:, 4 + h, :], ps[:, 5, 256 * (h % 2):256 * (h % 2) + 256], ACT.Copy,
                                     scale=sub8[:, 0:1]).then_inc(S("mix_high"), 1)

            exps(N1)
            exps(N1 + 1)
            for st in range(N2):
                h = st // 2
                if 1 <= st < 5:
                    split("bg", st - 1, st)
                elif 5 <= st < 7:
                    split("w2o_attn", st - 5, st - 4)
                if st % 2:
                    turn_out2(h)
                if st + 2 < N2:
                    exps(N1 + st + 2)
                if st % 2 and h >= 1:
                    squares_o2(h - 1)
                if st % 2 and h >= 2:
                    high_o2(h - 2)
                if st == 4:
                    act.wait_ge(S("cg_out"), 2)
                    for m in range(4):
                        nc.scalar.activation(cy[:, m, :], cz[:, m, :], ACT.Copy, scale=colT[:, w2c + 8 + m:w2c + 9 + m])\
                            .then_inc(S("cy_1"), 1)
            split("w2o_attn", 2, 3)
            high_o2(2)
            squares_o2(3)
            act.wait_ge(S("cy_ready"), 2)
            nc.scalar.activation(csq, cy, ACT.Square).then_inc(S("cv_sq"), 1)
            split("w2o_attn", 3)
            high_o2(3)
            split("w2o_conv", 0, 2)
            for m in range(4):
                act.wait_ge(S("mixF"), m + 1)
                nc.scalar.activation(aH[:, m, :], cy[:, m, :], ACT.Copy).then_inc(S("mix_high"), 1)
            split("w2o_conv", 2)
            for i in range(4):
                act.wait_ge(S("res_turned"), i + 1)
                nc.scalar.activation(hnH[:, i // 2, 512 * (i % 2):512 * (i % 2) + 512], ps[:, i, :], ACT.Square,
                                     accum_out=ssq[:, i:i + 1]).then_inc(S("row_sq"), 1)
            for i in range(4):
                nc.scalar.activation(y_acc[:, i // 2, 512 * (i % 2):512 * (i % 2) + 512], ps[:, i, :], ACT.Copy)\
                    .then_inc(S("y_sum"), 1)
            act.wait_ge(S("norm_rstd"), 5)
            for i in range(4):
                hf, tt = divmod(i, 2)
                nc.scalar.activation(hnH[:, tt, 512 * hf:512 * hf + 512], ps[:, 2 * tt + hf, :], ACT.Copy,
                                     scale=rstd[:, tt:tt + 1]).then_inc(S("hn_high"), 1)
            act.wait_ge(S("g_shift"), 1)
            nc.scalar.activation(gexp, gtmp, ACT.Exp).then_inc(S("g_exp"), 1)
            act.wait_ge(S("e_shift"), 1)
            nc.scalar.activation(ed, ed, ACT.Exp).then_inc(S("e_exp"), 1)
            def gather_out(count):
                for i in range(4):
                    act.wait_ge(S("gathered"), count + (i + 1))
                    for kk in range(2):
                        g2 = ROW["ffn_g2"] + 2 * i + kk
                        ins = nc.scalar.activation(xg[:, 2 * i + kk, :], ps[:, 6 + i % 2, SEQ * kk:SEQ * kk + SEQ], ACT.Copy,
                                                   scale=colT[:, g2:g2 + 1])
                    ins.then_inc(S("xg_out"), 1)

            gather_out(0)
            act.wait_ge(S("npass_ready"), 1)
            n = act.value_load(npass[0:1, 0:1], min_val=1, max_val=SEQ // CAP)
            with act.Fori(0, n) as p:
                with act.Fori(0, TURNS) as g:
                    turn = p * TURNS + g
                    act.wait_ge(S("put_turned"), turn + 1)
                    nc.scalar.activation(putT.rearrange("p a b -> p (a b)"), ps[:, 5, :], ACT.Copy).then_inc(S("putT_out"), 1)
                    for r in range(2):
                        act.wait_ge(S("expert_used"), turn * 8 + (4 * r + 1))
                        nc.scalar.activation(sg, ps[:, 0, :], ACT.Silu).then_inc(S("e_silu"), 1)
                        act.wait_ge(S("e_turned"), turn * 2 + (r + 1))
                        nc.scalar.activation(eactT.rearrange("p a b -> p (a b)"), ps[:, 2, :], ACT.Copy).then_inc(S("e_actT"), 1)
                        for hf in range(2):
                            act.wait_ge(S("expert_used"), turn * 8 + (4 * r + 3 + hf))
                            nc.scalar.activation(eout[:, 512 * hf:512 * hf + 512], ps[:, 3 + hf, :], ACT.Copy)\
                                .then_inc(S("e_out"), 1)
                    gather_out(turn * 4 + 4)

        @block.tensor
        def _(pe):
            def mm(o_, l, r, start, stop):
                return nc.tensor.matmul(o_, l, r, start=start, stop=stop, skip_group_check=True)

            def chunk(name, ci, xh, xl, by_token, banks=None, first=True, last=True, ready=None):
                it = IT[name]
                n = it["n"]
                b0 = it["acc"] if banks is None else banks
                main = n if n > 520 else min(n, 512)
                k0, kn = it["chunks"][ci]
                c = it["c0"] + ci
                pe.wait_ge(S("chunk_low"), c + 1)
                for kk in range(kn):
                    k = k0 + kk
                    if ready is not None:
                        pe.wait_ge(S(ready[0]), ready[1][k])
                    st, sp_ = first and k == 0, last and k == it["kn"] - 1
                    h = wh[:, c % CHUNKS, kk * n:(kk + 1) * n]
                    l = wl[:, c % CHUNKS, kk * n:(kk + 1) * n]
                    if by_token:
                        for tt in range(TT):
                            ts = slice(tt * P, tt * P + P)
                            o_ = ps[:, b0 + tt, 0:main]
                            mm(o_, xh[:, k, ts], h[:, 0:main], st, False)
                            mm(o_, xl[:, k, ts], h[:, 0:main], False, False)
                            ins = mm(o_, xh[:, k, ts], l[:, 0:main], False, sp_)
                            if n > main:
                                o_ = ps[:, 4, tt * (n - main):(tt + 1) * (n - main)]
                                mm(o_, xh[:, k, ts], h[:, main:n], st and tt == 0, False)
                                mm(o_, xl[:, k, ts], h[:, main:n], False, False)
                                ins = mm(o_, xh[:, k, ts], l[:, main:n], False, sp_)
                    else:
                        for m in range(n // P):
                            cs = slice(m * P, m * P + P)
                            o_ = ps[:, b0 + m // 2, 256 * (m % 2):256 * (m % 2) + 256]
                            mm(o_, h[:, cs], xh[:, k, :], st and m % 2 == 0, False)
                            mm(o_, h[:, cs], xl[:, k, :], False, False)
                            ins = mm(o_, l[:, cs], xh[:, k, :], False, sp_)
                ins.then_inc(S("chunk_used"), 1)

            def linear(name, xh, xl, by_token, banks=None, first=True, last=True, ready=None):
                for ci in range(len(IT[name]["chunks"])):
                    chunk(name, ci, xh, xl, by_token, banks, first, last, ready)

            def ada_part(third, i):
                it = IT[f"ada{third}{i}"]
                pe.wait_ge(S(f"slot{it['slot']}_loaded"), it["loaded"])
                w = slot_view(it)
                for kk in range(2):
                    k = 2 * i + kk
                    for q in range(4):
                        ins = mm(ps[32 * q:32 * q + 1, 7, :], cact[:, k:k + 1], w[:, kk, 512 * q:512 * q + 512],
                                 k == 0, k == KD - 1)
                ins.then_inc(S("ada_used"), 1)

            def ada_turn(third):
                pe.wait_ge(S("ada_row"), third + 1)
                for s in range(4):
                    ins = nc.tensor.transpose(ps[:, 6, s * P:s * P + P], ada_rows[third][:, s * P:s * P + P], ident[:])
                ins.then_inc(S("ada_turned"), 1)

            def norm_sums(n, count, bank):
                rows_n = 2 if n == 2 else 1
                for k in range(KD):
                    pe.wait_ge(S("norm_sq"), SQ_BASE[n] + k + 1)
                    ins = mm(ps[0:rows_n, bank, 0:SEQ], gain_sq[:, k, :] if n == 2 else ones[:, 0:1], n_sq[:, k, :],
                             k == 0, k == KD - 1)
                ins.then_inc(S("norm_sum"), 1)
                pe.wait_ge(S("norm_row"), count)
                for tt in range(TT):
                    c0 = SEQ + rows_n * tt
                    ins = nc.tensor.transpose(ps[:, bank, c0:c0 + rows_n], n_row[0:rows_n, tt * P:tt * P + P],
                                              ident[0:rows_n, 0:rows_n])
                ins.then_inc(S("norm_turned"), 1)

            def norm_spread(ready, count, src, bank, c0=0):
                pe.wait_ge(S(ready), count)
                for tt in range(TT):
                    ins = mm(ps[:, bank, c0 + tt * P:c0 + tt * P + P], src[:, tt:tt + 1].to_broadcast([P, P]), ident[:],
                             c0 == 0 and tt == 0, True)
                ins.then_inc(S("norm_bc"), 1)

            pe.wait_ge(S("consts"), 1)
            pe.wait_ge(S("c_loaded"), 16)
            nc.tensor.transpose(ps[:, 6, 0:KD], c_rows[:], ident[0:KD, 0:KD]).then_inc(S("c_steps"), 1)
            pe.wait_ge(S("c_steps"), 2)
            pe.wait_ge(S("bank7_zero"), 1)
            for i in range(2):
                ada_part(0, i)
            pe.wait_ge(S("x_loaded"), 16)
            for i in range(4):
                for kk in range(2):
                    for tt in range(TT):
                        k = 2 * i + kk
                        ins = nc.tensor.transpose(ps[:, 1 + i, 256 * kk + P * tt:256 * kk + P * tt + P],
                                                  x_tok[:, tt, k * P:k * P + P], ident[:])
                ins.then_inc(S("x_turned"), 1)
            pe.wait_ge(S("rows_loaded"), ROWS_TOTAL)
            for i in range(3):
                ins = nc.tensor.transpose(ps[:, 0, i * P:i * P + P], rows[:, i, :], ident[:])
            ins.then_inc(S("row_steps"), 1)
            norm_sums(0, 1, 5)
            norm_spread("norm_rstd", 1, rstd, 4)
            for i in range(2, 4):
                ada_part(0, i)
            ada_turn(0)
            linear("cq", hH, hL, True, ready=("norm_in", [IN_BASE[0] + k + 1 for k in range(KD)]))
            linear("ckv", hH, hL, True)
            pe.wait_ge(S("lat_copied"), 2)
            linear("fq", hH, hL, False)
            pe.wait_ge(S("ada_row"), 1)
            ada_part(1, 0)
            pe.wait_ge(S("lat_copied"), 4)
            linear("fk", hH, hL, False)
            ada_part(1, 1)
            pe.wait_ge(S("fq_out"), 2)
            linear("fv", hH, hL, True)
            pe.wait_ge(S("lat_n"), 1)
            pe.wait_ge(S("fz_in"), 1)
            for j in range(5):
                for tt in range(TT):
                    src = cqkv[:, tt, j * P:j * P + P]
                    ins = nc.tensor.transpose(ps[:, 4 + j // 2, 256 * (j % 2) + P * tt:256 * (j % 2) + P * tt + P], src, ident[:])
                if j % 2 or j == 4:
                    ins.then_inc(S("lat_turned"), 1)
            ada_part(1, 2)
            pe.wait_ge(S("fk_out"), 2)
            linear("uq0", aH, aL, True, ready=("lat_low", [1, 2, 3]))
            pe.wait_ge(S("logf_steps"), 3)
            logf = fz[:, 2]
            mm(ps[:, 6, 256:264], tri, logf[:, 0, :], False, True)
            mm(ps[:, 6, 264:272], ones, logf[:, 0, :], False, False)
            mm(ps[:, 6, 264:272], tri, logf[:, 1, :], False, True).then_inc(S("f_cum"), 1)
            pe.wait_ge(S("lat_low"), 5)
            mm(ps[0:8, 5, 0:256], logf[:, 0, :], tri_ones[:], True, False)
            mm(ps[0:8, 5, 128:256], logf[:, 1, :], tri, False, True).then_inc(S("f_cum"), 1)
            pe.wait_ge(S("fv_out"), 2)
            linear("uq1", aH, aL, True)
            pe.wait_ge(S("uq_out"), 2)
            linear("ukv0", aH[:, 3:5], aL[:, 3:5], True)
            ada_part(1, 3)
            pe.wait_ge(S("uq_out"), 4)
            linear("ukv1", aH[:, 3:5], aL[:, 3:5], True)
            pe.wait_ge(S("ukv_out"), 4)
            pe.wait_ge(S("f_out"), 2)
            for ci in range(4):
                if ci == 1:
                    ada_turn(1)
                chunk("g0", ci, hH, hL, False)
            pe.wait_ge(S("rope_done"), 1)
            for i in range(4):
                for src, bank, sem, free in ((q_tok, 4, "q_turned", "qT_out"), (k_tok, 6, "k_turned", "kT_out")):
                    if i >= 2:
                        pe.wait_ge(S(free), i - 1)
                    elif bank == 6 and i == 0:
                        pe.wait_ge(S("ada_cols"), 2)
                    for hh in range(2):
                        for tt in range(TT):
                            c0 = 256 * hh + P * tt
                            ins = nc.tensor.transpose(ps[0:QK, bank + i % 2, c0:c0 + P], src[:, tt, 2 * i + hh, :], ident[:])
                    ins.then_inc(S(sem), 1)

            def scores(a):
                if a >= 2:
                    pe.wait_ge(S("att_in"), a - 1)
                h = a % HEADS
                for tt, (c0, n) in enumerate(((0, P), (P, 2 * P))):
                    o_ = ps[:, 2 + a % 2, c0:c0 + n]
                    qs = slice(tt * P, tt * P + P)
                    if a < HEADS:
                        r = slice(64 * (h % 2), 64 * (h % 2) + 64)
                        mm(o_, fqT[r, h // 2, qs], fkT[r, h // 2, 0:n], tt == 0, False)
                        ins = mm(o_, ident[0:HEADS, h:h + 1].to_broadcast([HEADS, P]), nFT[:, 0:n], False, True)
                    else:
                        ins = mm(o_, qT[0:QK, h, qs], kT[0:QK, h, 0:n], tt == 0, True)
                ins.then_inc(S("att_logits"), 1)

            def turn(a):
                pe.wait_ge(S("att_p"), a + 1)
                if a >= 1:
                    pe.wait_ge(S("att_pT"), a)
                for i, c0 in enumerate((0, P, 2 * P)):
                    ins = nc.tensor.transpose(ps[:, 4, i * P:i * P + P], prob_of(a)[:, c0:c0 + P], ident[:])
                ins.then_inc(S("att_turned"), 1)

            def values(a):
                pe.wait_ge(S("att_pT"), a + 1)
                j = a // 2
                if a % 2 == 0 and j >= 2:
                    pe.wait_ge(S("o_low"), j - 1)
                h = a % HEADS
                v = fv_tok if a < HEADS else v_tok
                r = slice(64 * (a % 2), 64 * (a % 2) + 64)
                mm(ps[r, 5 + j % 2, 0:SEQ], v[:, 0, 64 * h:64 * h + 64], pT[:, a % 2, 0:SEQ], True, False)
                mm(ps[r, 5 + j % 2, P:SEQ], v[:, 1, 64 * h:64 * h + 64], pT[:, a % 2, SEQ:SEQ + P], False, True)\
                    .then_inc(S("att_pv"), 1)

            N1 = 2 * HEADS
            pe.wait_ge(S("gate_out"), 2)
            pe.wait_ge(S("qT_out"), 4)
            pe.wait_ge(S("kT_out"), 4)
            pe.wait_ge(S("ukv_out"), 8)
            scores(0)
            scores(1)
            ada_part(2, 0)
            for a in range(N1):
                if a + 2 < N1:
                    scores(a + 2)
                if a in GATE_STEPS:
                    i = GATE_STEPS.index(a)
                    if i and i % 4 == 0:
                        pe.wait_ge(S("gate_out"), 2 * (i // 4) + 2)
                    chunk(f"g{1 + i // 4}", i % 4, hH, hL, False)
                turn(a)
                if a >= 1:
                    values(a - 1)
                if a in GATE_STEPS and GATE_STEPS.index(a) % 4 == 3:
                    ada_part(2, 1 + GATE_STEPS.index(a) // 4)
            values(N1 - 1)
            pe.wait_ge(S("o_low"), HEADS)
            linear("om0", aH, aL, False)
            ada_turn(2)
            pe.wait_ge(S("gate_out"), 8)
            linear("om1", aH, aL, False)
            pe.wait_ge(S("om_out"), 2)
            linear("of0", aH[:, 4:8], aL[:, 4:8], False)
            pe.wait_ge(S("om_out"), 4)
            linear("of1", aH[:, 4:8], aL[:, 4:8], False)
            y_low = ("y_low", [1] * 4 + [2] * 4)
            pe.wait_ge(S("y_ready"), 2)
            linear("wo0", hH, hL, False, ready=y_low)
            pe.wait_ge(S("y_ready"), 4)
            linear("wo1", hH, hL, False)
            norm_sums(1, 2, 4)
            norm_spread("norm_rstd", 2, rstd, 5)
            for j in range(UP_A):
                if j >= 2:
                    pe.wait_ge(S("act_f"), j - 1)
                linear(f"up{j}", hH, hL, False, ready=("norm_in", [IN_BASE[1] + k + 1 for k in range(KD)]) if j == 0 else None)
            for i in range(3):
                pe.wait_ge(S("ff_low"), 2 * i + 2)
                linear(f"dn{i}", aH[:, 4 * i:4 * i + 4], aL[:, 4 * i:4 * i + 4], False, 4, i == 0, False)
            for j in range(UP_A, 11):
                pe.wait_ge(S("act_f"), j - 1)
                linear(f"up{j}", hH, hL, False)
            for i in range(3, 6):
                pe.wait_ge(S("ff_low"), min(2 * i + 2, 11))
                k = 4 * (i - 3)
                linear(f"dn{i}", aH[:, k:k + 4], aL[:, k:k + 4], False, 4, False, i == 5)
            pe.wait_ge(S("act_f"), 11)
            norm_sums(2, 3, 2)
            norm_spread("norm_rstd", 3, rstd, 3)
            norm_spread("norm_r12", 1, r12, 3, SEQ)
            linear("q2", hH, hL, True, ready=("norm_in", [IN_BASE[3] + k + 1 for k in range(KD)]))
            pe.wait_ge(S("xT_ready"), XT_BASE[4])
            linear("k2", hH, hL, True)
            pe.wait_ge(S("q2_out"), 2)
            linear("v2", hH, hL, True)
            pe.wait_ge(S("lam_steps"), 1)
            mm(ps[:, 4, 0:2], ones, lam[:, 0:2], True, True).then_inc(S("lam_steps"), 1)
            pe.wait_ge(S("k2_out"), 2)
            linear("xc", hH, hL, False)
            pe.wait_ge(S("lam_steps"), 3)
            for src, bank, ready, sem in ((qn, 4, "qn", "q2_turned"), (kn, 6, "kn", "k2_turned")):
                pe.wait_ge(S(ready), 1)
                for i in range(2):
                    for hh in range(2):
                        for tt in range(TT):
                            h = 2 * i + hh
                            ins = nc.tensor.transpose(ps[:, bank + i, 256 * hh + P * tt:256 * hh + P * tt + P],
                                                      src[:, tt, h * P:h * P + P], ident[:])
                    ins.then_inc(S(sem), 1)

            def scores2(a):
                h, c = divmod(a, 2)
                if a >= 2:
                    pe.wait_ge(S("att_in"), N1 + a - 1)
                r = slice(64 * c, 64 * c + 64)
                for tt, (c0, n) in enumerate(((0, P), (P, 2 * P))):
                    ins = mm(ps[:, 2 + a % 2, c0:c0 + n], qT2[r, h, tt * P:tt * P + P], kT2[r, h, 0:n], tt == 0, True)
                ins.then_inc(S("att_logits"), 1)

            def turn2(h):
                pe.wait_ge(S("diff_p"), h + 1)
                if h >= 1:
                    pe.wait_ge(S("diff_pT"), h)
                for i, c0 in enumerate((0, P, 2 * P)):
                    ins = nc.tensor.transpose(ps[:, 4, i * P:i * P + P], prob_of(N1 + 2 * h)[:, c0:c0 + P], ident[:])
                ins.then_inc(S("diff_turned"), 1)

            def turn_o2(h):
                pe.wait_ge(S("sub_n"), h + 1)
                if h >= 1:
                    pe.wait_ge(S("mix_low"), h)
                else:
                    pe.wait_ge(S("qT2_out"), 2)
                for tt in range(TT):
                    ins = nc.tensor.transpose(ps[:, 5, 256 * (h % 2) + P * tt:256 * (h % 2) + P * tt + P],
                                              o2[:, tt, h * P:h * P + P], ident[:])
                ins.then_inc(S("o2_turned"), 1)

            def values2(h):
                pe.wait_ge(S("diff_pT"), h + 1)
                if h >= 2:
                    pe.wait_ge(S("o2_out"), h - 1)
                vs = slice(h * V2, h * V2 + V2)
                mm(ps[:, 6 + h % 2, 0:P], pT[:, h % 2, 0:P], v2[:, 0, vs], True, True)
                mm(ps[:, 6 + h % 2, P:2 * P], pT[:, h % 2, P:2 * P], v2[:, 0, vs], False, False)
                mm(ps[:, 6 + h % 2, P:2 * P], pT[:, h % 2, 2 * P:3 * P], v2[:, 1, vs], False, True).then_inc(S("diff_pv"), 1)

            pe.wait_ge(S("v2_out"), 2)
            pe.wait_ge(S("xc_out"), 2)
            pe.wait_ge(S("qT2_out"), 2)
            pe.wait_ge(S("kT2_out"), 2)
            N2 = 2 * N_HEADS2
            scores2(0)
            scores2(1)
            for st in range(N2):
                h = st // 2
                if st + 2 < N2:
                    scores2(st + 2)
                if st < 4:
                    chunk("cg", st, hH, hL, False)
                else:
                    if st == 4:
                        pe.wait_ge(S("cg_out"), 2)
                    chunk("bg", st - 4, hH, hL, False)
                if st % 2:
                    turn2(h)
                    if h >= 1:
                        values2(h - 1)
                    if h >= 2:
                        turn_o2(h - 2)
            values2(N_HEADS2 - 1)
            turn_o2(2)
            pe.wait_ge(S("att_in"), N1 + N2)
            pe.wait_ge(S("cy_ready"), 2)
            o_in = ("mix_low", [1, 2, 3, 4])
            chunk("w2o_attn", 0, aH[:, 4:8], aL[:, 4:8], False, 0, True, False, o_in)
            pe.wait_ge(S("cv_sq"), 1)
            pe.wait_ge(S("o2_out"), 3)
            for tt in range(TT):
                for m in range(4):
                    c0 = 8 * tt + 2 * m
                    ins = mm(ps[:, 6, c0:c0 + 2], csq[:, m, tt * P:tt * P + P], half_ind[:], tt == 0 and m == 0, True)
            ins.then_inc(S("cv_sum"), 1)
            chunk("w2o_attn", 1, aH[:, 4:8], aL[:, 4:8], False, 0, True, False, o_in)
            turn_o2(3)
            chunk("w2o_attn", 2, aH[:, 4:8], aL[:, 4:8], False, 0, True, False, o_in)
            pe.wait_ge(S("cv_rstd"), 1)
            for m in range(4):
                for tt in range(TT):
                    for g in range(2):
                        c0 = 8 * tt + 2 * m + g
                        ins = mm(ps[64 * g:64 * g + 64, 6 + m // 2, 256 * (m % 2) + P * tt:256 * (m % 2) + P * tt + P],
                                 rstd[:, c0:c0 + 1].to_broadcast([P, 64]), ident[:], tt == 0 and m % 2 == 0, True)
            ins.then_inc(S("cv_bc"), 1)
            chunk("w2o_attn", 3, aH[:, 4:8], aL[:, 4:8], False, 0, True, False, o_in)
            linear("w2o_conv", aH, aL, False, 0, False, True, ("mix_low", [5, 6, 7, 8]))
            for i in range(4):
                for j in range(4):
                    k = 4 * (i % 2) + j
                    if i < 2:
                        pe.wait_ge(S("xT_ready"), XT_BASE[4] + max(k + 1, 2))
                    ins = nc.tensor.transpose(ps[:, i, j * P:j * P + P], xT[:, k, (i // 2) * P:(i // 2) * P + P], ident[:])
                ins.then_inc(S("res_turned"), 1)
            pe.wait_ge(S("router_scaled"), 1)
            for k in range(KD):
                for tt in range(TT):
                    ins = mm(ps[:, 6, tt * 64:tt * 64 + LG], xT[:, k, tt * P:tt * P + P], wr[:, k, :],
                             tt == 0 and k == 0, k == KD - 1)
            ins.then_inc(S("logits"), 1)
            pe.wait_ge(S("sel"), 1)
            s0, s1 = (sel[:, tt].rearrange("p g e -> p (g e)") for tt in range(TT))
            mm(ps[:, 7, 0:32], tri, s0, True, True)
            mm(ps[:, 7, 32:64], ones, s0, False, False)
            mm(ps[:, 7, 32:64], tri, s1, False, True)
            mm(ps[0:1, 7, 64:96], ones[:, 0:1], s0, False, False)
            mm(ps[0:1, 7, 64:96], ones[:, 0:1], s1, False, True).then_inc(S("places"), 1)

            def gather(turn, first=False):
                pe.wait_ge(S("pick_half"), turn * 2 + 2)
                for i in range(4):
                    if i >= 2:
                        pe.wait_ge(S("xg_out"), turn * 4 + (i - 1))
                    elif not first:
                        pe.wait_ge(S("y_sum"), turn * 8 + (3 + i))
                    if first and i % 2 == 0:
                        pe.wait_ge(S("hn_low"), i + 2)
                    for kk in range(2):
                        k = 2 * i + kk
                        o_ = ps[:, 6 + i % 2, 256 * kk:256 * kk + 256]
                        for tt in range(TT):
                            mm(o_, hnH[:, tt, k * P:k * P + P], pick[:, tt, :], kk == 0 and tt == 0, False)
                            ins = mm(o_, hnL[:, tt, k * P:k * P + P], pick[:, tt, :], False, tt == TT - 1)
                    ins.then_inc(S("gathered"), 1)

            def gate_weights(r, j, k):
                if r == 0 or j == 0:
                    return slot(j if r == 0 else 6)[:, D_EXP * k:D_EXP * k + D_EXP]
                return (slot7a[:] if k < 4 else slot7b)[:, D_EXP * (k % 4):D_EXP * (k % 4) + D_EXP]

            gather(0, first=True)
            pe.wait_ge(S("npass_ready"), 1)
            n = pe.value_load(npass[0:1, 0:1], min_val=1, max_val=SEQ // CAP)
            with pe.Fori(0, n) as p:
                with pe.Fori(0, TURNS) as g:
                    turn = p * TURNS + g
                    pe.wait_ge(S("put_half"), turn * 2 + 2)
                    for r in range(2):
                        for tt in range(TT):
                            ins = nc.tensor.transpose(ps[:, 5, 256 * r + P * tt:256 * r + P * tt + P],
                                                      put[:, tt, P * r:P * r + P], ident[:])
                    ins.then_inc(S("put_turned"), 1)
                    for r in range(2):
                        for part in range(2):
                            if part == 0 and r == 0:
                                for j in range(2):
                                    pe.wait_ge(S(f"slot{j}_loaded"), turn * 32 + (base_loaded[j] + 32))
                            elif part == 0:
                                pe.wait_ge(S("slot6_loaded"), turn * 16 + 16)
                                pe.wait_ge(S("slot7_loaded"), turn * 32 + 32)
                            for k in range(KD):
                                if part == 0 and r == 0 and k % 2 == 0:
                                    pe.wait_ge(S("xg_out"), turn * 4 + (k // 2 + 1))
                                if part == 1 and k % 4 == 0:
                                    pe.wait_ge(S(f"ups_half{k // 4}"), turn * 64 + (32 * r + 32))
                                for j in range(2):
                                    cs = slice(64 * (2 * r + j), 64 * (2 * r + j) + 64)
                                    w = gate_weights(r, j, k) if part == 0 else slot(2 + j)[:, D_EXP * k:D_EXP * k + D_EXP]
                                    ins = mm(ps[64 * j:64 * j + 64, part, :], xg[:, k, cs], w, k == 0, k == KD - 1)
                                if part == 0 and k == KD // 2 - 1:
                                    ins.then_inc(S("gate_half"), 1)
                            ins.then_inc(S("expert_used"), 1)
                        pe.wait_ge(S("e_act"), turn * 2 + (r + 1))
                        for f in range(4):
                            ins = nc.tensor.transpose(ps[:, 2, f * P:f * P + P], eact[:, f * P:f * P + P], ident[:])
                        ins.then_inc(S("e_turned"), 1)
                        pe.wait_ge(S("e_actT"), turn * 2 + (r + 1))
                        for hf in range(2):
                            pe.wait_ge(S(f"downs_half{hf}"), turn * 64 + (32 * r + 32))
                            for k in range(4):
                                for j in range(2):
                                    w = slot(4 + j)[:, 512 * (4 * hf + k):512 * (4 * hf + k) + 512]
                                    ins = mm(ps[64 * j:64 * j + 64, 3 + hf, :], eactT[:, k, 64 * j:64 * j + 64], w,
                                             k == 0, k == 3)
                            ins.then_inc(S("expert_used"), 1)
                        pe.wait_ge(S("putT_out"), turn + 1)
                        for i in range(4):
                            hf, tt = divmod(i, 2)
                            if tt == 0:
                                pe.wait_ge(S("e_out"), turn * 4 + (2 * r + hf + 1))
                            if r == 1 or i >= 2:
                                pe.wait_ge(S("y_sum"), turn * 8 + (4 * r + 4 + i - 1))
                            mm(ps[:, 6 + i % 2, :], putT[:, r, P * tt:P * tt + P], eout[:, 512 * hf:512 * hf + 512],
                               True, True).then_inc(S("e_put"), 1)
                    gather(turn + 1)

        @block.vector
        def _(dve):
            chain = [0]
            V = nc.vector

            def link(ins):
                chain[0] += 1
                ins.then_inc(S("dve_chain"), 1)
                dve.wait_ge(S("dve_chain"), chain[0])

            def split(name, a=0, b=None):
                it = IT[name]
                for ci in range(a, len(it["chunks"]) if b is None else b):
                    c = it["c0"] + ci
                    dve.wait_ge(S("chunk_high"), c + 1)
                    src, n = raw_chunk(it, ci)
                    V.tensor_tensor(wl[:, c % CHUNKS, 0:n], src, wh[:, c % CHUNKS, 0:n].bitcast(F32), ALU.subtract)\
                        .then_inc(S("chunk_low"), 1)

            def done(name):
                dve.wait_ge(S("chunk_used"), IT[name]["c1"])

            def mean_sq(dst, src, width, sem):
                V.tensor_scalar(dst, src, 1.0 / width, EPS, ALU.mult, ALU.add).then_inc(S(sem), 1)

            def norm_mean(n, count, bank):
                rows_n = 2 if n == 2 else 1
                dve.wait_ge(S("norm_sum"), count)
                V.tensor_copy(n_row[0:rows_n, :], ps[0:rows_n, bank, 0:SEQ]).then_inc(S("norm_row"), 1)
                dve.wait_ge(S("norm_turned"), count)
                cols = ps[:, bank, SEQ:SEQ + rows_n * TT].rearrange("p (t r) -> p r t", t=TT)
                mean_sq(ms[:, 0:TT], cols[:, 0, :], D, "norm_ms")
                return cols

            def norm_apply(n, bc, scale, shift):
                def low(k):
                    dve.wait_ge(S("norm_high"), IN_BASE[n] + k + 1)
                    if shift is None:
                        ins = V.tensor_tensor(hL[:, k, :], n_t[:, k, :], hH[:, k, :].bitcast(F32), ALU.subtract)
                    else:
                        ins = V.scalar_tensor_tensor(out=hL[:, k, :], in0=n_t[:, k, :], scalar=shift[:, k:k + 1],
                                                     in1=hH[:, k, :].bitcast(F32), op0=ALU.add, op1=ALU.subtract)
                    ins.then_inc(S("norm_in"), 1)

                for k in range(KD):
                    V.scalar_tensor_tensor(out=n_t[:, k, :], in0=xT[:, k, :], scalar=scale[:, k:k + 1], in1=bc,
                                           op0=ALU.mult, op1=ALU.mult).then_inc(S("norm_t"), 1)
                    if k >= 2:
                        low(k - 2)
                low(KD - 2)
                low(KD - 1)

            for g in range(2):
                V.memset(half_ind[64 * g:64 * g + 64, g:g + 1], 1.0)
                V.memset(half_ind[64 * g:64 * g + 64, 1 - g:2 - g], 0.0)
            V.memset(wc[:, 0:3 * P + 512], 0.0).then_inc(S("row_steps"), 1)
            V.memset(comb[:], 0.0)
            V.memset(posm[:], 0.0)
            V.memset(ps[:, 7, :], 0.0).then_inc(S("bank7_zero"), 1)
            for i in range(4):
                dve.wait_ge(S("x_turned"), i + 1)
                V.tensor_copy(xT[:, 2 * i:2 * i + 2, :].rearrange("p a b -> p (a b)"), ps[:, 1 + i, :])\
                    .then_inc(S("xT_ready"), 1)
            dve.wait_ge(S("row_steps"), 2)
            V.tensor_copy(colT[:], ps[:, 0, 0:3 * P]).then_inc(S("row_steps"), 1)
            dve.wait_ge(S("row_steps"), 3)
            dve.wait_ge(S("misc_loaded"), 64)
            dve.wait_ge(S("consts"), 1)
            link(V.tensor_copy(pos_f[:], pos_i[:]))
            for tt in range(TT):
                ins = V.tensor_scalar(trig[:, 0, tt], invf[:], pos_f[:, tt:tt + 1], None, ALU.mult)
            link(ins)
            magic = 1.5 * 2.0 ** 23
            link(V.tensor_scalar(trig[:, 1], trig[:, 0], 1.0 / (2 * math.pi), None, ALU.mult))
            link(V.tensor_scalar(trig[:, 1], trig[:, 1], magic, None, ALU.add))
            link(V.tensor_scalar(trig[:, 1], trig[:, 1], magic, None, ALU.subtract))
            cur = trig[:, 0]
            for part in two_pi_parts():
                link(V.scalar_tensor_tensor(out=trig[:, 2], in0=trig[:, 1], scalar=-part, in1=cur, op0=ALU.mult, op1=ALU.add))
                cur = trig[:, 2]
            pi_lo = float(np.nextafter(np.float32(math.pi), np.float32(0)))
            V.tensor_scalar(trig[:, 2], trig[:, 2], pi_lo, -pi_lo, ALU.min, ALU.max).then_inc(S("rope_steps"), 1)
            link(V.tensor_tensor(scale_2[:], colT[:, ROW["fin_g"]:ROW["fin_g"] + KD], colT[:, ROW["attn_g2"]:ROW["attn_g2"] + KD],
                                 ALU.mult))
            V.memset(gain_sq[:, :, 0], 1.0)
            V.tensor_tensor(wr[:], wr[:], colT[:, ROW["ffn_g2"]:ROW["ffn_g2"] + KD].unsqueeze(2).to_broadcast([P, KD, LG]),
                            ALU.mult).then_inc(S("router_scaled"), 1)
            fg = colT[:, ROW["fin_g"]:ROW["fin_g"] + KD]
            V.tensor_tensor(gain_sq[:, :, 1], fg, fg, ALU.mult)
            norm_mean(0, 1, 5)
            dve.wait_ge(S("rope_steps"), 3)
            link(V.tensor_tensor(trig[:, 1], trig[:, 4], trig[:, 4], ALU.mult))
            V.tensor_scalar(trig[:, 4], trig[:, 1], -2.0, 1.0, ALU.mult, ALU.add).then_inc(S("rope_steps"), 1)
            sin_t, cos_t = trig[:, 3], trig[:, 4]

            def ada_row_out(third):
                dve.wait_ge(S("ada_used"), 4 * third + 4)
                V.tensor_copy(ada_rows[third], ps[:, 7, :]).then_inc(S("ada_row"), 1)

            def ada_out(third):
                dve.wait_ge(S("ada_turned"), third + 1)
                src = ps[:, 6, :].rearrange("p (s q r) -> p q s r", s=4, q=4)[:, :, :, 0]
                dst = adaT[:, 16 * third:16 * third + 16].rearrange("p (q s) -> p q s", q=4)
                b = colT[:, ROW["b_ada"] + 16 * third:ROW["b_ada"] + 16 * third + 16].rearrange("p (q s) -> p q s", q=4)
                link(V.tensor_tensor(dst, src, b, ALU.add))

            split("cq")
            ada_row_out(0)
            ada_out(0)
            V.scalar_tensor_tensor(out=scale_m[:], in0=adaT[:, SC_M:SC_M + KD], scalar=1.0,
                                   in1=colT[:, ROW["mix_g"]:ROW["mix_g"] + KD], op0=ALU.add, op1=ALU.mult)\
                .then_inc(S("ada_cols"), 1)
            dve.wait_ge(S("ada_cols"), 1)
            dve.wait_ge(S("norm_bc"), 1)
            norm_apply(0, ps[:, 4, 0:SEQ], scale_m, adaT[:, SH_M:SH_M + KD])
            split("ckv")
            done("cq")
            for tt in range(TT):
                V.tensor_copy(cqkv[:, tt, 0:Q_RANK], ps[:, IT["cq"]["acc"] + tt, 0:Q_RANK]).then_inc(S("lat_copied"), 1)
            split("fq", 0, 2)
            done("ckv")
            for tt in range(TT):
                V.tensor_copy(cqkv[:, tt, Q_RANK:CKQ], ps[:, IT["ckv"]["acc"] + tt, 0:CKQ - Q_RANK]).then_inc(S("lat_copied"), 1)
            split("fq", 2)
            dve.wait_ge(S("lat_sq"), 4)
            link(V.tensor_scalar(ms[:, 0:2], ssq[:, 0:2], 1.0 / Q_RANK, EPS, ALU.mult, ALU.add))
            mean_sq(ms[:, 2:4], ssq[:, 2:4], KV_RANK, "lat_ms")
            split("fk", 0, 3)
            dve.wait_ge(S("lat_rstd"), 1)
            for j, (c0, n) in enumerate(((0, Q_RANK), (Q_RANK, KV_RANK))):
                for tt in range(TT):
                    v = cqkv[:, tt, c0:c0 + n]
                    ins = V.tensor_scalar(v, v, rstd[:, 2 * j + tt:2 * j + tt + 1], None, ALU.mult)
            ins.then_inc(S("lat_n"), 1)
            split("fk", 3)
            split("fv")
            split("uq0")
            done("fv")
            link(V.tensor_tensor(fz[:, 0], ps[:, 4, 0:TT * HEADS].rearrange("p (t h) -> p t h", t=TT),
                                 bf_b[:].unsqueeze(1).to_broadcast([P, TT, HEADS]), ALU.add))
            V.scalar_tensor_tensor(out=fz[:, 1], in0=fz[:, 0], scalar=-1.0, in1=fz[:, 0], op0=ALU.mult, op1=ALU.min)\
                .then_inc(S("logf_steps"), 1)
            V.tensor_scalar(fz[:, 0], fz[:, 0], 0.0, None, ALU.min).then_inc(S("fz_in"), 1)
            for tt in range(TT):
                V.tensor_copy(fv_tok[:, tt, :], ps[:, IT["fv"]["acc"] + tt, :]).then_inc(S("fv_out"), 1)
            for j in range(5):
                dve.wait_ge(S("lat_high"), min(2 * (j // 2) + 2, 5))
                g = colT[:, ROW["q_g"] + j:ROW["q_g"] + j + 1]
                V.scalar_tensor_tensor(out=aL[:, j, :], in0=ps[:, 4 + j // 2, 256 * (j % 2):256 * (j % 2) + 256], scalar=g,
                                       in1=aH[:, j, :].bitcast(F32), op0=ALU.mult, op1=ALU.subtract).then_inc(S("lat_low"), 1)
            dve.wait_ge(S("logf_steps"), 2)
            V.tensor_tensor(fz[:, 2], fz[:, 0], fz[:, 1], ALU.subtract).then_inc(S("logf_steps"), 1)
            dve.wait_ge(S("f_cum"), 2)
            V.tensor_copy(f_tok[:].rearrange("p t h -> p (t h)"), ps[:, 6, 256:256 + TT * HEADS]).then_inc(S("f_out"), 1)
            V.tensor_scalar(nFT[:], ps[0:HEADS, 5, 0:256], -1.0, None, ALU.mult).then_inc(S("f_out"), 1)
            split("uq1")
            split("ukv0")
            split("ukv1")
            split("g0", 0, 2)
            ada_row_out(1)
            ada_out(1)
            V.tensor_copy(lam[:, 4:5], adaT[:, 0:1]).then_inc(S("ada_cols"), 1)
            split("g0", 2)

            def rope(x1, x2, cos_b, sin_b, tmp_a, tmp_b, last_sem):
                V.tensor_tensor(tmp_a, x2, sin_b, ALU.mult)
                link(V.tensor_tensor(tmp_b, x1, sin_b, ALU.mult))
                V.tensor_tensor(x1, x1, cos_b, ALU.mult)
                link(V.tensor_tensor(x2, x2, cos_b, ALU.mult))
                V.tensor_tensor(x1, x1, tmp_a, ALU.subtract)
                ins = V.tensor_tensor(x2, x2, tmp_b, ALU.add)
                if last_sem:
                    ins.then_inc(S(last_sem), 1)
                else:
                    link(ins)

            dve.wait_ge(S("rope_steps"), 4)
            r0 = Q_RANK + KV_RANK
            ta = wc[:, 1408:1408 + TT * HALF].rearrange("p (t n) -> p t n", t=TT)
            tb = wc[:, 1664:1664 + TT * HALF].rearrange("p (t n) -> p t n", t=TT)
            rope(cqkv[:, :, r0:r0 + HALF], cqkv[:, :, r0 + HALF:r0 + ROPE], cos_t, sin_t, ta, tb, None)
            for tt in range(TT):
                V.tensor_copy(k_tok[:, tt, :, NOPE:QK], cqkv[:, tt, r0:r0 + ROPE].unsqueeze(1).to_broadcast([P, HEADS, ROPE]))
            dve.wait_ge(S("uq_out"), 4)
            ta = wc[:, 1408:1664].rearrange("p (t h n) -> p t h n", t=TT, h=HEADS)
            tb = wc[:, 1664:1920].rearrange("p (t h n) -> p t h n", t=TT, h=HEADS)
            cos_b = cos_t.unsqueeze(2).to_broadcast([P, TT, HEADS, HALF])
            sin_b = sin_t.unsqueeze(2).to_broadcast([P, TT, HEADS, HALF])
            rope(q_tok[:, :, :, NOPE:NOPE + HALF], q_tok[:, :, :, NOPE + HALF:QK], cos_b, sin_b, ta, tb, "rope_done")
            split("g1", 0, 2)
            for i in range(4):
                dve.wait_ge(S("q_turned"), i + 1)
                V.tensor_copy(qT[0:QK, 2 * i:2 * i + 2, :].rearrange("p a b -> p (a b)"), ps[0:QK, 4 + i % 2, :])\
                    .then_inc(S("qT_out"), 1)

            def logits_in(a):
                dve.wait_ge(S("att_logits"), a + 1)
                if a == 0:
                    dve.wait_ge(S("k_turned"), 4)
                if 3 <= a < 2 * HEADS + 3:
                    dve.wait_ge(S("att_turned"), min(a - 2, 2 * HEADS))
                if a >= 2 * HEADS + 4:
                    dve.wait_ge(S("diff_turned"), (a - 4 - 2 * HEADS) // 2 + 1)
                src = ps[:, 2 + a % 2, 0:3 * P]
                p = prob_of(a)
                if a < HEADS:
                    for tt, (c0, n) in enumerate(((0, P), (P, 2 * P))):
                        ins = V.scalar_tensor_tensor(out=p[:, c0:c0 + n], in0=src[:, c0:c0 + n],
                                                     scalar=f_tok[:, tt, a:a + 1], in1=mask[:, c0:c0 + n],
                                                     op0=ALU.add, op1=ALU.add)
                elif a < 2 * HEADS:
                    ins = V.scalar_tensor_tensor(out=p, in0=src, scalar=MLA_SCALE, in1=mask[:],
                                                 op0=ALU.mult, op1=ALU.add)
                else:
                    ins = V.tensor_tensor(p, src, mask[:], ALU.add)
                ins.then_inc(S("att_in"), 1)
                dve.wait_ge(S("att_in"), a + 1)
                V.tensor_reduce(nmax[:, a % 4, 0:1], p[:, 0:P], AX_X, ALU.max, negate=True)
                V.tensor_reduce(nmax[:, a % 4, 1:2], p[:, P:3 * P], AX_X, ALU.max, negate=True).then_inc(S("att_max"), 1)

            def norm_p(a):
                dve.wait_ge(S("att_exp"), 2 * a + 2)
                link(V.reciprocal(rinv[:, a % 4, :], rsum[:, a % 4, :]))
                p = prob_of(a)
                V.tensor_scalar(p[:, 0:P], p[:, 0:P], rinv[:, a % 4, 0:1], None, ALU.mult)
                V.tensor_scalar(p[:, P:3 * P], p[:, P:3 * P], rinv[:, a % 4, 1:2], None, ALU.mult)\
                    .then_inc(S("att_p"), 1)

            def o_low(j):
                dve.wait_ge(S("o_high"), j + 1)
                V.tensor_tensor(aL[:, (j + 4) % 8, :], ps[:, 5 + j % 2, 0:SEQ], aH[:, (j + 4) % 8, :].bitcast(F32),
                                ALU.subtract).then_inc(S("o_low"), 1)

            N1 = 2 * HEADS
            split("g1", 2, 3)
            logits_in(0)
            logits_in(1)
            for a in range(N1):
                norm_p(a)
                if a + 2 < N1:
                    logits_in(a + 2)
                if a in GATE_STEPS:
                    split_gate(split, GATE_STEPS.index(a) + CHUNKS - 1)
                if a >= 3 and a % 2 == 1:
                    o_low((a - 3) // 2)
            split("om1", 1)
            o_low(HEADS - 1)
            dve.wait_ge(S("att_turned"), 2 * HEADS)
            ada_row_out(2)

            def o_proj(name, i):
                done(f"{name}{i}")
                for j in range(2):
                    m = 4 * i + 2 * j
                    dve.wait_ge(S("sig_ready"), i + 1 + (2 if name == "of" else 0))
                    src = ps[:, IT[f"{name}{i}"]["acc"] + j, :].rearrange("p (a b) -> p a b", a=2)
                    if name == "om":
                        V.tensor_tensor(yF[:, m:m + 2, :], sig[:, m:m + 2, :], src, ALU.mult).then_inc(S("om_out"), 1)
                    else:
                        link(V.tensor_tensor(sig[:, 8 + m:10 + m, :], sig[:, 8 + m:10 + m, :], src, ALU.mult))
                        V.tensor_tensor(yF[:, m:m + 2, :], yF[:, m:m + 2, :], sig[:, 8 + m:10 + m, :], ALU.add)\
                            .then_inc(S("y_ready"), 1)

            split("of0")
            o_proj("om", 0)
            ada_out(2)
            V.scalar_tensor_tensor(out=scale_f[:], in0=adaT[:, SC_F:SC_F + KD], scalar=1.0,
                                   in1=colT[:, ROW["ffn_g"]:ROW["ffn_g"] + KD], op0=ALU.add, op1=ALU.mult)\
                .then_inc(S("ada_cols"), 1)
            split("of1")
            o_proj("om", 1)
            dve.wait_ge(S("om_out"), 4)
            for i in range(2):
                o_proj("of", i)
                split("wo0", i, 3 * i + 1)
                dve.wait_ge(S("y_high"), 4 * i + 4)
                V.tensor_tensor(hL[:, 4 * i:4 * i + 4, :], yF[:, 4 * i:4 * i + 4, :], hH[:, 4 * i:4 * i + 4, :].bitcast(F32),
                                ALU.subtract).then_inc(S("y_low"), 1)
            split("wo1")

            def residual(m, src, scale, sem):
                V.scalar_tensor_tensor(out=xT[:, m, :], in0=src, scalar=scale, in1=xT[:, m, :], op0=ALU.mult, op1=ALU.add)\
                    .then_inc(S(sem), 1)

            for i in range(2):
                done(f"wo{i}")
                for j in range(4):
                    residual(4 * i + j, ps[:, IT[f"wo{i}"]["acc"] + j // 2, 256 * (j % 2):256 * (j % 2) + 256],
                             adaT[:, G_M + 4 * i + j:G_M + 4 * i + j + 1], "xT_ready")
                if i == 0:
                    split("up0", 0, 3)
            norm_mean(1, 2, 4)
            split("up0", 3)
            dve.wait_ge(S("ada_cols"), 3)
            dve.wait_ge(S("norm_bc"), 2)
            norm_apply(1, ps[:, 5, 0:SEQ], scale_f, adaT[:, SH_F:SH_F + KD])

            def conv_rest(j):
                dve.wait_ge(S("conv_1"), 4 * j + 4)
                for tap, row in ((1, "conv_w1"), (2, "conv_w0")):
                    for m in range(4):
                        tile = 2 * j + m if m < 2 else FT + 2 * j + m - 2
                        src = ps[:, IT[f"up{j}"]["acc"] + m // 2, 256 * (m % 2):256 * (m % 2) + 256 - tap]
                        v = conv[:, j % 2, m, tap:SEQ]
                        ins = V.scalar_tensor_tensor(out=v, in0=src, scalar=colT[:, ROW[row] + tile:ROW[row] + tile + 1], in1=v,
                                                     op0=ALU.mult, op1=ALU.add)
                    if tap == 1:
                        link(ins)
                ins.then_inc(S("conv_2"), 1)

            def act_mul(j):
                dve.wait_ge(S("silu"), j + 1)
                if j >= 2:
                    dve.wait_ge(S("ff_low"), j - 1)
                V.tensor_tensor(actF[:, j % 2], conv[:, j % 2, 0:2, :], conv[:, j % 2, 2:4, :], ALU.mult).then_inc(S("act_f"), 1)

            def ff_low(j):
                dve.wait_ge(S("ff_high"), j + 1)
                k = 2 * j if j < UP_A else 2 * (j - UP_A)
                V.tensor_tensor(aL[:, k:k + 2, :], actF[:, j % 2], aH[:, k:k + 2, :].bitcast(F32), ALU.subtract)\
                    .then_inc(S("ff_low"), 1)

            def after_up(j, name):
                conv_rest(j)
                split(name, 0, 1)
                act_mul(j)
                split(name, 1, 2)
                ff_low(j)
                split(name, 2)

            split("up1")
            for j in range(2, UP_A):
                after_up(j - 2, f"up{j}")
            after_up(UP_A - 2, "dn0")
            after_up(UP_A - 1, "dn1")
            split("dn2")
            split(f"up{UP_A}")
            split(f"up{UP_A + 1}")
            for j in range(UP_A + 2, 11):
                after_up(j - 2, f"up{j}")
            after_up(9, "dn3")
            after_up(10, "dn4")
            split("dn5")
            split("q2", 0, 2)
            done("dn5")
            for m in range(KD):
                residual(m, ps[:, 4 + m // 2, 256 * (m % 2):256 * (m % 2) + 256], adaT[:, G_F + m:G_F + m + 1], "xT_ready")
            cols = norm_mean(2, 3, 2)
            split("q2", 2, 3)
            dve.wait_ge(S("norm_rstd"), 3)
            link(V.tensor_tensor(ssq[:, 0:TT], cols[:, 1, :], rstd[:, 0:TT], ALU.mult))
            link(V.tensor_tensor(ssq[:, 0:TT], ssq[:, 0:TT], rstd[:, 0:TT], ALU.mult))
            mean_sq(ms[:, TT:2 * TT], ssq[:, 0:TT], D, "norm_ms")
            split("q2", 3)
            dve.wait_ge(S("norm_rstd"), 4)
            V.tensor_tensor(r12[:], rstd[:, 0:TT], rstd[:, TT:2 * TT], ALU.mult).then_inc(S("norm_r12"), 1)
            dve.wait_ge(S("norm_bc"), 4)
            norm_apply(3, ps[:, 3, SEQ:2 * SEQ], scale_2, None)
            for k in range(KD):
                V.scalar_tensor_tensor(out=xT[:, k, :], in0=xT[:, k, :], scalar=colT[:, ROW["fin_g"] + k:ROW["fin_g"] + k + 1],
                                       in1=ps[:, 3, 0:SEQ], op0=ALU.mult, op1=ALU.mult).then_inc(S("xT_ready"), 1)
            V.tensor_scalar(qg8[:], colT[:, ROW["qg2"]:ROW["qg2"] + 1], HEAD2 ** -0.5, None, ALU.mult)
            V.tensor_scalar(sub8[:], colT[:, ROW["subln"]:ROW["subln"] + 1], 1.0 - LAM_INIT, None, ALU.mult)
            lr = colT[:, ROW["lam"]:ROW["lam"] + 4].rearrange("p (a b) -> p a b", b=2)
            V.tensor_tensor(lam[:, 0:2], lr[:, :, 0], lr[:, :, 1], ALU.mult).then_inc(S("lam_steps"), 1)
            split("k2")

            def tok_out(name, dst):
                done(name)
                for tt in range(TT):
                    V.tensor_copy(dst[:, tt, :], ps[:, IT[name]["acc"] + tt, :]).then_inc(S(f"{name}_out"), 1)

            def tok_sum(name, width, n):
                dve.wait_ge(S(f"{name}_sq"), 1)
                link(V.tensor_reduce(ms[:, 0:n], sq2.rearrange("p t (h n) -> p (t h) n", n=width), AX_X, ALU.add))
                mean_sq(ms[:, 0:n], ms[:, 0:n], width, f"{name}_ms")

            def tok_norm(name, src, dst, width, n, sem):
                dve.wait_ge(S(f"{name}_rstd"), 1)
                V.tensor_tensor(dst.rearrange("p t (h n) -> p (t h) n", n=width), src.rearrange("p t (h n) -> p (t h) n", n=width),
                                rstd[:, 0:n].unsqueeze(2).to_broadcast([P, n, width]), ALU.mult).then_inc(S(sem), 1)

            def mean_o2(h):
                dve.wait_ge(S("sub_sq"), TT * h + TT)
                mean_sq(ms[:, TT * h:TT * h + TT], ssq_o[:, h, :], V2, "sub_ms")

            def norm_o2(h):
                dve.wait_ge(S("sub_rstd"), h + 1)
                v = o2[:, :, h * V2:h * V2 + V2]
                V.tensor_tensor(v, v, rstd[:, TT * h:TT * h + TT].unsqueeze(2).to_broadcast([P, TT, V2]), ALU.mult)\
                    .then_inc(S("sub_n"), 1)

            def low_o2(h):
                dve.wait_ge(S("mix_high"), h + 1)
                V.scalar_tensor_tensor(out=aL[:, 4 + h, :], in0=ps[:, 5, 256 * (h % 2):256 * (h % 2) + 256], scalar=sub8[:, 0:1],
                                       in1=aH[:, 4 + h, :].bitcast(F32), op0=ALU.mult, op1=ALU.subtract)\
                    .then_inc(S("mix_low"), 1)

            tok_out("q2", q2)
            tok_sum("q2", HEAD2, 16)
            split("v2")
            tok_out("k2", k2)
            tok_norm("q2", q2, qn, HEAD2, 16, "qn")
            split("xc", 0, 2)
            tok_sum("k2", HEAD2, 16)
            split("xc", 2)
            tok_norm("k2", k2, kn, HEAD2, 16, "kn")
            split("cg")
            dve.wait_ge(S("lam_steps"), 3)
            link(V.tensor_tensor(lam[:, 5:6], lam[:, 3:4], lam[:, 2:3], ALU.subtract))
            link(V.tensor_scalar(lam[:, 5:6], lam[:, 5:6], LAM_INIT, None, ALU.subtract))
            for i in range(2):
                dve.wait_ge(S("q2_turned"), i + 1)
                V.tensor_scalar(qT2[:, 2 * i:2 * i + 2, :].rearrange("p a b -> p (a b)"), ps[:, 4 + i, :], qg8[:, 0:1], None,
                                ALU.mult).then_inc(S("qT2_out"), 1)

            def diff_p(h):
                a0, a1 = N1 + 2 * h, N1 + 2 * h + 1
                b0, b1 = a0 % 4, a1 % 4
                dve.wait_ge(S("att_exp"), 2 * a1 + 2)
                V.reciprocal(rinv[:, b0, :], rsum[:, b0, :])
                link(V.reciprocal(rinv[:, b1, :], rsum[:, b1, :]))
                link(V.scalar_tensor_tensor(out=rinv[:, b1, :], in0=rinv[:, b1, :], scalar=lam[:, 5:6], in1=rsum[:, b0, :],
                                            op0=ALU.mult, op1=ALU.mult))
                for tt, (c0, n) in enumerate(((0, P), (P, 2 * P))):
                    v = prob_of(a0)[:, c0:c0 + n]
                    ins = V.scalar_tensor_tensor(out=v, in0=prob_of(a1)[:, c0:c0 + n], scalar=rinv[:, b1, tt:tt + 1], in1=v,
                                                 op0=ALU.mult, op1=ALU.add)
                ins.then_inc(S("diff_p"), 1)

            def o2_out(h):
                dve.wait_ge(S("diff_pv"), h + 1)
                for tt in range(TT):
                    ins = V.tensor_scalar(o2[:, tt, h * V2:h * V2 + V2], ps[:, 6 + h % 2, tt * P:tt * P + P],
                                          rinv[:, (N1 + 2 * h) % 4, tt:tt + 1], None, ALU.mult)
                ins.then_inc(S("o2_out"), 1)

            def taps(tap):
                for m in range(4):
                    dve.wait_ge(S("cy_1"), m + 1)
                    v = cy[:, m, tap:SEQ]
                    col = w2c + 4 * (2 - tap) + m
                    ins = V.scalar_tensor_tensor(out=v, in0=cz[:, m, 0:SEQ - tap], scalar=colT[:, col:col + 1], in1=v,
                                                 op0=ALU.mult, op1=ALU.add)
                link(ins)

            w2c = ROW["conv_w2"]
            N2 = 2 * N_HEADS2
            dve.wait_ge(S("k2_turned"), 2)
            logits_in(N1)
            logits_in(N1 + 1)
            for st in range(N2):
                h = st // 2
                if st % 2:
                    diff_p(h)
                    dve.wait_ge(S("diff_p"), h + 1)
                if st == N2 - 1:
                    taps(1)
                    taps(2)
                if st == 4:
                    done("cg")
                    dve.wait_ge(S("xc_out"), 2)
                    for i in range(2):
                        V.tensor_tensor(cz[:, 2 * i:2 * i + 2, :],
                                        ps[:, IT["cg"]["acc"] + i, :].rearrange("p (a b) -> p a b", a=2),
                                        cz[:, 2 * i:2 * i + 2, :], ALU.mult).then_inc(S("cg_out"), 1)
                if st + 2 < N2:
                    logits_in(N1 + st + 2)
                if 1 <= st < 5:
                    split("bg", st - 1, st)
                elif 5 <= st < 7:
                    split("w2o_attn", st - 5, st - 4)
                if st % 2:
                    if h >= 1:
                        o2_out(h - 1)
                    if h >= 2:
                        norm_o2(h - 2)
                else:
                    if h >= 2:
                        mean_o2(h - 2)
                    if h >= 3:
                        low_o2(h - 3)
            mean_o2(2)
            low_o2(1)
            norm_o2(2)
            done("bg")
            for i in range(2):
                v = cy[:, 2 * i:2 * i + 2, :]
                V.tensor_tensor(v, v, ps[:, IT["bg"]["acc"] + i, :].rearrange("p (a b) -> p a b", a=2), ALU.mult)\
                    .then_inc(S("cy_ready"), 1)
            split("w2o_attn", 2, 3)
            o2_out(N_HEADS2 - 1)
            low_o2(2)
            mean_o2(3)
            norm_o2(3)
            split("w2o_attn", 3)
            dve.wait_ge(S("cv_sum"), 1)
            mean_sq(ms[:, 0:16], ps[:, 6, 0:16], D_CONV // 8, "cv_ms")
            low_o2(3)
            split("w2o_conv", 0, 2)
            dve.wait_ge(S("cv_bc"), 1)
            for m in range(4):
                V.scalar_tensor_tensor(out=cy[:, m, :], in0=cy[:, m, :],
                                       scalar=colT[:, ROW["conv_out_g2"] + m:ROW["conv_out_g2"] + m + 1],
                                       in1=ps[:, 6 + m // 2, 256 * (m % 2):256 * (m % 2) + 256],
                                       op0=ALU.mult, op1=ALU.mult).then_inc(S("mixF"), 1)
            for m in range(4):
                dve.wait_ge(S("mix_high"), N_HEADS2 + m + 1)
                V.tensor_tensor(aL[:, m, :], cy[:, m, :], aH[:, m, :].bitcast(F32), ALU.subtract).then_inc(S("mix_low"), 1)
            split("w2o_conv", 2)
            done("w2o_conv")
            for m in range(KD):
                V.tensor_tensor(xT[:, m, :], ps[:, m // 2, 256 * (m % 2):256 * (m % 2) + 256], xT[:, m, :], ALU.add)\
                    .then_inc(S("xT_ready"), 1)
            dve.wait_ge(S("row_sq"), 4)
            halves = ssq[:, 0:4].rearrange("p (t h) -> p t h", t=TT)
            link(V.tensor_tensor(ms[:, 0:TT], halves[:, :, 0], halves[:, :, 1], ALU.add))
            mean_sq(ms[:, 0:TT], ms[:, 0:TT], D, "norm_ms")

            def low_tokens(i):
                hf, tt = divmod(i, 2)
                cs = slice(512 * hf, 512 * hf + 512)
                dve.wait_ge(S("hn_high"), i + 1)
                dve.wait_ge(S("y_sum"), 2 * tt + hf + 1)
                V.scalar_tensor_tensor(out=hnL[:, tt, cs], in0=y_acc[:, tt, cs], scalar=rstd[:, tt:tt + 1],
                                       in1=hnH[:, tt, cs].bitcast(F32), op0=ALU.mult, op1=ALU.subtract).then_inc(S("hn_low"), 1)

            dve.wait_ge(S("norm_rstd"), 5)
            dve.wait_ge(S("logits"), 1)
            for tt in range(TT):
                ins = V.tensor_scalar(lg[:, tt, :], ps[:, 6, tt * 64:tt * 64 + LG], rstd[:, tt:tt + 1], None, ALU.mult)
            link(ins)
            gl = lg[:, :, 0:GROUPS]

            def wide(v, n):
                return v.unsqueeze(2).to_broadcast([P, TT, n])

            def first_max(src, top, tmp, oh, n):
                link(V.tensor_reduce(top, src, AX_X, ALU.max))
                link(V.tensor_tensor(tmp, src, wide(top, n), ALU.is_equal))
                link(V.tensor_tensor(tmp, tmp, desc[:, 0:n].unsqueeze(1).to_broadcast([P, TT, n]), ALU.mult))
                link(V.tensor_reduce(wm, tmp, AX_X, ALU.max))
                link(V.tensor_tensor(oh, tmp, wide(wm, n), ALU.is_equal))

            first_max(gl, gmax, gtmp, goh, GROUPS)
            gw = goh.unsqueeze(3).to_broadcast([P, TT, GROUPS, EPG])
            link(V.tensor_tensor(gprod, lg[:, :, GROUPS:LG].rearrange("p t (g e) -> p t g e", g=GROUPS), gw, ALU.mult))
            link(V.tensor_reduce(lsel, gprod.rearrange("p t g e -> p t e g"), AX_X, ALU.add))
            first_max(lsel, m1, etmp, oh1, EPG)
            link(V.scalar_tensor_tensor(out=l2, in0=oh1, scalar=NEG, in1=lsel, op0=ALU.mult, op1=ALU.add))
            first_max(l2, m2, etmp, oh2, EPG)
            link(V.tensor_tensor(etmp, oh1, oh2, ALU.add))
            V.tensor_tensor(sel, etmp.unsqueeze(2).to_broadcast([P, TT, GROUPS, EPG]), gw, ALU.mult).then_inc(S("sel"), 1)
            V.tensor_tensor(ed, m2, m1, ALU.subtract).then_inc(S("e_shift"), 1)
            V.tensor_tensor(gtmp, gl, wide(gmax, GROUPS), ALU.subtract).then_inc(S("g_shift"), 1)
            for i in range(2):
                low_tokens(i)
            dve.wait_ge(S("places"), 1)
            for tt in range(TT):
                ins = V.tensor_tensor(posm[:, tt, 0:EXPERTS], ps[:, 7, 32 * tt:32 * tt + 32],
                                      sel[:, tt].rearrange("p g e -> p (g e)"), ALU.mult)
            link(ins)
            V.tensor_scalar(posm[:, :, EXPERTS:EXPERTS + PER_IT], posm[:, :, 0:PER_IT], float(CAP), None, ALU.subtract)
            link(V.tensor_reduce(npass_f[0:1, 0:1], ps[0:1, 7, 64:96], AX_X, ALU.max))

            def pick_tokens(e0, turn):
                for tt in range(TT):
                    V.tensor_tensor(pick[:, tt, :].rearrange("p (e s) -> p e s", e=PER_IT),
                                    slot_no[:].unsqueeze(1).to_broadcast([P, PER_IT, CAP]),
                                    posm[:, tt, bass.ds(e0, PER_IT)].unsqueeze(2).to_broadcast([P, PER_IT, CAP]), ALU.is_equal)\
                        .then_inc(S("pick_half"), 1)
                dve.wait_ge(S("pick_half"), turn * 2 + 2)

            def weigh_tokens(e0):
                for tt in range(TT):
                    V.tensor_tensor(put[:, tt, :].rearrange("p (e s) -> p e s", e=PER_IT),
                                    pick[:, tt, :].bitcast(F32).rearrange("p (e s) -> p e s", e=PER_IT),
                                    comb[:, tt, bass.ds(e0, PER_IT)].unsqueeze(2).to_broadcast([P, PER_IT, CAP]), ALU.mult)\
                        .then_inc(S("put_half"), 1)

            pick_tokens(0, 0)
            for i in range(2, 4):
                low_tokens(i)
            link(V.tensor_scalar(npass[0:1, 1:2], npass_f[0:1, 0:1], float(CAP - 1), None, ALU.add))
            V.tensor_scalar(npass[0:1, 0:1], npass[0:1, 1:2], int(math.log2(CAP)), None, ALU.arith_shift_right)\
                .then_inc(S("npass_ready"), 1)
            dve.wait_ge(S("g_exp"), 1)
            link(V.tensor_reduce(gsum, gexp, AX_X, ALU.add))
            link(V.reciprocal(ggate, gsum))
            dve.wait_ge(S("e_exp"), 1)
            link(V.tensor_scalar(w1, ed, 1.0, None, ALU.add))
            link(V.reciprocal(w1, w1))
            link(V.tensor_tensor(w2, ed, w1, ALU.mult))
            link(V.tensor_tensor(oh1, oh1, wide(w1, EPG), ALU.mult))
            link(V.tensor_tensor(oh2, oh2, wide(w2, EPG), ALU.mult))
            link(V.tensor_tensor(oh1, oh1, oh2, ALU.add))
            link(V.tensor_tensor(oh1, oh1, wide(ggate, EPG), ALU.mult))
            for tt in range(TT):
                ins = V.tensor_tensor(comb[:, tt, 0:EXPERTS].rearrange("p (g e) -> p g e", g=GROUPS),
                                      oh1[:, tt].unsqueeze(1).to_broadcast([P, GROUPS, EPG]),
                                      goh[:, tt].unsqueeze(2).to_broadcast([P, GROUPS, EPG]), ALU.mult)
            link(ins)
            link(V.tensor_copy(comb[:, :, EXPERTS:EXPERTS + PER_IT], comb[:, :, 0:PER_IT]))
            weigh_tokens(0)
            dve.wait_ge(S("y_sum"), 4)
            dve.wait_ge(S("npass_ready"), 1)
            n = dve.value_load(npass[0:1, 0:1], min_val=1, max_val=SEQ // CAP)
            with dve.Fori(0, n) as p:
                with dve.Fori(0, TURNS) as g:
                    turn = p * TURNS + g
                    for r in range(2):
                        dve.wait_ge(S("e_silu"), turn * 2 + (r + 1))
                        dve.wait_ge(S("expert_used"), turn * 8 + (4 * r + 2))
                        V.tensor_tensor(eact, sg, ps[:, 1, :], ALU.mult).then_inc(S("e_act"), 1)
                        if r == 0:
                            dve.wait_ge(S("gathered"), turn * 4 + 4)
                            dve.wait_ge(S("put_half"), turn * 2 + 2)
                            pick_tokens((g + 1) * PER_IT, turn + 1)
                            dve.wait_ge(S("put_turned"), turn + 1)
                            weigh_tokens((g + 1) * PER_IT)
                        for i in range(4):
                            hf, tt = divmod(i, 2)
                            v = y_acc[:, tt, 512 * hf:512 * hf + 512]
                            dve.wait_ge(S("e_put"), turn * 8 + (4 * r + i + 1))
                            dve.wait_ge(S("y_sum"), turn * 8 + (4 * r + i + 1))
                            V.tensor_tensor(v, v, ps[:, 6 + i % 2, :], ALU.add).then_inc(S("y_sum"), 1)
                V.tensor_scalar(slot_no[:], slot_no[:], float(CAP), None, ALU.add).then_inc(S("slot_next"), 1)
                dve.wait_ge(S("slot_next"), p + 1)


def kernel(**inputs):
    import concourse.bacc as bacc
    from concourse.bass_utils import run_bass_kernel_spmd

    nc = bacc.Bacc("TRN2", target_bir_lowering=False, num_devices=1)
    two_dim = ("w_ada", "w_in", "w_uq", "w_ukv", "w_o_mla", "w_o_fox", "w_out", "w_up", "conv_w", "w_down", "w_in_2",
               "w_out_2", "w_router_group_2", "w_router_expert_2", "x")
    feeds, t = {}, {}
    for name, value in inputs.items():
        a = np.ascontiguousarray(np.asarray(value))
        if name in two_dim:
            a = a.reshape(a.shape[-2:])
        elif name.startswith("w_exp"):
            a = a.reshape((EXPERTS,) + a.shape[-2:])
        elif name == "b_forget":
            a = a.reshape(-1)
        else:
            a = a.reshape(1, -1)
        feeds[name] = a
        t[name] = nc.dram_tensor(name, a.shape, mybir.dt.from_np(a.dtype), kind="ExternalInput").ap()
    out = nc.dram_tensor("out", (SEQ, D), F32, kind="ExternalOutput").ap()
    build(nc, t, out)
    nc.finalize()
    res = run_bass_kernel_spmd(nc, [feeds], core_ids=[0])
    return res.results[0]["out"].reshape(1, SEQ, D)
```
